# Optimizing a Trainium2 kernel written in Bass

```python
import math
import jax, jax.numpy as jnp
from jax import lax
import numpy as np

D_MODEL = 1024
BATCH = 1
SEQ = 256
DEPTH = 1

HEAD_DIM = 64
GDN_HEADS = 6
GDN_CONV = 4
GDN_CHUNK = 64
GDN_WIDTH = GDN_HEADS * HEAD_DIM
NSA_HEADS = 6
NSA_KV_HEADS = 2
NSA_GROUP = NSA_HEADS // NSA_KV_HEADS
NSA_WIDTH = NSA_HEADS * HEAD_DIM
NSA_KV_WIDTH = NSA_KV_HEADS * HEAD_DIM
CMP_LEN = 32
CMP_STRIDE = 16
CMP_HIDDEN = 256
SEL_BLOCK = 64
SEL_TOPK = 16
WINDOW = 512
Q_BLOCK = 128
FORCED_SCORE = 1e4
POOL_WINDOWS = (2, 4, 8, 16)
POOL_GROUP_DIM = 64
POOL_WIDTH = 4 * POOL_GROUP_DIM
D_MIX = GDN_WIDTH + NSA_WIDTH + POOL_WIDTH
IN_SPLITS = (3 * GDN_WIDTH, GDN_WIDTH, GDN_HEADS, GDN_HEADS, NSA_WIDTH, 6 * NSA_KV_WIDTH, 3 * NSA_HEADS, POOL_WIDTH)
D_IN = 3 * GDN_WIDTH + GDN_WIDTH + GDN_HEADS + GDN_HEADS + NSA_WIDTH + 6 * NSA_KV_WIDTH + 3 * NSA_HEADS + POOL_WIDTH
D_FF = 4 * D_MODEL
EPS = 1e-6


def rms_norm(x, g):
    xf = x.astype(jnp.float32)
    return (xf * lax.rsqrt(jnp.mean(xf * xf, axis=-1, keepdims=True) + EPS) * g).astype(x.dtype)

def l2norm(x):
    xf = x.astype(jnp.float32)
    return xf * lax.rsqrt(jnp.sum(xf * xf, axis=-1, keepdims=True) + EPS)

def masked_softmax(s, mask):
    s = jnp.where(mask, s.astype(jnp.float32), -1e30)
    return jax.nn.softmax(s, axis=-1) * mask

def split_columns(proj):
    offs = []
    acc = 0
    for s in IN_SPLITS[:-1]:
        acc += s
        offs.append(acc)
    return jnp.split(proj, offs, axis=-1)

def causal_conv(x, w):
    T = x.shape[1]
    K = w.shape[0]
    xp = jnp.pad(x, ((0, 0), (K - 1, 0), (0, 0)))
    return sum(xp[:, k:k + T] * w[k] for k in range(K))

def gated_delta_rule(q, k, v, beta, g):
    B, T, H, Dk = q.shape
    Dv = v.shape[-1]
    C = GDN_CHUNK
    N = T // C
    f32 = jnp.float32

    def chunks(a):
        a = a.astype(f32).reshape((B, N, C, H) + a.shape[3:])
        return jnp.moveaxis(a, 3, 1)

    q, k, v, beta, g = map(chunks, (q, k, v, beta, g))
    q = q * Dk ** -0.5
    gc = jnp.cumsum(g, axis=-1)
    causal = jnp.tril(jnp.ones((C, C), bool))
    strict = jnp.tril(jnp.ones((C, C), bool), -1)
    decay = jnp.exp(jnp.where(causal, gc[..., :, None] - gc[..., None, :], -jnp.inf))
    k_beta = k * beta[..., None]
    L = jnp.where(strict, jnp.einsum('bhncd,bhnsd->bhncs', k_beta, k) * decay, 0.0)
    A = jnp.eye(C, dtype=f32) + L
    u = lax.linalg.triangular_solve(A, v * beta[..., None], left_side=True, lower=True, unit_diagonal=True)
    w = lax.linalg.triangular_solve(A, k_beta * jnp.exp(gc)[..., None], left_side=True, lower=True, unit_diagonal=True)
    qk = jnp.einsum('bhncd,bhnsd->bhncs', q, k) * decay
    q_dec = q * jnp.exp(gc)[..., None]
    k_dec = k * jnp.exp(gc[..., -1:] - gc)[..., None]
    g_last = jnp.exp(gc[..., -1])

    def step(S, xs):
        u_i, w_i, qk_i, qd_i, kd_i, gl_i = xs
        v_new = u_i - jnp.einsum('bhcd,bhde->bhce', w_i, S)
        o = jnp.einsum('bhcd,bhde->bhce', qd_i, S) + jnp.einsum('bhcs,bhse->bhce', qk_i, v_new)
        S = S * gl_i[..., None, None] + jnp.einsum('bhcd,bhce->bhde', kd_i, v_new)
        return S, o

    xs = tuple(jnp.moveaxis(a, 2, 0) for a in (u, w, qk, q_dec, k_dec, g_last))
    S0 = jnp.zeros((B, H, Dk, Dv), f32)
    _, o = lax.scan(step, S0, xs)
    return jnp.transpose(o, (1, 0, 3, 2, 4)).reshape(B, T, H, Dv)

def gdn_mixer(qkv, z, b, a, conv_w, a_log, dt_bias, norm_g):
    B, T, _ = qkv.shape
    qkv = jax.nn.silu(causal_conv(qkv, conv_w))
    q, k, v = jnp.split(qkv, 3, axis=-1)
    heads = lambda t: t.reshape(B, T, GDN_HEADS, HEAD_DIM)
    q, k, v = l2norm(heads(q)), l2norm(heads(k)), heads(v)
    beta = jax.nn.sigmoid(b.astype(jnp.float32))
    g = -jnp.exp(a_log.astype(jnp.float32)) * jax.nn.softplus(a.astype(jnp.float32) + dt_bias)
    o = gated_delta_rule(q, k, v, beta, g)
    o = rms_norm(o, norm_g) * jax.nn.silu(heads(z).astype(jnp.float32))
    return o.reshape(B, T, GDN_WIDTH).astype(qkv.dtype)

def compress(x, pos, w1, w2):
    B, T, H, D = x.shape
    R = CMP_LEN // CMP_STRIDE
    Nr = T // CMP_STRIDE
    r = x.reshape(B, Nr, CMP_STRIDE, H, D)
    blocks = jnp.concatenate([r[:, i:Nr - R + 1 + i] for i in range(R)], axis=2)
    blocks = blocks + pos[None, None, :, None, :]
    Nc = blocks.shape[1]
    flat = blocks.transpose(0, 1, 3, 2, 4).reshape(B, Nc, H, CMP_LEN * D)
    out = jax.nn.silu(flat @ w1) @ w2
    return out.transpose(0, 2, 1, 3)

def cmp_to_sel(p):
    R = SEL_BLOCK // CMP_STRIDE
    P = CMP_LEN // CMP_STRIDE - 1
    Ns = (p.shape[-1] + P) // R
    pp = jnp.pad(p, [(0, 0)] * (p.ndim - 1) + [(P, P)])
    return sum(lax.slice_in_dim(pp, o, o + R * (Ns - 1) + 1, stride=R, axis=-1) for o in range(R + P))

def nsa_mixer(q, kv, gate_logits, q_norm, k_norm, cmp_pos, cmp_w1, cmp_w2):
    B, T, _ = q.shape
    Hkv, G, Dh = NSA_KV_HEADS, NSA_GROUP, HEAD_DIM
    out_dtype = q.dtype
    scale = Dh ** -0.5
    q = rms_norm(q.reshape(B, T, NSA_HEADS, Dh), q_norm)
    q = q.reshape(B, T, Hkv, G, Dh).transpose(0, 2, 3, 1, 4)
    kc, vc, ks, vs, kw, vw = [t.reshape(B, T, Hkv, Dh) for t in jnp.split(kv, 6, axis=-1)]
    kc = rms_norm(compress(kc, cmp_pos[0], cmp_w1[0], cmp_w2[0]), k_norm[0])
    vc = compress(vc, cmp_pos[1], cmp_w1[1], cmp_w2[1])
    Nc = kc.shape[2]
    Ns = T // SEL_BLOCK
    K_SEL = min(SEL_TOPK, Ns)
    ks = rms_norm(ks, k_norm[1]).transpose(0, 2, 1, 3).reshape(B, Hkv, Ns, SEL_BLOCK, Dh)
    vs = vs.transpose(0, 2, 1, 3).reshape(B, Hkv, Ns, SEL_BLOCK, Dh)
    pad = ((0, 0), (0, 0), (WINDOW, 0), (0, 0))
    kw = jnp.pad(rms_norm(kw, k_norm[2]).transpose(0, 2, 1, 3), pad)
    vw = jnp.pad(vw.transpose(0, 2, 1, 3), pad)
    gates = jax.nn.sigmoid(gate_logits.astype(jnp.float32)).reshape(B, T, Hkv, G, 3).transpose(0, 2, 3, 1, 4)
    cmp_end = jnp.arange(Nc) * CMP_STRIDE + CMP_LEN - 1
    blk = jnp.arange(Ns)
    bidx = jnp.arange(B)[:, None, None, None]
    hidx = jnp.arange(Hkv)[None, :, None, None]

    def block(i):
        t0 = i * Q_BLOCK
        pos = t0 + jnp.arange(Q_BLOCK)
        qb = lax.dynamic_slice_in_dim(q, t0, Q_BLOCK, axis=3) * scale
        gb = lax.dynamic_slice_in_dim(gates, t0, Q_BLOCK, axis=3)
        s = jnp.einsum('bhgqd,bhcd->bhgqc', qb, kc)
        p_c = masked_softmax(s, cmp_end[None, :] <= pos[:, None])
        o_c = jnp.einsum('bhgqc,bhcd->bhgqd', p_c, vc)
        imp = cmp_to_sel(p_c.sum(axis=2))
        cur = pos // SEL_BLOCK
        forced = (blk[None] == 0) | (blk[None] == cur[:, None]) | (blk[None] == cur[:, None] - 1)
        valid = blk[None] * SEL_BLOCK <= pos[:, None]
        imp = jnp.where(forced, FORCED_SCORE, jnp.where(valid, imp, -1.0))
        _, idx = lax.top_k(imp, K_SEL)
        ksel = ks[bidx, hidx, idx]
        vsel = vs[bidx, hidx, idx].reshape(B, Hkv, Q_BLOCK, K_SEL * SEL_BLOCK, Dh)
        s = jnp.einsum('bhgqd,bhqksd->bhgqks', qb, ksel).reshape(B, Hkv, G, Q_BLOCK, K_SEL * SEL_BLOCK)
        key_pos = idx[..., None] * SEL_BLOCK + jnp.arange(SEL_BLOCK)
        mask_s = (key_pos <= pos[:, None, None]).reshape(B, Hkv, 1, Q_BLOCK, K_SEL * SEL_BLOCK)
        o_s = jnp.einsum('bhgqn,bhqnd->bhgqd', masked_softmax(s, mask_s), vsel)
        kwb = lax.dynamic_slice_in_dim(kw, t0, Q_BLOCK + WINDOW, axis=2)
        vwb = lax.dynamic_slice_in_dim(vw, t0, Q_BLOCK + WINDOW, axis=2)
        kpos = t0 - WINDOW + jnp.arange(Q_BLOCK + WINDOW)
        mask_w = (kpos[None] <= pos[:, None]) & (kpos[None] > pos[:, None] - WINDOW) & (kpos[None] >= 0)
        s = jnp.einsum('bhgqd,bhkd->bhgqk', qb, kwb)
        o_w = jnp.einsum('bhgqk,bhkd->bhgqd', masked_softmax(s, mask_w), vwb)
        return gb[..., 0:1] * o_c + gb[..., 1:2] * o_s + gb[..., 2:3] * o_w

    out = lax.map(block, jnp.arange(T // Q_BLOCK))
    return out.transpose(1, 0, 4, 2, 3, 5).reshape(B, T, NSA_WIDTH).astype(out_dtype)

def pool_mixer(u, pool_w, pool_scale):
    B, T, _ = u.shape
    uf = u.astype(jnp.float32)
    c = jnp.pad(jnp.cumsum(uf, axis=1), ((0, 0), (1, 0), (0, 0)))
    t1 = jnp.arange(1, T + 1, dtype=jnp.float32)
    outs = []
    for gi, w in enumerate(POOL_WINDOWS):
        sl = slice(gi * POOL_GROUP_DIM, (gi + 1) * POOL_GROUP_DIM)
        cg = c[..., sl]
        cg_lag = jnp.pad(cg, ((0, 0), (w - 1, 0), (0, 0)))[:, :T]
        mean = (cg[:, 1:] - cg_lag) / jnp.minimum(t1, float(w))[None, :, None]
        outs.append(jnp.einsum('btc,cd->btd', mean - uf[..., sl], pool_w[gi]))
    return (jnp.concatenate(outs, axis=-1) * pool_scale).astype(u.dtype)

def first_inputs(seed: int = 0) -> dict:
    key = jax.random.key(seed)
    keys = jax.random.split(key, 20)
    nrm = lambda k, shape, s: jax.random.normal(k, shape, jnp.float32) * s
    L = DEPTH
    x = nrm(keys[0], (BATCH, SEQ, D_MODEL), 1.0)
    norm_mix = 1.0 + nrm(keys[1], (L, D_MODEL), 0.02)
    w_in = nrm(keys[2], (L, D_MODEL, D_IN), D_MODEL ** -0.5)
    conv_w = nrm(keys[3], (L, GDN_CONV, 3 * GDN_WIDTH), GDN_CONV ** -0.5)
    a_log = jnp.log(jax.random.uniform(keys[4], (L, GDN_HEADS), jnp.float32, 1.0, 16.0))
    dt = jnp.exp(jax.random.uniform(keys[5], (L, GDN_HEADS), jnp.float32, math.log(1e-3), math.log(1e-1)))
    dt_bias = dt + jnp.log(-jnp.expm1(-dt))
    gdn_norm = 1.0 + nrm(keys[6], (L, HEAD_DIM), 0.02)
    nsa_q_norm = 1.0 + nrm(keys[7], (L, HEAD_DIM), 0.02)
    nsa_k_norm = 1.0 + nrm(keys[8], (L, 3, HEAD_DIM), 0.02)
    cmp_pos = nrm(keys[9], (L, 2, CMP_LEN, HEAD_DIM), 0.1)
    cmp_w1 = nrm(keys[10], (L, 2, CMP_LEN * HEAD_DIM, CMP_HIDDEN), (CMP_LEN * HEAD_DIM) ** -0.5)
    cmp_w2 = nrm(keys[11], (L, 2, CMP_HIDDEN, HEAD_DIM), CMP_HIDDEN ** -0.5)
    pool_w = nrm(keys[12], (L, len(POOL_WINDOWS), POOL_GROUP_DIM, POOL_GROUP_DIM), POOL_GROUP_DIM ** -0.5)
    pool_scale = 1.0 + nrm(keys[13], (L, POOL_WIDTH), 0.1)
    w_out = nrm(keys[14], (L, D_MIX, D_MODEL), (2 * DEPTH * D_MIX) ** -0.5)
    norm_ffn = 1.0 + nrm(keys[15], (L, D_MODEL), 0.02)
    w_ffn1 = nrm(keys[16], (L, D_MODEL, D_FF), D_MODEL ** -0.5)
    w_ffn2 = nrm(keys[17], (L, D_FF, D_MODEL), (2 * DEPTH * D_FF) ** -0.5)
    return {"x": x, "norm_mix": norm_mix, "w_in": w_in, "conv_w": conv_w, "a_log": a_log, "dt_bias": dt_bias,
            "gdn_norm": gdn_norm, "nsa_q_norm": nsa_q_norm, "nsa_k_norm": nsa_k_norm, "cmp_pos": cmp_pos,
            "cmp_w1": cmp_w1, "cmp_w2": cmp_w2, "pool_w": pool_w, "pool_scale": pool_scale, "w_out": w_out,
            "norm_ffn": norm_ffn, "w_ffn1": w_ffn1, "w_ffn2": w_ffn2}

def first_block(x, norm_mix, w_in, conv_w, a_log, dt_bias, gdn_norm, nsa_q_norm, nsa_k_norm, cmp_pos,
              cmp_w1, cmp_w2, pool_w, pool_scale, w_out, norm_ffn, w_ffn1, w_ffn2):
    for l in range(DEPTH):
        h = rms_norm(x, norm_mix[l])
        proj = h @ w_in[l]
        qkv_a, z_a, b_a, a_a, q_b, kv_b, gate_b, u_c = split_columns(proj)
        y_a = gdn_mixer(qkv_a, z_a, b_a, a_a, conv_w[l], a_log[l], dt_bias[l], gdn_norm[l])
        y_b = nsa_mixer(q_b, kv_b, gate_b, nsa_q_norm[l], nsa_k_norm[l], cmp_pos[l], cmp_w1[l], cmp_w2[l])
        y_c = pool_mixer(u_c, pool_w[l], pool_scale[l])
        y = jnp.concatenate([y_a.astype(x.dtype), y_b.astype(x.dtype), y_c.astype(x.dtype)], axis=-1)
        x = x + y @ w_out[l]
        h = rms_norm(x, norm_ffn[l])
        x = x + jnp.square(jax.nn.relu(h @ w_ffn1[l])) @ w_ffn2[l]
    return x


N_MIXERS = 4
RMS_EPS = 1e-6
N_MOD = 6

SB_HEADS = 16
SB_HEAD_DIM = D_MODEL // SB_HEADS
SB_QBLOCK = 128

GLA_HEADS = 4
GLA_DK = D_MODEL // (2 * GLA_HEADS)
GLA_DV = D_MODEL // GLA_HEADS
GLA_GATE_RANK = 16
GLA_GATE_TAU = 16.0
GLA_CHUNK = 64
GLA_IN = 2 * GLA_HEADS * GLA_DK + 2 * GLA_HEADS * GLA_DV + GLA_GATE_RANK

CONV_WIDTH = 3

DIL_PATTERNS = ((128, 1), (512, 4), (2048, 16))
DIL_GROUPS = len(DIL_PATTERNS)
DIL_HEADS = 8
DIL_HEAD_DIM = 64
DIL_QBLOCK = 128

MOE_GROUPS = 4
MOE_PER_GROUP = 8
MOE_EXPERTS = MOE_GROUPS * MOE_PER_GROUP
MOE_TOPK = 2
MOE_D_FF = D_MODEL // 2
MOE_BLOCK = 128

N_SB = (DEPTH + 3) // N_MIXERS
N_GLA = (DEPTH + 2) // N_MIXERS
N_CONV = (DEPTH + 1) // N_MIXERS
N_DIL = DEPTH // N_MIXERS


def rms_norm_2(x, g):
    x32 = x.astype(jnp.float32)
    y = x32 * lax.rsqrt(jnp.mean(x32 * x32, axis=-1, keepdims=True) + RMS_EPS)
    return (y * g.astype(jnp.float32)).astype(x.dtype)

def stick_breaking_attention(q, k, v):
    B, H, S, d = q.shape
    nb = S // SB_QBLOCK
    scale = d ** -0.5
    kpos = jnp.arange(S)
    qb = jnp.moveaxis(q.reshape(B, H, nb, SB_QBLOCK, d), 2, 0)

    def one_block(args):
        q_blk, blk = args
        qpos = blk * SB_QBLOCK + jnp.arange(SB_QBLOCK)
        z = jnp.einsum('bhqd,bhkd->bhqk', q_blk, k, preferred_element_type=jnp.float32) * scale
        causal = kpos[None, :] < qpos[:, None]
        log_keep = jnp.where(causal, jax.nn.log_sigmoid(-z), 0.0)
        suffix = lax.cumsum(log_keep, axis=3, reverse=True) - log_keep
        a = jnp.where(causal, jnp.exp(jax.nn.log_sigmoid(z) + suffix), 0.0)
        return jnp.einsum('bhqk,bhkd->bhqd', a.astype(v.dtype), v)

    out = lax.map(one_block, (qb, jnp.arange(nb)))
    return jnp.moveaxis(out, 0, 2).reshape(B, H, S, d)

def sb_mixer(h, w_in, w_out):
    B, S, _ = h.shape
    qkv = (h @ w_in).reshape(B, S, 3, SB_HEADS, SB_HEAD_DIM)
    qkv = jnp.transpose(qkv, (2, 0, 3, 1, 4))
    o = stick_breaking_attention(qkv[0], qkv[1], qkv[2])
    return jnp.transpose(o, (0, 2, 1, 3)).reshape(B, S, SB_HEADS * SB_HEAD_DIM) @ w_out

def gla_chunked(q, k, v, log_a):
    B, H, S, dk = q.shape
    dv = v.shape[-1]
    C = GLA_CHUNK
    nc = S // C
    f32 = jnp.float32

    def chunks(a):
        return a.astype(f32).reshape(B, H, nc, C, a.shape[-1])

    q, k, v, g = chunks(q), chunks(k), chunks(v), chunks(log_a)
    b = jnp.cumsum(g, axis=3)
    b_last = b[:, :, :, -1:, :]
    q_in = q * jnp.exp(b)
    k_in = k * jnp.exp(-b)
    k_state = k * jnp.exp(b_last - b)
    causal = jnp.tril(jnp.ones((C, C), dtype=bool))
    scores = jnp.where(causal, jnp.einsum('bhnid,bhnjd->bhnij', q_in, k_in), 0.0)
    o_intra = jnp.einsum('bhnij,bhnjv->bhniv', scores, v)

    def step(state, inp):
        q_n, k_n, v_n, decay_n = inp
        o_n = jnp.einsum('bhid,bhdv->bhiv', q_n, state)
        state = decay_n[..., None] * state + jnp.einsum('bhjd,bhjv->bhdv', k_n, v_n)
        return state, o_n

    xs = (jnp.moveaxis(q_in, 2, 0), jnp.moveaxis(k_state, 2, 0), jnp.moveaxis(v, 2, 0),
          jnp.moveaxis(jnp.exp(b_last[:, :, :, 0, :]), 2, 0))
    _, o_inter = lax.scan(step, jnp.zeros((B, H, dk, dv), f32), xs)
    o = o_intra + jnp.moveaxis(o_inter, 0, 2)
    return o.reshape(B, H, S, dv)

def gla_mixer(h, w_in, w_gate_up, b_gate, norm_g, w_out):
    B, S, _ = h.shape
    dqk = GLA_HEADS * GLA_DK
    dv = GLA_HEADS * GLA_DV
    proj = h @ w_in
    q, k, v, r, g_down = jnp.split(proj, [dqk, 2 * dqk, 2 * dqk + dv, 2 * dqk + 2 * dv], axis=-1)
    log_a = jax.nn.log_sigmoid((g_down @ w_gate_up + b_gate).astype(jnp.float32)) / GLA_GATE_TAU

    def heads(a, d):
        return jnp.transpose(a.reshape(B, S, GLA_HEADS, d), (0, 2, 1, 3))

    o = gla_chunked(heads(q, GLA_DK) * GLA_DK ** -0.5, heads(k, GLA_DK),
                    heads(v, GLA_DV), heads(log_a, GLA_DK))
    o = rms_norm_2(o, norm_g)
    o = jnp.transpose(o, (0, 2, 1, 3)).reshape(B, S, dv).astype(h.dtype) * jax.nn.silu(r)
    return o @ w_out

def conv_mixer(h, w_in, conv_w, conv_b, w_out):
    S = h.shape[1]
    gate_b, gate_c, u = jnp.split(h @ w_in, 3, axis=-1)
    u = gate_c * u
    u_pad = jnp.pad(u, ((0, 0), (CONV_WIDTH - 1, 0), (0, 0)))
    y = sum(conv_w[j] * u_pad[:, j:j + S] for j in range(CONV_WIDTH)) + conv_b
    return (gate_b * y) @ w_out

def dilated_window_attention(q, k, v, window, dilation):
    B, H, S, d = q.shape
    Q = DIL_QBLOCK
    steps = window // dilation
    span = dilation * Q
    Sp = -(-S // span) * span
    L = Sp // dilation
    nb = L // Q

    def strided(a):
        a = jnp.pad(a, ((0, 0), (0, 0), (0, Sp - S), (0, 0)))
        a = jnp.transpose(a.reshape(B, H, L, dilation, d), (0, 1, 3, 2, 4))
        return a.reshape(B, H, dilation, nb, Q, d)

    def with_prev(a):
        prev = jnp.concatenate([jnp.zeros_like(a[:, :, :, :1]), a[:, :, :, :-1]], axis=3)
        return jnp.concatenate([prev, a], axis=4)

    qb = strided(q)
    kc, vc = with_prev(strided(k)), with_prev(strided(v))
    z = jnp.einsum('bhrnqd,bhrnkd->bhrnqk', qb, kc, preferred_element_type=jnp.float32) * d ** -0.5
    qi = jnp.arange(Q)[:, None]
    kj = jnp.arange(2 * Q)[None, :]
    dist = qi + Q - kj
    in_window = (dist >= 0) & (dist <= steps)
    before_start = (jnp.arange(nb)[:, None, None] == 0) & (kj < Q)[None]
    valid = in_window[None] & ~before_start
    z = jnp.where(valid, z, -jnp.inf)
    m = jnp.max(z, axis=-1, keepdims=True)
    lse = m + jnp.log(jnp.sum(jnp.exp(z - m), axis=-1, keepdims=True))
    p = jnp.exp(z - lse)
    o = jnp.einsum('bhrnqk,bhrnkd->bhrnqd', p.astype(vc.dtype), vc)

    def unstride(a):
        e = a.shape[-1]
        a = jnp.moveaxis(a.reshape(B, H, dilation, L, e), 2, 3).reshape(B, H, Sp, e)
        return a[:, :, :S]

    return unstride(o), unstride(lse)[..., 0]

def dil_mixer(h, w_in, w_out):
    B, S, _ = h.shape
    proj = (h @ w_in).reshape(B, S, DIL_GROUPS, 3, DIL_HEADS, DIL_HEAD_DIM)
    proj = jnp.transpose(proj, (2, 3, 0, 4, 1, 5))
    outs, lses = [], []
    for g, (window, dilation) in enumerate(DIL_PATTERNS):
        o_g, lse_g = dilated_window_attention(proj[g, 0], proj[g, 1], proj[g, 2], window, dilation)
        outs.append(o_g)
        lses.append(lse_g)
    o = jnp.stack(outs)
    w = jax.nn.softmax(jnp.stack(lses), axis=0)
    o = jnp.einsum('gbhs,gbhsd->bshd', w.astype(o.dtype), o).reshape(B, S, DIL_HEADS * DIL_HEAD_DIM)
    return o @ w_out

def hier_moe(h, w_grp, b_grp, w_exp, b_exp, w_gate, w_up, w_down):
    T, D = h.shape
    f32 = jnp.float32
    grp_logits = (h @ w_grp + b_grp).astype(f32)
    grp = jnp.argmax(grp_logits, axis=-1)
    p_grp = jnp.take_along_axis(jax.nn.softmax(grp_logits, axis=-1), grp[:, None], axis=-1)
    exp_logits = (h @ w_exp + b_exp).astype(f32).reshape(T, MOE_GROUPS, MOE_PER_GROUP)
    in_grp = jnp.take_along_axis(exp_logits, grp[:, None, None], axis=1)[:, 0]
    p_in, top_i = lax.top_k(jax.nn.softmax(in_grp, axis=-1), MOE_TOPK)
    gate = p_grp * p_in / jnp.sum(p_in, axis=-1, keepdims=True)
    expert = grp[:, None] * MOE_PER_GROUP + top_i

    A = T * MOE_TOPK
    flat_e = expert.reshape(A)
    order = jnp.argsort(flat_e)
    sorted_e = flat_e[order]
    sorted_tok = order // MOE_TOPK
    sorted_w = gate.reshape(A)[order]
    counts = jnp.bincount(flat_e, length=MOE_EXPERTS)
    padded = (counts + MOE_BLOCK - 1) // MOE_BLOCK * MOE_BLOCK
    pad_end = jnp.cumsum(padded)
    pad_start = pad_end - padded
    start = jnp.cumsum(counts) - counts
    dest = pad_start[sorted_e] + jnp.arange(A) - start[sorted_e]
    P = (-(-A // MOE_BLOCK) + MOE_EXPERTS) * MOE_BLOCK
    NB = P // MOE_BLOCK
    slot_tok = jnp.full((P,), T, dtype=jnp.int32).at[dest].set(sorted_tok.astype(jnp.int32))
    slot_w = jnp.zeros((P,), f32).at[dest].set(sorted_w)
    blk_e = jnp.minimum(jnp.searchsorted(pad_end, jnp.arange(NB) * MOE_BLOCK, side='right'),
                        MOE_EXPERTS - 1)
    h_pad = jnp.concatenate([h, jnp.zeros((1, D), h.dtype)], axis=0)
    xb = h_pad[slot_tok].reshape(NB, MOE_BLOCK, D)

    def expert_block(args):
        x_blk, e = args
        return (jax.nn.silu(x_blk @ w_gate[e]) * (x_blk @ w_up[e])) @ w_down[e]

    yb = lax.map(expert_block, (xb, blk_e)).reshape(P, D)
    y = jax.ops.segment_sum(yb.astype(f32) * slot_w[:, None], slot_tok, num_segments=T + 1)[:T]
    return y.astype(h.dtype)

def second_inputs(seed: int = 0) -> dict:
    key = jax.random.key(seed)
    keys = jax.random.split(key, 26)
    D = D_MODEL

    def nrm(i, shape, scale):
        return jax.random.normal(keys[i], shape, jnp.float32) * scale

    sb_w = SB_HEADS * SB_HEAD_DIM
    gla_dqk = GLA_HEADS * GLA_DK
    gla_dv = GLA_HEADS * GLA_DV
    dil_w = DIL_HEADS * DIL_HEAD_DIM
    return {
        "x": nrm(0, (BATCH, SEQ, D), 1.0),
        "c": nrm(1, (BATCH, D), 1.0),
        "ada_w": nrm(2, (DEPTH, D, N_MOD * D), 0.5 * D ** -0.5),
        "ada_b": nrm(3, (DEPTH, N_MOD * D), 0.01),
        "norm_g": 1.0 + nrm(4, (DEPTH, 2, D), 0.02),
        "final_g": 1.0 + nrm(5, (D,), 0.02),
        "sb_w_in": nrm(6, (N_SB, D, 3 * sb_w), D ** -0.5),
        "sb_w_out": nrm(7, (N_SB, sb_w, D), sb_w ** -0.5),
        "gla_w_in": nrm(8, (N_GLA, D, GLA_IN), D ** -0.5),
        "gla_w_gate_up": nrm(9, (N_GLA, GLA_GATE_RANK, gla_dqk), GLA_GATE_RANK ** -0.5),
        "gla_b_gate": nrm(10, (N_GLA, gla_dqk), 0.01),
        "gla_norm_g": 1.0 + nrm(11, (N_GLA, GLA_DV), 0.02),
        "gla_w_out": nrm(12, (N_GLA, gla_dv, D), gla_dv ** -0.5),
        "conv_w_in": nrm(13, (N_CONV, D, 3 * D), D ** -0.5),
        "conv_w": nrm(14, (N_CONV, CONV_WIDTH, D), CONV_WIDTH ** -0.5),
        "conv_b": nrm(15, (N_CONV, D), 0.01),
        "conv_w_out": nrm(16, (N_CONV, D, D), D ** -0.5),
        "dil_w_in": nrm(17, (N_DIL, D, DIL_GROUPS * 3 * dil_w), D ** -0.5),
        "dil_w_out": nrm(18, (N_DIL, dil_w, D), dil_w ** -0.5),
        "moe_w_grp": nrm(19, (DEPTH, D, MOE_GROUPS), D ** -0.5),
        "moe_b_grp": nrm(20, (DEPTH, MOE_GROUPS), 0.01),
        "moe_w_exp": nrm(21, (DEPTH, D, MOE_EXPERTS), D ** -0.5),
        "moe_b_exp": nrm(22, (DEPTH, MOE_EXPERTS), 0.01),
        "moe_w_gate": nrm(23, (DEPTH, MOE_EXPERTS, D, MOE_D_FF), D ** -0.5),
        "moe_w_up": nrm(24, (DEPTH, MOE_EXPERTS, D, MOE_D_FF), D ** -0.5),
        "moe_w_down": nrm(25, (DEPTH, MOE_EXPERTS, MOE_D_FF, D), MOE_D_FF ** -0.5),
    }

def second_block(x, c, ada_w, ada_b, norm_g, final_g, sb_w_in, sb_w_out, gla_w_in, gla_w_gate_up,
              gla_b_gate, gla_norm_g, gla_w_out, conv_w_in, conv_w, conv_b, conv_w_out,
              dil_w_in, dil_w_out, moe_w_grp, moe_b_grp, moe_w_exp, moe_b_exp, moe_w_gate,
              moe_w_up, moe_w_down):
    B, S, D = x.shape
    cond = jax.nn.silu(c)
    for i in range(DEPTH):
        mod = cond @ ada_w[i] + ada_b[i]
        sh1, sc1, g1, sh2, sc2, g2 = jnp.split(mod[:, None, :], N_MOD, axis=-1)

        h = rms_norm_2(x, norm_g[i, 0]) * (1.0 + sc1) + sh1
        kind, j = i % N_MIXERS, i // N_MIXERS
        if kind == 0:
            y = sb_mixer(h, sb_w_in[j], sb_w_out[j])
        elif kind == 1:
            y = gla_mixer(h, gla_w_in[j], gla_w_gate_up[j], gla_b_gate[j], gla_norm_g[j], gla_w_out[j])
        elif kind == 2:
            y = conv_mixer(h, conv_w_in[j], conv_w[j], conv_b[j], conv_w_out[j])
        else:
            y = dil_mixer(h, dil_w_in[j], dil_w_out[j])
        x = (x + g1 * y).astype(x.dtype)

        h = rms_norm_2(x, norm_g[i, 1]) * (1.0 + sc2) + sh2
        y = hier_moe(h.reshape(B * S, D), moe_w_grp[i], moe_b_grp[i], moe_w_exp[i], moe_b_exp[i],
                     moe_w_gate[i], moe_w_up[i], moe_w_down[i]).reshape(B, S, D)
        x = (x + g2 * y).astype(x.dtype)
    return rms_norm_2(x, final_g)


def setup_inputs(seed=0):
    out = dict(first_inputs(seed))
    for name, value in second_inputs(seed + 1).items():
        if name != "x":
            out[name + "_2"] = value
    return out


def reference(
    x, norm_mix, w_in, conv_w, a_log, dt_bias, gdn_norm, nsa_q_norm, nsa_k_norm, cmp_pos,
    cmp_w1, cmp_w2, pool_w, pool_scale, w_out, norm_ffn, w_ffn1, w_ffn2, c_2, ada_w_2, ada_b_2,
    norm_g_2, final_g_2, sb_w_in_2, sb_w_out_2, gla_w_in_2, gla_w_gate_up_2, gla_b_gate_2,
    gla_norm_g_2, gla_w_out_2, conv_w_in_2, conv_w_2, conv_b_2, conv_w_out_2, dil_w_in_2,
    dil_w_out_2, moe_w_grp_2, moe_b_grp_2, moe_w_exp_2, moe_b_exp_2, moe_w_gate_2, moe_w_up_2,
    moe_w_down_2,
):
    x = first_block(
        x, norm_mix, w_in, conv_w, a_log, dt_bias, gdn_norm, nsa_q_norm, nsa_k_norm, cmp_pos,
        cmp_w1, cmp_w2, pool_w, pool_scale, w_out, norm_ffn, w_ffn1, w_ffn2,
    )
    return second_block(
        x, c_2, ada_w_2, ada_b_2, norm_g_2, final_g_2, sb_w_in_2, sb_w_out_2, gla_w_in_2,
        gla_w_gate_up_2, gla_b_gate_2, gla_norm_g_2, gla_w_out_2, conv_w_in_2, conv_w_2,
        conv_b_2, conv_w_out_2, dil_w_in_2, dil_w_out_2, moe_w_grp_2, moe_b_grp_2, moe_w_exp_2,
        moe_b_exp_2, moe_w_gate_2, moe_w_up_2, moe_w_down_2,
    )


_drawn_inputs = setup_inputs


def setup_inputs(seed=0):
    import zlib

    import numpy as np

    out = dict(_drawn_inputs(seed))
    spreads = {}
    factors = {'norm_mix': 3.71,
     'gdn_norm': 8.0,
     'nsa_q_norm': 8.0,
     'nsa_k_norm': 8.0,
     'cmp_pos': 4.035,
     'norm_ffn': 3.506,
     'ada_b_2': 6.147,
     'norm_g_2': 6.465,
     'final_g_2': 8.37,
     'moe_b_grp_2': 8.0,
     'moe_b_exp_2': 22.449}
    for name, (base, spread) in spreads.items():
        noise = np.random.default_rng([zlib.crc32(name.encode()), seed]).standard_normal(out[name].shape)
        drawn = base * np.exp(spread * noise) if base else spread * noise
        out[name] = __import__('jax').numpy.asarray(drawn.astype(out[name].dtype))
    for name, factor in factors.items():
        out[name] = (out[name] * factor).astype(out[name].dtype)
    return out
```

```python
from contextlib import ExitStack

import concourse.bass as bass
from concourse import mybir

F32 = mybir.dt.float32
I32 = mybir.dt.int32
ALU = mybir.AluOpType
ACT = mybir.ActivationFunctionType
X = mybir.AxisListType.X

P = 128
T = 256
NT = T // P
D = 1024
KC = D // P
EPS = 1e-6
NEG = -1e30
GH, HD = 6, 64
GW = GH * HD
HID = 256
CL, CS = 32, 16
NCB = T // CS - CL // CS + 1
POOLS = (2, 4, 8, 16)
DFF = 4 * D
SBH = D // HD
NE, EFF = 32, 512
NG, PG = 4, 8
CAP = 64
SLOT = 4096
NSLOT = 6
SCALE = HD ** -0.5

C_QKV, C_Z, C_B = 0, 3 * GW, 4 * GW
C_Q = C_B + 2 * GH
C_KV = C_Q + GW
C_GATE = C_KV + 6 * P
C_U = C_GATE + 3 * GH
D_IN = C_U + 4 * HD
IN_UNITS = [(0, 512), (512, 512), (1024, 512), (C_B, 2 * GH + GW), (C_KV, 512), (C_KV + 512, 256 + 3 * GH), (C_U, 256)]

R_MIX, R_FFN, R_NG, R_CONV, R_PS, R_ADA, R_QN, R_KN, R_GN = 0, 8, 16, 32, 68, 70, 118, 119, 122
N_ROWS = 123
R2_POS, R2_C, N_ROWS2 = 0, 32, 40


def group_table():
    g = [("cols", "D")]
    g += [(f"norm0_{b}", "D") for b in range(4)]
    g += [(f"qkv{b}", "A") for b in range(5)]
    for n in ("z", "bq"):
        g += [(f"{n}{i}", "A") for i in range(NT)]
    g += [("kcvc", "A")]
    for n in ("kv", "kw", "u"):
        g += [(f"{n}{i}", "A") for i in range(NT)]
    g += [("hid", "A"), ("pm0", "A"), ("pm1", "A"), ("py0", "D"), ("py1", "D"), ("cmp", "D")]
    g += [(f"tr{i}{b}", "A") for i in range(NT) for b in range(3)]
    g += [(f"nt{b}", "D") for b in range(3)] + [("kct", "D")]
    for i in range(NT):
        nb = 2 + i
        g += [(f"cs{i}", "D")]
        g += [(f"s{t}{i}{b}", "D") for t in "sw" for b in range(nb)]
        g += [(f"pc{i}0", "A"), (f"pc{i}1", "A")]
        g += [(f"p{t}{i}{b}", "A") for t in "sw" for b in range(nb)]
        g += [(f"no{i}", "A")]
    g += [(f"qk{b}", "A") for b in range(3)] + [("gc", "D")]
    g += [(f"r{b}", "D") for b in range(3)]
    g += [(f"kk{b}", "D") for b in range(6)]
    for lv in range(7):
        g += [(f"P{lv}{b}", "D") for b in range(3)]
        for b in range(3):
            g += ([(f"T{lv}{b}", "A")] if lv < 6 else []) + [(f"TT{lv}{b}", "A")]
    g += [("x0", "D"), ("S", "D"), ("ks1", "D"), ("x1", "D"), ("o0", "D"), ("qs1", "D"), ("o1", "D")]
    g += [(f"ya{b}", "D") for b in range(3)]
    g += [(f"out{n}{i}", "D") for n in range(2) for i in range(NT)]
    g += [(f"norm1_{b}", "D") for b in range(4)]
    g += [("mod", "D")] + [(f"gb{b}", "D") for b in range(4)]
    g += [(f"norm2_{b}", "D") for b in range(4)]
    g += [(f"sq{b}", "A") for b in range(8)]
    g += [(f"sv{n}{i}", "A") for n in range(2) for i in range(NT)]
    for s in range(SBH + 4):
        if s < SBH:
            g += [(f"Z{s}", "D")]
        if 2 <= s < SBH + 2:
            g += [(f"C{s - 2}", "D")]
        if s >= 4 and s % 2 == 1:
            g += [(f"O{(s - 4) // 2}", "A")]
    g += [(f"so{n}{i}", "D") for n in range(2) for i in range(NT)]
    g += [(f"norm3_{b}", "D") for b in range(4)]
    g += [("lg", "D")] + [(f"h2{i}{b}", "A") for i in range(NT) for b in range(2)] + [("rank", "D")]
    return g


def build(nc, a, out):
    ctx = ExitStack()
    with ctx:
        def sb(name, shape, dt=F32):
            return ctx.enter_context(nc.sbuf_tensor(name, shape, dt))

        sems = {}

        def sem(*names):
            for n in names:
                sems[n] = ctx.enter_context(nc.semaphore(n))

        PS = ctx.enter_context(nc.psum_tensor("PS", [P, 8, 512], F32))

        slots = [sb(f"slot{s}", [P, SLOT]) for s in range(NSLOT)]
        XR = sb("XR", [P, NT, D])
        XN = sb("XN", [P, NT, D])
        HT = sb("HT", [P, KC, T])
        YT = sb("YT", [P, KC, T])
        IDENT = sb("IDENT", [P, P])
        UPI = sb("UPI", [P, P])
        UPS = sb("UPS", [P, P])
        ONES = sb("ONES", [P, P])
        NLOW = sb("NLOW", [P, P])
        NONES = sb("NONES", [P, P])
        LVM = sb("LVM", [P, 7, P])
        QNEG = sb("QNEG", [P, 2, P])
        SBNEG = sb("SBNEG", [P, 3, P])
        CNEG = sb("CNEG", [P, NT, 16])
        CONE = sb("CONE", [P, NT, 16])
        IOTA = sb("IOTA", [P, 4 * CAP])
        EPSC = sb("EPSC", [P, 2])
        COL = sb("COL", [P, 168])
        ROWS = sb("ROWS", [P, 2, P])
        PBC = sb("PBC", [P, 12 + 36])
        W2 = sb("W2", [P, 4, HD])
        POOLW = sb("POOLW", [P, 2, HD])
        RW = sb("RW", [P, KC, 36])
        SM = sb("SM", [P, 640])
        AR = sb("AR", [P, 17900])

        def carve(at, *dims):
            n = 1
            for d in dims:
                n *= d
            v = AR[:, at:at + n]
            if len(dims) == 2:
                v = v.rearrange("p (a b) -> p a b", b=dims[1])
            if len(dims) == 3:
                v = v.rearrange("p (a b c) -> p a b c", b=dims[1], c=dims[2])
            return v

        at = 0
        TOK = carve(at, NT, 18, HD); at += NT * 18 * HD
        NTT = carve(at, 5, T); at += 5 * T
        QKT = carve(at, 6, T); at += 6 * T
        SIG = carve(at, NT, 408); at += NT * 408
        SG = carve(at, NT, 408); at += NT * 408
        VS = carve(at, NT, P); at += NT * P
        VW = carve(at, NT, P); at += NT * P
        B0 = at
        QKVT = carve(at, 9, 3 + T); at += 9 * (3 + T)
        CV = carve(at, 9, T); at += 9 * T
        EX = carve(at, 9, T); at += 9 * T
        D0 = at
        UTOK = QKT[:, 0:2, :]
        MT = QKT[:, 2:4, :]
        XK = carve(at, 2, 3, T); at += 2 * 3 * T
        NQK = carve(at, NT, 10, HD); at += NT * 10 * HD
        HIDT = carve(at, 4, 45); at += 180
        HX = carve(at, 4, 30); at += 120
        KCN = carve(at, 64); at += 64
        VC = carve(at, 2, HD); at += 128
        KCT = carve(at, 16); at += 16
        RCP = NTT[:, 0:4, :]
        assert at <= 17900, at
        BAND = XN[:, :, :].rearrange("p a b -> p (a b)").rearrange("p (w i t) -> p w i t", w=4, i=NT)
        at = B0
        PR = {"s": carve(at, GH, T), "w": carve(at + GH * T, GH, T)}
        at += 2 * GH * T
        PT = {"s": carve(at, 2, GH * P), "w": carve(at + 2 * GH * P, 2, GH * P)}
        at += 4 * GH * P
        PCM = carve(at, GH, 16); at += 96
        PCT = carve(at, GH, P); at += GH * P
        assert at <= 17900, at
        at = B0
        TM = carve(at, 12, P); at += 12 * P
        TTM = carve(at, 12, P); at += 12 * P
        PM = carve(at, 12, P); at += 12 * P
        DEC = carve(at, 12, P); at += 12 * P
        LT = carve(at, 12, P); at += 12 * P
        QKD = carve(at, 12, P); at += 12 * P
        VN = PM.rearrange("p a b -> p (a b)")[:, 0:2 * GW].rearrange("p (i h d) -> p i h d", i=NT, h=GH)
        OT2 = DEC.rearrange("p a b -> p (a b)")[:, 0:2 * GW].rearrange("p (i h d) -> p i h d", i=NT, h=GH)
        TMP = DEC.rearrange("p a b -> p (a b)")[:, 2 * GW:4 * GW].rearrange("p (i h d) -> p i h d", i=NT, h=GH)
        SST = TM.rearrange("p a b -> p (a b)")[:, 0:3 * HD].rearrange("p (j d) -> p j d", d=HD)
        KD = TM.rearrange("p a b -> p (a b)")[:, 256:256 + GW].rearrange("p (h d) -> p h d", h=GH)
        RHS = TM.rearrange("p a b -> p (a b)")[:, 700:700 + GW].rearrange("p (h d) -> p h d", h=GH)
        assert at <= 17900, at

        AT = carve(0, 2, 4 * T)
        ADW = 384
        ADA = carve(2048, 2, KC, ADW)
        ACC = carve(2048 + 2 * KC * ADW, 6 * D)
        at = 2048 + 2 * KC * ADW + 6 * D
        G12 = carve(at, 2, D); at += 2 * D
        FG = carve(at, D); at += D
        MODC = carve(at, 48); at += 48
        COND = carve(at, 16); at += 16
        assert at <= 17900, at
        SQK = carve(0, 16, T)
        SV = carve(4096, NT, D)
        at = 6144
        SPB = carve(at, 3, 3 * P); at += 9 * P
        SAB = carve(at, 3, 3 * P); at += 9 * P
        SA = carve(at, 3, 3 * P); at += 9 * P
        at = 0
        H2 = XN
        LG = carve(at, NT, 36); at += 72
        RT = carve(at, 24 * NT * 8); at += 24 * NT * 8
        E32 = carve(at, 8, NT * NE); at += 8 * NT * NE
        KEY = carve(at, NT, NE + 2); at += NT * (NE + 2)
        WT = carve(at, NT, NE + 2); at += NT * (NE + 2)
        REV = carve(at, 8); at += 8
        SEL = carve(at, NT, 2 * CAP); at += NT * 2 * CAP
        SELW = carve(at, NT, 2 * CAP); at += NT * 2 * CAP
        HS = carve(at, KC, 2 * CAP); at += KC * 2 * CAP
        ES = carve(at, EFF); at += EFF
        AM = carve(at, EFF); at += EFF
        AC = carve(at, 4, 2 * CAP); at += 4 * 2 * CAP
        GT = carve(at, T); at += T
        YB = carve(at, D); at += D
        OVN = T * 2 // (CAP + 1)
        OVK = carve(at, NT, OVN); at += NT * OVN
        OVW = carve(at, NT, OVN); at += NT * OVN
        OVS = carve(at, 2, OVN, NE); at += 2 * OVN * NE
        OVF = carve(at, 16); at += 16
        OVI = carve(at, 16).bitcast(I32); at += 16
        assert at <= 2048 + 2 * KC * ADW + 6 * D, at

        YTMP = XN[:, :, :]

        def rv(k, n):
            return RT[:, 16 * k:16 * k + NT * n].rearrange("p (i n) -> p i n", n=n)

        sm = [0]

        def small(*dims):
            n = 1
            for d in dims:
                n *= d
            v = SM[:, sm[0]:sm[0] + n]
            sm[0] += n
            assert sm[0] <= 640
            return v.rearrange("p (a b) -> p a b", b=dims[1]) if len(dims) == 2 else v

        SS = small(2)
        LNV = small(2)
        RSTD = small(2)
        N2 = small(24)
        RN = small(24)
        M2 = small(20)
        MR = small(20)
        SPV = small(NT, 6)
        SPE = small(NT, 6)
        GG = small(NT, 6)
        EA = small(6)
        GCS = small(12)
        GLS = small(6)
        EGC = small(6)
        KDE = small(6)
        MX = small(6)
        NMX = small(6)
        SUM = small(6)
        CF = small(6)
        CSUM = small(3, 6)
        O2 = small(12)
        OR = small(12)
        KN2 = small(2)
        BG = small(NT, 12)

        sem("x_loaded", "rows_loaded", "misc_loaded", "const_ready", "filled", "emptied_by_act", "emptied_by_dve",
            "halves_switched", "pool_step", "act_step", "dve_step", "rstd_ready", "xn_ready", "counts_ready",
            "recip_ready", "sig_exp", "conv_ready", "conv_exp", "silu_ready", "qk_sumsq", "qk_rnorm", "qk_ready",
            "hid_bias", "hid_exp", "hid_ready", "nqk_sumsq", "nqk_rnorm", "nqk_ready", "kc_sumsq", "kc_rnorm",
            "kc_ready", "pos_ready", "cmax", "cexp", "smax", "sexp", "probs_ready", "dt_added", "dt_parts",
            "g_ready", "decay_exp", "egc_ready", "lt_ready", "pm_ready", "rhs_ready", "o_sumsq", "o_rnorm",
            "ya_ready", "stored", "kd_ready", "x_ready", "ffn_hid_filled", "ffn_out_done", "ffn_relu",
            "ffn_act_ready", "ada_used0", "ada_used1", "ada_loaded0", "ada_loaded1", "ada_step", "rows_bc",
            "cond_exp", "sp_ln", "sp_ready", "gr_in", "gr_exp", "t2_in", "t2_exp", "onehot_ready", "over_ready",
            "out_ready", "down_filled", "hs0_ready", "hs1_ready", "gt_ready", "yb0_ready", "yb1_ready", "sel_ready",
            "selw_ready", "x_done", "sa_ready", "gate_filled", "up_filled", "gathered", "gate_exp", "hid_turned",
            "weights_turned", "ac_ready", "am_ready", "silu_step")
        for s in range(NSLOT):
            sem(f"loaded{s}")

        GROUPS = group_table()
        order = {n: k for k, (n, _) in enumerate(GROUPS)}

        def owner_count(k):
            return sum(o == GROUPS[k][1] for _, o in GROUPS[:k + 1])

        def bank(name):
            return PS[:, order[name] % 8, :]

        class Steps:

            def __init__(self, eng, name):
                self.eng, self.sem, self.n = eng, sems[name], 0

            def __call__(self, ins):
                self.n += 1
                ins.then_inc(self.sem, 1)
                self.eng.wait_ge(self.sem, self.n)

        emptied = {"A": sems["emptied_by_act"], "D": sems["emptied_by_dve"]}

        def pe_open(pe, name):
            k = order[name]
            if k >= 8:
                pe.wait_ge(emptied[GROUPS[k - 8][1]], owner_count(k - 8))
            return bank(name)

        def wait_emptied(eng, name):
            k = order[name]
            eng.wait_ge(emptied[GROUPS[k][1]], owner_count(k))

        def pv_seen(h):
            return order[f"Z{h + 5}" if h + 5 < SBH else (f"C{h + 3}" if h + 3 < SBH else f"O{h // 2}")] + 1

        def wait_filled(eng, name):
            eng.wait_ge(sems["filled"], order[name] + 1)
            return bank(name)

        uses = [("in0", 0, "qkv1"), ("in1", 1, "qkv3"), ("in2", 2, "z1"), ("in3", 3, "bq1"), ("in4", 4, "kv1"),
                ("in5", 5, "kw1"), ("in6", 0, "u1"), ("w1k", 1, "hid"), ("w1v", 2, "hid"), ("out0", 3, "out01"),
                ("out1", 4, "out11")]
        uses += [(f"ffn{v}{s}", s, None) for v in range(4) for s in range(4)]
        uses += [("sb0", 5, "sq1"), ("sb1", 4, "sq3"), ("sb2", 0, "sq5"), ("sb3", 1, "sq7"), ("sb4", 2, "sv01"),
                 ("sb5", 3, "sv11"), ("so0", 5, "so01"), ("so1", 4, "so11")]

        def use(name):
            k = [n for n, _, _ in uses].index(name)
            s = uses[k][1]
            return s, sum(t == s for _, t, _ in uses[:k + 1])

        def last_reader(name):
            k = [n for n, _, _ in uses].index(name)
            before = [r for _, t, r in uses[:k] if t == uses[k][1]]
            return before[-1] if before else None

        def bc(ap, axis, n):
            v = ap.unsqueeze(axis)
            shape = list(v.shape)
            shape[axis] = n
            return v.to_broadcast(shape)

        block = ctx.enter_context(nc.Block())

        @block.sync
        def _(sp):
            def fill(s, src):
                return sp.dma_start(slots[s][:, 0:src.shape[1] * src.shape[2]].rearrange("p (c n) -> p c n", n=src.shape[2]), src)\
                    .then_inc(sems[f"loaded{s}"], 16)

            def load(name, src):
                s, n = use(name)
                r = last_reader(name)
                if r is not None:
                    sp.wait_ge(sems["filled"], order[r] + 1)
                fill(s, src)

            for i in range(NT):
                sp.dma_start(XR[:, i, :], a["x"][0, i * P:(i + 1) * P, :]).then_inc(sems["x_loaded"], 16)
            w_in = a["w_in"][0].rearrange("(c p) n -> p c n", p=P)
            for u, (c0, w) in enumerate(IN_UNITS):
                load(f"in{u}", w_in[:, :, c0:c0 + w])
            for kv, n in enumerate(("w1k", "w1v")):
                load(n, a["cmp_w1"][0, kv].rearrange("(m p) n -> p m n", p=P))
            w_out = a["w_out"][0].rearrange("(c p) n -> p c n", p=P)
            for h in range(2):
                load(f"out{h}", w_out[:, :, h * 512:(h + 1) * 512])
            sb_in = a["sb_w_in_2"][0].rearrange("(c p) n -> p c n", p=P)
            sb_out = a["sb_w_out_2"][0].rearrange("(c p) n -> p c n", p=P)
            w_f1 = a["w_ffn1"][0].rearrange("(c p) n -> p c n", p=P)
            w_f2 = a["w_ffn2"][0].rearrange("(u c p) n -> u p c n", c=4, p=P)
            w_ada = a["ada_w_2"][0].rearrange("(c p) n -> p c n", p=P)

            def ffn_round(v, first):
                for j in range(2):
                    if not first:
                        sp.wait_ge(sems["ffn_hid_filled"], 4 * v - 2 + 2 * j)
                    fill(2 * j, w_f1[:, :, bass.ds((2 * v + j) * 512, 512)])
                    if not first:
                        sp.wait_ge(sems["ffn_out_done"], 2 * v - 1 + j)
                    fill(2 * j + 1, w_f2[bass.ds(2 * v + j, 1), :, :, :].rearrange("u p c n -> p (u c) n"))
                    for k in range(2):
                        if not (first and j == 0):
                            sp.wait_ge(sems[f"ada_used{k}"], 2 * v + j)
                        sp.dma_start(ADA[:, k], w_ada[:, :, bass.ds((4 * v + 2 * j + k) * ADW, ADW)])\
                            .then_inc(sems[f"ada_loaded{k}"], 16)

            load("sb0", sb_in[:, :, 0:512])
            for s, r in ((0, "u1"), (1, "hid"), (2, "hid"), (3, "out01")):
                sp.wait_ge(sems["filled"], order[r] + 1)
            wait_emptied(sp, "norm1_0")
            ffn_round(0, True)
            with sp.Fori(1, 4) as v:
                ffn_round(v, False)
            load("sb1", sb_in[:, :, 512:1024])
            sp.wait_ge(sems["ffn_hid_filled"], 14)
            fill(0, sb_in[:, :, 1024:1536])
            sp.wait_ge(sems["ffn_out_done"], 7)
            fill(1, sb_in[:, :, 1536:2048])
            sp.wait_ge(sems["ffn_hid_filled"], 16)
            fill(2, sb_in[:, :, 2048:2560])
            sp.wait_ge(sems["ffn_out_done"], 8)
            fill(3, sb_in[:, :, 2560:3072])
            for k, seg in enumerate((2, 5)):
                sp.dma_start(G12[:, k, :], a["ada_b_2"][0, seg * D:(seg + 1) * D].partition_broadcast(P)).then_inc(sems["rows_bc"], 16)
            sp.dma_start(FG[:, :], a["final_g_2"].partition_broadcast(P)).then_inc(sems["rows_bc"], 16)
            load("so0", sb_out[:, :, 0:512])
            load("so1", sb_out[:, :, 512:1024])
            gate = a["moe_w_gate_2"][0].rearrange("e (c p) n -> e p c n", p=P)
            up = a["moe_w_up_2"][0].rearrange("e (c p) n -> e p c n", p=P)
            down = a["moe_w_down_2"][0].rearrange("e (c p) n -> e p c n", p=P)

            def expert(w, e, s):
                fill(s, w[bass.ds(e, 1), :, :, :].rearrange("e p c n -> p (e c) n"))

            freeing = {0: ("gate_filled", 1), 3: ("gate_filled", 1), 1: ("up_filled", 1), 4: ("up_filled", 1),
                       2: ("down_filled", 2), 5: ("down_filled", 2)}
            for w, e, s, r in ((gate, 0, 0, "sq5"), (up, 0, 1, "sq7"), (down, 0, 2, "sv01"), (gate, 1, 3, "sv11"),
                               (down, 1, 5, "so01"), (up, 1, 4, "so11")):
                sp.wait_ge(sems["filled"], order[r] + 1)
                expert(w, e, s)
            with sp.Fori(1, NE // 2) as m:
                for w, e, s in ((gate, 0, 0), (gate, 1, 3), (up, 0, 1), (up, 1, 4), (down, 0, 2), (down, 1, 5)):
                    name, per = freeing[s]
                    sp.wait_ge(sems[name], per * m)
                    expert(w, 2 * m + e, s)
            sp.wait_ge(sems["over_ready"], 1)
            n_over = sp.value_load(OVI[0:1, OVN:OVN + 1], min_val=0, max_val=OVN)
            with sp.Fori(0, OVN) as k:
                with sp.If(n_over > k):
                    e = sp.value_load(OVI[0:1, bass.ds(k, 1)], min_val=0, max_val=NE - 1)
                    for s, w in ((0, gate), (1, up), (2, down)):
                        name, per = freeing[s]
                        sp.wait_ge(sems[name], k + per * (NE // 2))
                        expert(w, e, s)
            for i in range(NT):
                sp.wait_ge(sems["out_ready"], i + 1)
                sp.dma_start(out[0, i * P:(i + 1) * P, :], XR[:, i, :]).then_inc(sems["stored"], 16)
            sp.wait_ge(sems["stored"], 16 * NT)

        @block.gpsimd
        def _(pool):
            step = Steps(pool, "pool_step")
            ready = sems["const_ready"]

            def tri(t, fill_true, cond, base, mult, pattern, op=ALU.is_ge, fill=0.0):
                step(pool.affine_select(out=t, in_=t, compare_op=op, fill=fill, base=base,
                                        pattern=pattern, channel_multiplier=mult))

            step(pool.memset(IDENT[:, :], 0.0))
            pool.affine_select(out=IDENT[:, :], in_=IDENT[:, :], compare_op=ALU.not_equal, fill=1.0, base=0,
                               pattern=[[-1, P]], channel_multiplier=1).then_inc(ready, 1)
            pool.memset(EPSC[:, 0:1], EPS)
            step(pool.memset(EPSC[:, 1:2], 1.0))
            pool.memset(ONES[:, :], 1.0)
            pool.memset(NONES[:, :], -1.0)
            pool.memset(QKVT[:, :, 0:3], 0.0)
            pool.memset(XK[:, :, 2, :], 0.0)
            pool.memset(NLOW[:, :], -1.0)
            pool.memset(UPI[:, :], 1.0)
            step(pool.memset(UPS[:, :], 1.0))
            pool.affine_select(out=UPI[:, :], in_=UPI[:, :], compare_op=ALU.is_ge, fill=0.0, base=0,
                               pattern=[[1, P]], channel_multiplier=-1)
            pool.affine_select(out=UPS[:, :], in_=UPS[:, :], compare_op=ALU.is_gt, fill=0.0, base=0,
                               pattern=[[1, P]], channel_multiplier=-1)
            pool.affine_select(out=NLOW[:, :], in_=NLOW[:, :], compare_op=ALU.is_ge, fill=0.0, base=0,
                               pattern=[[-1, P]], channel_multiplier=1).then_inc(ready, 1)
            TP = SG[:, :, :].rearrange("p a b -> p (a b)")
            tp1 = TP[:, 0:T]
            pool.iota(tp1, [[1, T]], base=1, channel_multiplier=0,
                      allow_small_or_imprecise_dtypes=True).then_inc(sems["counts_ready"], 1)
            pool.wait_ge(sems["filled"], order["norm0_3"] + 1)
            for w in range(4):
                step(pool.memset(BAND[:, w], 1.0))
                step(pool.affine_select(out=BAND[:, w], in_=BAND[:, w], compare_op=ALU.is_ge, fill=0.0, base=0,
                                        pattern=[[-P, NT], [1, T]], channel_multiplier=-1))
                step(pool.affine_select(out=BAND[:, w], in_=BAND[:, w], compare_op=ALU.is_ge, fill=0.0,
                                        base=POOLS[w] - 1, pattern=[[P, NT], [-1, T]], channel_multiplier=1))
            pool.wait_ge(sems["recip_ready"], 1)
            for w in range(4):
                for i in range(NT):
                    ins = pool.tensor_tensor(BAND[:, w, i], BAND[:, w, i], RCP[:, w, :], ALU.mult)
            step(ins)
            for w in range(4):
                for i in range(NT):
                    last = pool.tensor_tensor(BAND[:, w, i, i * P:(i + 1) * P], BAND[:, w, i, i * P:(i + 1) * P],
                                              IDENT[:, :], ALU.subtract)
            last.then_inc(ready, 1)
            pool.memset(QNEG[:, :, :], 0.0)
            pool.memset(CNEG[:, :, :], 0.0)
            pool.memset(SBNEG[:, :, :], 0.0)
            step(pool.memset(CONE[:, :, :], 1.0))
            pool.affine_select(out=QNEG[:, 1, :], in_=QNEG[:, 1, :], compare_op=ALU.is_ge, fill=NEG, base=0,
                               pattern=[[-1, P]], channel_multiplier=1)
            for m, fill in ((CNEG, NEG), (CONE, 0.0)):
                last = pool.affine_select(out=m[:, :, :], in_=m[:, :, :], compare_op=ALU.is_ge, fill=fill,
                                          base=-(CL - 1), pattern=[[P, NT], [-CS, 16]], channel_multiplier=1)
            for j in (0, 2):
                last = pool.affine_select(out=SBNEG[:, j, :], in_=SBNEG[:, j, :], compare_op=ALU.is_gt, fill=NEG,
                                          base=0, pattern=[[1, P]], channel_multiplier=-1)
            last.then_inc(ready, 1)
            for lv in range(7):
                b = 1 << lv
                v = LVM[:, lv, :].rearrange("p (n h r) -> p n h r", h=2, r=b)
                pool.memset(v[:, :, 0, :], -1.0)
                step(pool.memset(v[:, :, 1, :], 0.0))
                w = LVM[:, lv, :].rearrange("p (n r) -> p n r", r=2 * b)
                step(pool.affine_select(out=w, in_=w, compare_op=ALU.is_ge, fill=0.0, base=-b,
                                        pattern=[[-2 * b, P // (2 * b)], [0, 2 * b]], channel_multiplier=1))
                last = pool.affine_select(out=w, in_=w, compare_op=ALU.is_ge, fill=0.0, base=2 * b - 1,
                                          pattern=[[2 * b, P // (2 * b)], [0, 2 * b]], channel_multiplier=-1)
            last.then_inc(ready, 1)
            pool.iota(IOTA[:, :], [[1, 4 * CAP]], base=0, channel_multiplier=0,
                      allow_small_or_imprecise_dtypes=True).then_inc(ready, 1)

        @block.scalar
        def _(act):
            step = Steps(act, "act_step")
            pieces = [
                (R_MIX, a["norm_mix"][0].rearrange("(r p) -> r p", p=P), 0, P),
                (R_FFN, a["norm_ffn"][0].rearrange("(r p) -> r p", p=P), 0, P),
                (R_NG, a["norm_g_2"][0].rearrange("n (r p) -> (n r) p", p=P), 0, P),
                (R_CONV, a["conv_w"][0].rearrange("k (r p) -> (k r) p", p=P), 0, P),
                (R_PS, a["pool_scale"][0].rearrange("(r p) -> r p", p=P), 0, P),
                (R_ADA, a["ada_b_2"][0].rearrange("(r p) -> r p", p=P), 0, P),
            ]
            for h in range(2):
                pieces += [
                    (R_QN, a["nsa_q_norm"], h * HD, HD),
                    (R_KN, a["nsa_k_norm"][0], h * HD, HD),
                    (R_GN, a["gdn_norm"], h * HD, HD),
                ]
            for r, src, c, w in pieces:
                act.dma_start(ROWS[r:r + src.shape[0], 0, c:c + w], src).then_inc(sems["rows_loaded"], 16)
            for kv in range(2):
                act.dma_start(ROWS[R2_POS + kv * 16:R2_POS + kv * 16 + 16, 1, :],
                              a["cmp_pos"][0, kv].rearrange("(m l) d -> m (l d)", l=2)).then_inc(sems["rows_loaded"], 16)
            act.dma_start(ROWS[R2_C:R2_C + 8, 1, :], a["c_2"][0].rearrange("(r p) -> r p", p=P)).then_inc(sems["rows_loaded"], 16)
            act.dma_start(PBC[:, 0:6], a["a_log"][0].partition_broadcast(P)).then_inc(sems["misc_loaded"], 16)
            act.dma_start(PBC[:, 6:12], a["dt_bias"][0].partition_broadcast(P)).then_inc(sems["misc_loaded"], 16)
            act.dma_start(W2[:, :, :].rearrange("p (k m) d -> p k m d", m=2),
                          a["cmp_w2"][0].rearrange("k (m p) d -> p k m d", p=P)).then_inc(sems["misc_loaded"], 16)
            act.dma_start(POOLW[:, :, :], a["pool_w"][0].rearrange("(j g) c d -> (g c) j d", g=2)).then_inc(sems["misc_loaded"], 16)
            act.dma_start(PBC[:, 12:16], a["moe_b_grp_2"][0].partition_broadcast(P)).then_inc(sems["misc_loaded"], 16)
            act.dma_start(PBC[:, 16:48], a["moe_b_exp_2"][0].partition_broadcast(P)).then_inc(sems["misc_loaded"], 16)
            act.dma_start(RW[:, :, 0:4], a["moe_w_grp_2"][0].rearrange("(c p) n -> p c n", p=P)).then_inc(sems["misc_loaded"], 16)
            act.dma_start(RW[:, :, 4:36], a["moe_w_exp_2"][0].rearrange("(c p) n -> p c n", p=P)).then_inc(sems["misc_loaded"], 16)

            def rsqrt(dst, src, scale, tmp, done):
                step(act.activation(tmp, src, ACT.Ln, scale=scale, bias=EPSC[0:src.shape[0], 0:1]))
                act.activation(dst, tmp, ACT.Exp, scale=-0.5).then_inc(done, 1)

            def norm_stats(n):
                for i in range(NT):
                    step(act.activation(XN[:, i, :], XR[:, i, :], ACT.Square, accum_out=SS[:, i:i + 1]))
                rsqrt(RSTD, SS, 1.0 / D, LNV, sems["rstd_ready"])

            def empty(name, *pairs):
                b = wait_filled(act, name)
                for k, (dst, src) in enumerate(pairs):
                    ins = act.activation(dst, src(b), ACT.Copy)
                ins.then_inc(sems["emptied_by_act"], 1)

            act.wait_ge(sems["const_ready"], 1)
            act.wait_ge(sems["pool_step"], 2)
            act.wait_ge(sems["x_loaded"], 16 * NT)
            norm_stats(0)

            act.wait_ge(sems["const_ready"], 2)
            for b in range(5):
                n = 2 if b < 4 else 1
                empty(f"qkv{b}", (QKVT[:, 2 * b:2 * b + n, 3:3 + T], lambda s, n=n: s[:, 0:n * T].rearrange("p (j t) -> p j t", t=T)))
            for i in range(NT):
                if i == 0:
                    act.wait_ge(sems["const_ready"], 3)
                empty(f"z{i}", (SIG[:, i, 0:GW], lambda s: s[:, 0:GW]))
            for i in range(NT):
                empty(f"bq{i}",
                      (BG[:, i, :], lambda s: s[:, 0:12]),
                      (SIG[:, i, GW:GW + 6], lambda s: s[:, 0:6]),
                      (NQK[:, i, 0:6, :].rearrange("p (j g) d -> p g j d", g=2),
                       lambda s: s[:, 12:12 + GW].rearrange("p (g j d) -> p g j d", g=2, d=HD)))
            act.wait_ge(sems["conv_ready"], 1)
            act.activation(EX[:, :, :], CV[:, :, :], ACT.Exp, scale=-1.0).then_inc(sems["conv_exp"], 1)
            parts = []
            for kv in range(2):
                for h in range(2):
                    for l in range(2):
                        parts.append((XK[l * HD:(l + 1) * HD, kv, h, 0:T - l],
                                      lambda s, kv=kv, h=h, l=l: s[h * HD:(h + 1) * HD, kv * T + l:(kv + 1) * T]))
            empty("kcvc", *parts)
            for i in range(NT):
                empty(f"kv{i}", (NQK[:, i, 6:8, :], lambda s: s[:, 0:P].rearrange("p (h d) -> p h d", d=HD)),
                      (VS[:, i, :], lambda s: s[:, P:2 * P]))
            for i in range(NT):
                empty(f"kw{i}", (NQK[:, i, 8:10, :], lambda s: s[:, 0:P].rearrange("p (h d) -> p h d", d=HD)),
                      (VW[:, i, :], lambda s: s[:, P:2 * P]),
                      (SIG[:, i, GW + 6:GW + 24], lambda s: s[:, 2 * P:2 * P + 18]))
            for i in range(NT):
                empty(f"u{i}", (UTOK[:, i, :], lambda s: s[:, 0:T]))
            wait_emptied(act, "u1")
            act.activation(SG[:, :, :], SIG[:, :, :], ACT.Exp, scale=-1.0).then_inc(sems["sig_exp"], 1)
            act.wait_ge(sems["dt_added"], 1)
            step(act.activation(SPE, SPV, ACT.Abs))
            step(act.activation(SPE, SPE, ACT.Exp, scale=-1.0))
            act.activation(EA, PBC[:, 0:6], ACT.Exp)
            act.activation(SPE, SPE, ACT.Ln, bias=EPSC[:, 1:2]).then_inc(sems["dt_parts"], 1)
            empty("hid", (HIDT[:, :, :], lambda s: s[:, 0:180].rearrange("p (g n) -> p g n", n=45)))
            for j in range(2):
                empty(f"pm{j}", (MT[:, j, :], lambda s: s[:, 0:T]))
            act.wait_ge(sems["hid_bias"], 1)
            act.activation(HIDT[:, :, 0:30], HX[:, :, :], ACT.Exp, scale=-1.0).then_inc(sems["hid_exp"], 1)
            for i in range(NT):
                for b in range(3):
                    n = 4 if b < 2 else 1
                    empty(f"tr{i}{b}", (TOK[:, i, 8 * b:8 * b + 2 * n, :],
                                        lambda s, n=n: s[:, 0:n * P].rearrange("p (h d) -> p h d", d=HD)))
            act.wait_ge(sems["nqk_sumsq"], 1)
            rsqrt(MR, M2, 1.0 / HD, N2[:, 0:20], sems["nqk_rnorm"])
            act.wait_ge(sems["kc_sumsq"], 1)
            rsqrt(KN2[0:30, 1:2], KN2[0:30, 0:1], 1.0 / HD, LNV[0:30, 0:1], sems["kc_rnorm"])
            act.wait_ge(sems["qk_sumsq"], 1)
            rsqrt(RN, N2, 1.0, EX[:, 0, 0:24], sems["qk_rnorm"])
            for i in range(NT):
                nb = 2 + i
                w = (i + 1) * P
                act.wait_ge(sems["cmax"], i + 1)
                act.activation(PCM[:, :, 0:NCB], PCM[:, :, 0:NCB], ACT.Exp, scale=SCALE).then_inc(sems["cexp"], 1)
                for t in range(2):
                    act.wait_ge(sems["smax"], 2 * i + t + 1)
                    for h in range(GH):
                        ins = act.activation(PR["sw"[t]][:, h, 0:w], PR["sw"[t]][:, h, 0:w], ACT.Exp, scale=SCALE,
                                             bias=(NMX if t == 0 else MX)[:, h:h + 1],
                                             accum_out=(SUM if t == 0 else CF)[:, h:h + 1])
                    ins.then_inc(sems["sexp"], 1)
                if i > 0:
                    act.wait_ge(sems["filled"], order[f"no{i - 1}"] + 1)
                for j in range(2):
                    empty(f"pc{i}{j}", (PCT[0:NCB, 3 * j:3 * j + 3, :],
                                        lambda s: s[0:NCB, 0:3 * P].rearrange("p (h q) -> p h q", q=P)))
                for t in "sw":
                    for b in range(nb):
                        if i == 0:
                            n = 4 if b == 0 else 2
                            empty(f"p{t}{i}{b}", (PT[t][:, 0, 4 * b * P:(4 * b + n) * P], lambda s, n=n: s[:, 0:n * P]))
                        else:
                            empty(f"p{t}{i}{b}", (PT[t][:, :, 2 * b * P:(2 * b + 2) * P],
                                                  lambda s: s[:, 0:512].rearrange("p (k q) -> p k q", k=2)))
                empty(f"no{i}", (YT[:, 3:6, i * P:(i + 1) * P], lambda s: s[:, 0:3 * P].rearrange("p (j q) -> p j q", q=P)))
            for b in range(3):
                empty(f"qk{b}", (QKT[:, 2 * b:2 * b + 2, :], lambda s: s[:, 0:512].rearrange("p (j t) -> p j t", t=T)))
            wait_emptied(act, "r2")
            act.activation(DEC[:, :, :], DEC[:, :, :], ACT.Exp).then_inc(sems["decay_exp"], 1)
            act.activation(EGC, GCS[:, 6:12], ACT.Exp)
            act.activation(KDE, KDE, ACT.Exp).then_inc(sems["egc_ready"], 1)
            for lv in range(7):
                for b in range(3):
                    v4 = lambda s: s[:, 0:512].rearrange("p (a b) -> p a b", b=P)
                    if lv < 6:
                        empty(f"T{lv}{b}", (TM[:, 4 * b:4 * b + 4, :], v4))
                    empty(f"TT{lv}{b}", (TTM[:, 4 * b:4 * b + 4, :], v4))
            act.wait_ge(sems["o_sumsq"], 1)
            rsqrt(OR, O2, 1.0 / HD, M2[:, 0:12], sems["o_rnorm"])
            wait_emptied(act, "out11")
            norm_stats(1)
            act.activation(COND[:, 8:16], COL[:, P + R2_C:P + R2_C + 8], ACT.Exp, scale=-1.0).then_inc(sems["cond_exp"], 1)

            def ffn_units(v, first):
                for j in range(2):
                    if not first:
                        act.wait_ge(sems["ffn_out_done"], 2 * v - 1 + j)
                    for k in range(2):
                        act.wait_ge(sems["ffn_hid_filled"], 4 * v + 2 * j + k + 1)
                        act.activation(AT[:, j, k * 512:(k + 1) * 512], PS[:, 2 * j + k, :], ACT.Relu).then_inc(sems["ffn_relu"], 1)
                    for k in range(2):
                        act.wait_ge(sems["ffn_relu"], 4 * v + 2 * j + k + 1)
                        act.activation(AT[:, j, k * 512:(k + 1) * 512], AT[:, j, k * 512:(k + 1) * 512], ACT.Square)\
                            .then_inc(sems["ffn_act_ready"], 1)

            ffn_units(0, True)
            with act.Fori(1, 4) as v:
                ffn_units(v, False)
            act.wait_ge(sems["x_ready"], 1)
            norm_stats(2)
            for b in range(8):
                bk = wait_filled(act, f"sq{b}")
                act.activation(SQK[:, 2 * b:2 * b + 2, :], bk[:, 0:512].rearrange("p (j t) -> p j t", t=T), ACT.Copy,
                               scale=SCALE if b < 4 else 1.0).then_inc(sems["emptied_by_act"], 1)
            for n in range(2):
                for i in range(NT):
                    empty(f"sv{n}{i}", (SV[:, i, n * 512:(n + 1) * 512], lambda s: s[:, 0:512]))
            for s in range(SBH + 4):
                if s < SBH:
                    b = wait_filled(act, f"Z{s}")
                    if s >= 3:
                        wait_emptied(act, f"Z{s - 3}")
                    ln = SAB[:, s % 3, :]
                    step(act.activation(ln, b[:, 0:3 * P], ACT.Abs))
                    step(act.activation(ln, ln, ACT.Exp, scale=-1.0))
                    act.activation(ln, ln, ACT.Ln, bias=EPSC[:, 1:2]).then_inc(sems["sp_ln"], 1)
                if 2 <= s < SBH + 2:
                    wait_emptied(act, f"C{s - 2}")
                    w = SA[:, (s - 2) % 3, :]
                    act.activation(w, w, ACT.Exp).then_inc(sems["sa_ready"], 1)
                if s >= 4 and s % 2 == 1:
                    j = (s - 4) // 2
                    empty(f"O{j}", (YT[:, j, :], lambda s: s[:, 0:T]))
            wait_emptied(act, "so11")
            norm_stats(3)
            act.wait_ge(sems["gr_in"], 1)
            act.activation(rv(4, 4), rv(4, 4), ACT.Exp).then_inc(sems["gr_exp"], 1)
            for i in range(NT):
                for b in range(2):
                    empty(f"h2{i}{b}", (H2[:, i, b * 512:(b + 1) * 512], lambda s: s[:, 0:512]))
            act.wait_ge(sems["t2_in"], 1)
            act.activation(rv(16, 1), rv(16, 1), ACT.Exp).then_inc(sems["t2_exp"], 1)

            def half_of_tokens(count):
                act.wait_ge(sems["gathered"], count)
                act.activation(HS[:, 4:8, :], PS[:, 7, :].rearrange("p (c n) -> p c n", n=2 * CAP), ACT.Copy)\
                    .then_inc(sems["hs1_ready"], 1)

            def expert_copies(m, width):
                act.wait_ge(sems["gate_filled"], m + 1)
                act.activation(ES[:, 0:width], PS[:, 4, 0:width], ACT.Exp, scale=-1.0).then_inc(sems["gate_exp"], 1)

            def expert_transposed(m, width):
                act.wait_ge(sems["hid_turned"], m + 1)
                act.activation(AC[:, 0:width // P, :], PS[:, 4, 0:width].rearrange("p (f n) -> p f n", n=2 * CAP), ACT.Copy)\
                    .then_inc(sems["ac_ready"], 1)
                act.wait_ge(sems["weights_turned"], m + 1)
                act.activation(GT[:, :], PS[:, 5, 0:T], ACT.Copy).then_inc(sems["gt_ready"], 1)

            half_of_tokens(1)
            with act.Fori(0, NE // 2) as m:
                expert_copies(m, EFF)
                half_of_tokens(m + 2)
                expert_transposed(m, EFF)
                act.wait_ge(sems["down_filled"], 2 * m + 1)
                act.activation(YB[:, 0:512], PS[:, 6, :], ACT.Copy).then_inc(sems["yb0_ready"], 1)
            act.wait_ge(sems["over_ready"], 1)
            n_over = act.value_load(OVI[0:1, OVN:OVN + 1], min_val=0, max_val=OVN)
            with act.Fori(0, OVN) as k:
                with act.If(n_over > k):
                    half_of_tokens(k + NE // 2 + 2)
                    expert_copies(k + NE // 2, EFF // 2)
                    expert_transposed(k + NE // 2, EFF // 2)
                    act.wait_ge(sems["down_filled"], k + NE + 1)
                    act.activation(YB[:, 0:512], PS[:, 6, :], ACT.Copy).then_inc(sems["yb0_ready"], 1)
            act.wait_ge(sems["x_ready"], 2)
            norm_stats(4)

        @block.tensor
        def _(pe):
            filled = sems["filled"]

            def weights(name):
                s, n = use(name)
                pe.wait_ge(sems[f"loaded{s}"], 16 * n)
                return slots[s]

            class Halves:
                n, last, p0 = 0, None, None

            def half(ins=None, p0=None, fresh=False):
                if fresh:
                    Halves.last = None
                elif ins is not None:
                    Halves.last, Halves.p0 = ins, p0
                elif Halves.last is not None and Halves.p0 != p0:
                    Halves.n += 1
                    Halves.last.then_inc(sems["halves_switched"], 1)
                    pe.wait_ge(sems["halves_switched"], Halves.n)
                return ins

            pe.wait_ge(sems["const_ready"], 1)
            pe.wait_ge(sems["rows_loaded"], 16 * 15)
            b = pe_open(pe, "cols")
            pe.transpose(b[:, 0:N_ROWS], ROWS[0:N_ROWS, 0, :], IDENT[0:N_ROWS, 0:N_ROWS])
            pe.transpose(b[:, P:P + N_ROWS2], ROWS[0:N_ROWS2, 1, :], IDENT[0:N_ROWS2, 0:N_ROWS2]).then_inc(filled, 1)

            def norm_transposes(n):
                for b4 in range(4):
                    b = pe_open(pe, f"norm{n}_{b4}")
                    for c in (2 * b4, 2 * b4 + 1):
                        for i in range(NT):
                            if b4 == 0 and c == 0:
                                pe.wait_ge(sems["xn_ready"], NT * n + i + 1)
                            o = (c % 2) * T + i * P
                            ins = pe.transpose(b[:, o:o + P], XN[:, i, c * P:(c + 1) * P], IDENT[:, :])
                    ins.then_inc(filled, 1)

            norm_transposes(0)
            wait_emptied(pe, "norm0_3")

            def channel_major(dst, w, width, col, n=P):
                for c in range(KC):
                    ins = pe.matmul(dst, w[:, c * width + col:c * width + col + n], HT[:, c, :], start=(c == 0), stop=(c == KC - 1))
                return ins

            def token_major(dst, w, width, col, n, i, src=HT):
                for c in range(KC):
                    ins = pe.matmul(dst, src[:, c, i * P:(i + 1) * P], w[:, c * width + col:c * width + col + n],
                                    start=(c == 0), stop=(c == KC - 1))
                return ins

            for g in range(5):
                b = pe_open(pe, f"qkv{g}")
                for j in (2 * g, 2 * g + 1):
                    if j < 9:
                        if j % 4 == 0:
                            w = weights(f"in{j // 4}")
                        ins = channel_major(b[:, (j % 2) * T:(j % 2) * T + T], w, 512, (j % 4) * P)
                        if j == 8 or j % 2 == 1:
                            ins.then_inc(filled, 1)
            for name, u, width, col, n in (("z", 2, 512, P, GW), ("bq", 3, 396, 0, 396), ("kcvc", 4, 512, 0, 0),
                                           ("kv", 4, 512, 256, 256), ("kw", 5, 274, 0, 274), ("u", 6, 256, 0, 256)):
                w = weights(f"in{u}")
                if name == "kcvc":
                    b = pe_open(pe, "kcvc")
                    for kv in range(2):
                        ins = channel_major(b[:, kv * T:(kv + 1) * T], w, width, kv * P)
                    ins.then_inc(filled, 1)
                    continue
                for i in range(NT):
                    b = pe_open(pe, f"{name}{i}")
                    token_major(b[:, 0:n], w, width, col, n, i).then_inc(filled, 1)

            b = pe_open(pe, "hid")
            wait_emptied(pe, "kcvc")
            pe.wait_ge(sems["pos_ready"], 1)
            for kv in range(2):
                w = weights("w1" + "kv"[kv])
                for hc in range(2):
                    g = kv * 2 + hc
                    for m in range(16):
                        ins = pe.matmul(b[:, g * 45:(g + 1) * 45], w[:, m * HID + hc * P:m * HID + (hc + 1) * P],
                                        XK[:, kv, :, 2 * m:2 * m + CS * (NCB - 1) + 1:CS], start=(m == 0), stop=(m == 15))
            ins.then_inc(filled, 1)

            pe.wait_ge(sems["const_ready"], 3)
            wait_emptied(pe, "u1")
            for j in range(2):
                b = pe_open(pe, f"pm{j}")
                for g in range(2):
                    w = 2 * j + g
                    for i in range(NT):
                        ins = pe.matmul(b[g * HD:(g + 1) * HD, 0:T], UTOK[:, i, w * HD:(w + 1) * HD], BAND[:, w, i, :],
                                        start=(i == 0), stop=(i == NT - 1))
                ins.then_inc(filled, 1)
            pe.wait_ge(sems["misc_loaded"], 16 * 8)
            for j in range(2):
                wait_emptied(pe, f"pm{j}")
                b = pe_open(pe, f"py{j}")
                for g in range(2):
                    ins = pe.matmul(b[g * HD:(g + 1) * HD, 0:T], POOLW[g * HD:(g + 1) * HD, j, :], MT[g * HD:(g + 1) * HD, j, :],
                                    start=True, stop=True)
                ins.then_inc(filled, 1)
            pe.wait_ge(sems["hid_ready"], 1)
            b = pe_open(pe, "cmp")
            for hc in range(2):
                pe.matmul(b[0:30, 0:HD], HX[:, hc, :], W2[:, hc, :], start=(hc == 0), stop=(hc == 1))
            for h in range(2):
                for hc in range(2):
                    ins = pe.matmul(b[0:NCB, HD * (h + 1):HD * (h + 2)], HX[:, 2 + hc, h * NCB:(h + 1) * NCB], W2[:, 2 + hc, :],
                                    start=(hc == 0), stop=(hc == 1))
            ins.then_inc(filled, 1)
            pe.wait_ge(sems["silu_ready"], 1)
            for i in range(NT):
                for b3 in range(3):
                    b = pe_open(pe, f"tr{i}{b3}")
                    for j in range(4 * b3, min(4 * b3 + 4, 9)):
                        ins = pe.transpose(b[:, (j % 4) * P:(j % 4 + 1) * P], CV[:, j, i * P:(i + 1) * P], IDENT[:, :])
                    ins.then_inc(filled, 1)
            pe.wait_ge(sems["nqk_ready"], 1)
            for b3 in range(3):
                b = pe_open(pe, f"nt{b3}")
                for j in range(2 * b3, min(2 * b3 + 2, 5)):
                    for i in range(NT):
                        o = (j % 2) * T + i * P
                        ins = pe.transpose(b[:, o:o + P], NQK[:, i, 2 * j:2 * j + 2, :].rearrange("p h d -> p (h d)"), IDENT[:, :])
                ins.then_inc(filled, 1)
            pe.wait_ge(sems["kc_ready"], 1)
            b = pe_open(pe, "kct")
            pe.transpose(b[0:HD, 0:30], KCN[0:30, :], IDENT[0:30, 0:30]).then_inc(filled, 1)

            wait_emptied(pe, "kct")
            q_at = lambda h: ((h % 3), (h // 3) * HD)
            for i in range(NT):
                nb = 2 + i
                b = pe_open(pe, f"cs{i}")
                half(fresh=True)
                for h in range(GH):
                    j, p0 = q_at(h)
                    half(p0=p0)
                    ins = half(pe.matmul(b[:, h * 16:h * 16 + NCB], NTT[p0:p0 + HD, j, i * P:(i + 1) * P],
                                         KCT[p0:p0 + HD, 0:NCB], start=True, stop=True), p0)
                ins.then_inc(filled, 1)
                for t, kc in (("s", 3), ("w", 4)):
                    w = (i + 1) * P
                    for b3 in range(nb):
                        b = pe_open(pe, f"s{t}{i}{b3}")
                        per = 512 // w
                        half(fresh=True)
                        for h in range(per * b3, min(per * b3 + per, GH)):
                            j, p0 = q_at(h)
                            half(p0=p0)
                            ins = half(pe.matmul(b[:, (h % per) * w:(h % per) * w + w], NTT[p0:p0 + HD, j, i * P:(i + 1) * P],
                                                 NTT[p0:p0 + HD, kc, 0:w], start=True, stop=True), p0)
                        ins.then_inc(filled, 1)
                pe.wait_ge(sems["probs_ready"], 3 * i + 1)
                for j in range(2):
                    b = pe_open(pe, f"pc{i}{j}")
                    for h in range(3 * j, 3 * j + 3):
                        ins = pe.transpose(b[0:NCB, (h % 3) * P:(h % 3 + 1) * P], PCM[:, h, 0:NCB], IDENT[:, :])
                    ins.then_inc(filled, 1)
                for k, t in enumerate("sw"):
                    pe.wait_ge(sems["probs_ready"], 3 * i + 2 + k)
                    for b3 in range(nb):
                        b = pe_open(pe, f"p{t}{i}{b3}")
                        if i == 0:
                            for h in range(4 * b3, min(4 * b3 + 4, GH)):
                                ins = pe.transpose(b[:, (h % 4) * P:(h % 4 + 1) * P], PR[t][:, h, 0:P], IDENT[:, :])
                        else:
                            for kt in range(2):
                                for h in (2 * b3, 2 * b3 + 1):
                                    o = kt * 256 + (h % 2) * P
                                    ins = pe.transpose(b[:, o:o + P], PR[t][:, h, kt * P:(kt + 1) * P], IDENT[:, :])
                        ins.then_inc(filled, 1)
                wait_emptied(pe, f"pw{i}{nb - 1}")
                b = pe_open(pe, f"no{i}")
                for h in range(GH):
                    g = h // 3
                    o = b[(h % 2) * HD:(h % 2 + 1) * HD, (h // 2) * P:(h // 2 + 1) * P]
                    pe.matmul(o, VC[0:NCB, g, :], PCT[0:NCB, h, :], start=True, stop=False)
                    for t, v in (("s", VS), ("w", VW)):
                        for kt in range(i + 1):
                            ins = pe.matmul(o, v[:, kt, g * HD:(g + 1) * HD], PT[t][:, kt, h * P:(h + 1) * P],
                                            start=False, stop=(t == "w" and kt == i))
                ins.then_inc(filled, 1)

            pe.wait_ge(sems["qk_ready"], 1)
            for b3 in range(3):
                b = pe_open(pe, f"qk{b3}")
                for j in (2 * b3, 2 * b3 + 1):
                    for i in range(NT):
                        o = (j % 2) * T + i * P
                        ins = pe.transpose(b[:, o:o + P], TOK[:, i, 2 * j:2 * j + 2, :].rearrange("p h d -> p (h d)"), IDENT[:, :])
                ins.then_inc(filled, 1)
            pe.wait_ge(sems["g_ready"], 1)
            b = pe_open(pe, "gc")
            for i in range(NT):
                pe.matmul(b[:, i * 6:(i + 1) * 6], UPI[:, :], GG[:, i, :], start=True, stop=True)
            pe.matmul(b[:, 12:18], ONES[:, :], GG[:, 0, :], start=True, stop=True).then_inc(filled, 1)
            for b3 in range(3):
                b = pe_open(pe, f"r{b3}")
                for q in range(4 * b3, 4 * b3 + 4):
                    ins = pe.matmul(b[:, (q % 4) * P:(q % 4 + 1) * P], GG[:, q // 6, q % 6:q % 6 + 1].to_broadcast([P, P]),
                                    UPI[:, :], start=True, stop=True)
                ins.then_inc(filled, 1)
            wait_emptied(pe, "qk2")
            for b6 in range(6):
                b = pe_open(pe, f"kk{b6}")
                half(fresh=True)
                for q in (2 * b6, 2 * b6 + 1):
                    i, h = q // 6, q % 6
                    p0 = (h % 2) * HD
                    half(p0=p0)
                    k = QKT[p0:p0 + HD, 3 + h // 2, i * P:(i + 1) * P]
                    ins = half(pe.matmul(b[:, (q % 2) * 256:(q % 2) * 256 + 256], k,
                                         QKT[p0:p0 + HD, h // 2:h // 2 + 4:3, i * P:(i + 1) * P], start=True, stop=True), p0)
                ins.then_inc(filled, 1)
            for lv in range(7):
                for b3 in range(3):
                    if lv == 0 and b3 == 0:
                        pe.wait_ge(sems["lt_ready"], 1)
                    b = pe_open(pe, f"P{lv}{b3}")
                    if lv > 0:
                        wait_emptied(pe, f"TT{lv - 1}{b3}")
                    for q in range(4 * b3, 4 * b3 + 4):
                        ins = pe.matmul(b[:, (q % 4) * P:(q % 4 + 1) * P], LT[:, q, :], TM[:, q, :] if lv else IDENT[:, :],
                                        start=True, stop=True)
                    ins.then_inc(filled, 1)
                for b3 in range(3):
                    pe.wait_ge(sems["pm_ready"], 3 * lv + b3 + 1)
                    for kind in (("T", "TT") if lv < 6 else ("TT",)):
                        b = pe_open(pe, f"{kind}{lv}{b3}")
                        for q in range(4 * b3, 4 * b3 + 4):
                            tt = TTM[:, q, :] if lv else IDENT[:, :]
                            l, r = (tt, PM[:, q, :]) if kind == "T" else (PM[:, q, :], tt)
                            ins = pe.matmul(b[:, (q % 4) * P:(q % 4 + 1) * P], l, r, start=True, stop=True)
                        ins.then_inc(filled, 1)
            wait_emptied(pe, "TT62")

            def solve(i, rhs):
                b = pe_open(pe, f"x{i}")
                for h in range(GH):
                    ins = pe.matmul(b[:, h * HD:(h + 1) * HD], TTM[:, 6 * i + h, :], rhs(h), start=True, stop=True)
                ins.then_inc(filled, 1)

            solve(0, lambda h: TOK[:, 0, 12 + h, :])
            wait_emptied(pe, "x0")
            pe.wait_ge(sems["kd_ready"], 1)
            b = pe_open(pe, "S")
            for h in range(GH):
                ins = pe.matmul(b[(h % 2) * HD:(h % 2 + 1) * HD, (h // 2) * HD:(h // 2 + 1) * HD], KD[:, h, :], VN[:, 0, h, :],
                                start=True, stop=True)
            ins.then_inc(filled, 1)
            wait_emptied(pe, "S")
            b = pe_open(pe, "ks1")
            half(fresh=True)
            for h in (0, 2, 4, 1, 3, 5):
                p0 = (h % 2) * HD
                half(p0=p0)
                ins = half(pe.matmul(b[:, h * HD:(h + 1) * HD], QKT[p0:p0 + HD, 3 + h // 2, P:T],
                                     SST[p0:p0 + HD, h // 2, :], start=True, stop=True), p0)
            ins.then_inc(filled, 1)
            pe.wait_ge(sems["rhs_ready"], 1)
            solve(1, lambda h: RHS[:, h, :])
            for i in range(NT):
                if i:
                    b = pe_open(pe, "qs1")
                    half(fresh=True)
                    for h in (0, 2, 4, 1, 3, 5):
                        p0 = (h % 2) * HD
                        half(p0=p0)
                        ins = half(pe.matmul(b[:, h * HD:(h + 1) * HD], QKT[p0:p0 + HD, h // 2, P:T],
                                             SST[p0:p0 + HD, h // 2, :], start=True, stop=True), p0)
                    ins.then_inc(filled, 1)
                wait_emptied(pe, f"x{i}")
                if i == 0:
                    b = pe_open(pe, "o0")
                else:
                    b = pe_open(pe, "o1")
                for h in range(GH):
                    ins = pe.matmul(b[:, h * HD:(h + 1) * HD], QKD[:, 6 * i + h, :], VN[:, i, h, :], start=True, stop=True)
                ins.then_inc(filled, 1)
            pe.wait_ge(sems["ya_ready"], 1)
            for j in range(3):
                b = pe_open(pe, f"ya{j}")
                for i in range(NT):
                    ins = pe.transpose(b[:, i * P:(i + 1) * P], OT2[:, i, 2 * j:2 * j + 2, :].rearrange("p h d -> p (h d)"), IDENT[:, :])
                ins.then_inc(filled, 1)
            wait_emptied(pe, "ya2")
            wait_emptied(pe, "no1")
            for n in range(2):
                w = weights(f"out{n}")
                for i in range(NT):
                    b = pe_open(pe, f"out{n}{i}")
                    token_major(b[:, 0:512], w, 512, 0, 512, i, src=YT).then_inc(filled, 1)
            norm_transposes(1)

            wait_emptied(pe, "norm1_3")
            for i in range(NT):
                for n in range(2):
                    pe.matmul(PS[:, 4 + 2 * i + n, :], IDENT[:, :], XR[:, i, n * 512:(n + 1) * 512], start=True, stop=False,
                              skip_group_check=True)

            def ffn_hidden(j, count):
                s = 2 * j
                pe.wait_ge(sems[f"loaded{s}"], 16 * (use(f"ffn0{s}")[1] + count))
                for f in range(4):
                    for c in range(KC):
                        ins = pe.matmul(PS[:, 2 * j + f // 2, (f % 2) * T:(f % 2 + 1) * T],
                                        slots[s][:, c * 512 + f * P:c * 512 + (f + 1) * P], HT[:, c, :],
                                        start=(c == 0), stop=(c == KC - 1), skip_group_check=True)
                    if f % 2 == 1:
                        ins.then_inc(sems["ffn_hid_filled"], 1)

            def ffn_out(j, v):
                s = 2 * j + 1
                pe.wait_ge(sems[f"loaded{s}"], 16 * (use(f"ffn0{s}")[1] + v))
                for f in range(4):
                    if f % 2 == 0:
                        pe.wait_ge(sems["ffn_act_ready"], 4 * v + 2 * j + f // 2 + 1)
                    for i in range(NT):
                        for n in range(2):
                            ins = pe.matmul(PS[:, 4 + 2 * i + n, :], AT[:, j, f * T + i * P:f * T + (i + 1) * P],
                                            slots[s][:, f * D + n * 512:f * D + (n + 1) * 512], start=False, stop=False,
                                            skip_group_check=True)
                ins.then_inc(sems["ffn_out_done"], 1)

            ffn_hidden(0, 0)
            ffn_hidden(1, 0)
            with pe.Fori(0, 3) as v:
                ffn_out(0, v)
                ffn_hidden(0, v + 1)
                ffn_out(1, v)
                ffn_hidden(1, v + 1)
            ffn_out(0, 3)
            ffn_out(1, 3)

            pe.wait_ge(sems["ada_used0"], 8)
            pe.wait_ge(sems["ada_used1"], 8)
            pe.wait_ge(sems["x_ready"], 1)
            b = pe_open(pe, "mod")
            for k, seg in enumerate((0, 1, 3, 4)):
                for c in range(KC):
                    ins = pe.matmul(b[:, 8 * k + c:8 * k + c + 1], ACC[:, seg * D + c * P:seg * D + (c + 1) * P], ONES[:, 0:1],
                                    start=True, stop=True)
            ins.then_inc(filled, 1)
            for k, seg in enumerate((2, 5)):
                for n in range(2):
                    b = pe_open(pe, f"gb{2 * k + n}")
                    pe.matmul(b[:, 0:512], ONES[:, :], ACC[:, seg * D + n * 512:seg * D + (n + 1) * 512], start=True, stop=True)\
                        .then_inc(filled, 1)
            norm_transposes(2)
            wait_emptied(pe, "norm2_3")
            for b8 in range(8):
                b = pe_open(pe, f"sq{b8}")
                w = weights(f"sb{b8 // 2}")
                for j in range(2):
                    ins = channel_major(b[:, j * T:(j + 1) * T], w, 512, (b8 % 2) * 256 + j * P)
                ins.then_inc(filled, 1)
            for n in range(2):
                w = weights(f"sb{4 + n}")
                for i in range(NT):
                    b = pe_open(pe, f"sv{n}{i}")
                    token_major(b[:, 0:512], w, 512, 0, 512, i).then_inc(filled, 1)
            wait_emptied(pe, "sv11")

            def scores(b, h, stop):
                p0 = (h % 2) * HD
                for kt in range(NT):
                    yield pe.matmul(b[:, kt * T:kt * P + T], SQK[p0:p0 + HD, 8 + h // 2, kt * P:(kt + 1) * P],
                                    SQK[p0:p0 + HD, h // 2, kt * P:T], start=True, stop=stop)

            for s in range(SBH + 4):
                if s < SBH:
                    b = pe_open(pe, f"Z{s}")
                    for ins in scores(b, s, True):
                        pass
                    ins.then_inc(filled, 1)
                if 2 <= s < SBH + 2:
                    h = s - 2
                    b = pe_open(pe, f"C{h}")
                    pe.wait_ge(sems["sp_ready"], h + 1)
                    sp_ = SPB[:, h % 3, :]
                    for kt, ins in enumerate(scores(b, h, False)):
                        ins = pe.matmul(b[:, kt * T:kt * P + T], NLOW[:, :], sp_[:, kt * T:kt * P + T], start=False, stop=(kt == 1))
                        if kt == 0:
                            pe.matmul(b[:, P:T], NONES[:, :], sp_[:, T:T + P], start=False, stop=True)
                    ins.then_inc(filled, 1)
                if s >= 4:
                    h = s - 4
                    if h % 2 == 0:
                        bo = pe_open(pe, f"O{h // 2}")
                    pe.wait_ge(sems["sa_ready"], h + 1)
                    o = bo[(h % 2) * HD:(h % 2 + 1) * HD, 0:T]
                    pe.matmul(o, SV[:, 0, h * HD:(h + 1) * HD], SA[:, h % 3, 0:T], start=True, stop=False)
                    ins = pe.matmul(o[:, P:T], SV[:, 1, h * HD:(h + 1) * HD], SA[:, h % 3, T:T + P], start=False, stop=True)
                    if h % 2 == 1:
                        ins.then_inc(filled, 1)
            wait_emptied(pe, "O7")
            for n in range(2):
                w = weights(f"so{n}")
                for i in range(NT):
                    b = pe_open(pe, f"so{n}{i}")
                    token_major(b[:, 0:512], w, 512, 0, 512, i, src=YT).then_inc(filled, 1)
            norm_transposes(3)
            wait_emptied(pe, "norm3_3")
            b = pe_open(pe, "lg")
            for i in range(NT):
                for c in range(KC):
                    ins = pe.matmul(b[:, i * 36:(i + 1) * 36], HT[:, c, i * P:(i + 1) * P], RW[:, c, :],
                                    start=(c == 0), stop=(c == KC - 1))
            ins.then_inc(filled, 1)
            for i in range(NT):
                for b2 in range(2):
                    b = pe_open(pe, f"h2{i}{b2}")
                    for c in range(4 * b2, 4 * b2 + 4):
                        ins = pe.transpose(b[:, (c % 4) * P:(c % 4 + 1) * P], HT[:, c, i * P:(i + 1) * P], IDENT[:, :])
                    ins.then_inc(filled, 1)
            pe.wait_ge(sems["onehot_ready"], 1)
            b = pe_open(pe, "rank")
            A0, A1 = E32[:, 1, 0:NE], E32[:, 1, NE:2 * NE]
            pe.matmul(b[:, 0:NE], UPS[:, :], A0, start=True, stop=True)
            pe.matmul(b[:, NE:2 * NE], UPS[:, :], A1, start=True, stop=False)
            pe.matmul(b[:, NE:2 * NE], ONES[:, :], A0, start=False, stop=True)
            pe.matmul(b[:, 2 * NE:3 * NE], ONES[:, :], A0, start=True, stop=False)
            pe.matmul(b[:, 2 * NE:3 * NE], ONES[:, :], A1, start=False, stop=True).then_inc(filled, 1)

            def gather():
                for c in range(KC):
                    for i in range(NT):
                        ins = pe.matmul(PS[:, 6 + c // 4, (c % 4) * 2 * CAP:(c % 4 + 1) * 2 * CAP], H2[:, i, c * P:(c + 1) * P],
                                        SEL[:, i, :], start=(i == 0), stop=(i == NT - 1))
                ins.then_inc(sems["gathered"], 1)

            def into_hidden(bank_, parts):
                for c in range(KC):
                    for k, (s, f0, n) in enumerate(parts):
                        ins = pe.matmul(PS[k * CAP:(k + 1) * CAP, bank_, 0:n], HS[:, c, k * CAP:(k + 1) * CAP],
                                        slots[s][:, c * EFF + f0:c * EFF + f0 + n], start=(c == 0), stop=(c == KC - 1))
                return ins

            def turn_hidden(n):
                for f in range(n):
                    ins = pe.transpose(PS[:, 4, f * P:(f + 1) * P], AM[:, f * P:(f + 1) * P], IDENT[:, :])
                ins.then_inc(sems["hid_turned"], 1)

            def turn_weights():
                for i in range(NT):
                    ins = pe.transpose(PS[:, 5, i * P:(i + 1) * P], SELW[:, i, :], IDENT[:, :])
                ins.then_inc(sems["weights_turned"], 1)

            def scatter(i):
                for n in range(2):
                    ins = pe.matmul(PS[:, 2 * i + n, :], GT[:, i * P:(i + 1) * P], YB[:, n * 512:(n + 1) * 512],
                                    start=False, stop=False, skip_group_check=True)
                return ins

            base = [max(use(n)[1] for n, t, _ in uses if t == s) for s in range(NSLOT)]
            wait_emptied(pe, "h211")
            wait_emptied(pe, "rank")
            pe.wait_ge(sems["yb0_ready"], 1)
            pe.wait_ge(sems["yb1_ready"], 1)
            for q in range(4):
                pe.matmul(PS[:, q, :], ONES[:, :], YB[:, 0:512], start=True, stop=False, skip_group_check=True)
            pe.wait_ge(sems["sel_ready"], 1)
            gather()
            with pe.Fori(0, NE // 2) as m:
                def loaded(s):
                    pe.wait_ge(sems[f"loaded{s}"], 16 * (m + base[s] + 1))

                pe.wait_ge(sems["hs0_ready"], m + 1)
                pe.wait_ge(sems["hs1_ready"], m + 1)
                loaded(0)
                loaded(3)
                into_hidden(4, ((0, 0, EFF), (3, 0, EFF))).then_inc(sems["gate_filled"], 1)
                pe.wait_ge(sems["gt_ready"], m + 1)
                loaded(1)
                loaded(4)
                into_hidden(5, ((1, 0, EFF), (4, 0, EFF))).then_inc(sems["up_filled"], 1)
                pe.wait_ge(sems["yb0_ready"], m + 1)
                pe.wait_ge(sems["yb1_ready"], m + 1)
                scatter(0)
                pe.wait_ge(sems["sel_ready"], m + 2)
                gather()
                pe.wait_ge(sems["am_ready"], m + 1)
                turn_hidden(4)
                scatter(1)
                pe.wait_ge(sems["selw_ready"], m + 1)
                turn_weights()
                pe.wait_ge(sems["hs0_ready"], m + 2)
                pe.wait_ge(sems["hs1_ready"], m + 2)
                loaded(2)
                loaded(5)
                pe.wait_ge(sems["ac_ready"], m + 1)
                for n in range(2):
                    for f in range(4):
                        for k in range(2):
                            ins = pe.matmul(PS[k * CAP:(k + 1) * CAP, 6 + n, :], AC[:, f, k * CAP:(k + 1) * CAP],
                                            slots[2 + 3 * k][:, f * D + n * 512:f * D + (n + 1) * 512],
                                            start=(f == 0), stop=(f == 3))
                    ins.then_inc(sems["down_filled"], 1)
            pe.wait_ge(sems["gt_ready"], NE // 2 + 1)
            pe.wait_ge(sems["yb0_ready"], NE // 2 + 1)
            pe.wait_ge(sems["yb1_ready"], NE // 2 + 1)
            scatter(0)
            scatter(1).then_inc(sems["x_done"], 1)
            pe.wait_ge(sems["over_ready"], 1)
            n_over = pe.value_load(OVI[0:1, OVN:OVN + 1], min_val=0, max_val=OVN)
            with pe.Fori(0, OVN) as x:
                with pe.If(n_over > x):
                    pe.wait_ge(sems["sel_ready"], x + NE // 2 + 2)
                    gather()
                    pe.wait_ge(sems["hs0_ready"], x + NE // 2 + 2)
                    pe.wait_ge(sems["hs1_ready"], x + NE // 2 + 2)
                    for s, name in ((0, "gate_filled"), (1, "up_filled")):
                        pe.wait_ge(sems[f"loaded{s}"], 16 * (x + base[s] + NE // 2 + 1))
                        into_hidden(4 + s, ((s, 0, EFF // 2), (s, EFF // 2, EFF // 2))).then_inc(sems[name], 1)
                    pe.wait_ge(sems["am_ready"], x + NE // 2 + 1)
                    turn_hidden(2)
                    pe.wait_ge(sems["selw_ready"], x + NE // 2 + 2)
                    turn_weights()
                    pe.wait_ge(sems["loaded2"], 16 * (x + base[2] + NE // 2 + 1))
                    pe.wait_ge(sems["ac_ready"], x + NE // 2 + 1)
                    for f in range(4):
                        for n in range(2):
                            ins = pe.matmul(PS[n * CAP:(n + 1) * CAP, 6, :], AC[:, f % 2, (f // 2) * CAP:(f // 2 + 1) * CAP],
                                            slots[2][:, f * D + n * 512:f * D + (n + 1) * 512], start=(f == 0), stop=(f == 3))
                    ins.then_inc(sems["down_filled"], 1)
                    pe.wait_ge(sems["gt_ready"], x + NE // 2 + 2)
                    pe.wait_ge(sems["yb0_ready"], x + NE // 2 + 2)
                    for i in range(NT):
                        for n in range(2):
                            ins = pe.matmul(PS[:, 2 * i + n, :], GT[n * CAP:(n + 1) * CAP, i * P:(i + 1) * P],
                                            YB[n * CAP:(n + 1) * CAP, 0:512], start=False, stop=False, skip_group_check=True)
                    ins.then_inc(sems["x_done"], 1)

        @block.vector
        def _(dve):
            step = Steps(dve, "dve_step")
            tt, ts, stt = dve.tensor_tensor, dve.tensor_scalar, dve.scalar_tensor_tensor
            freed = sems["emptied_by_dve"]

            b = wait_filled(dve, "cols")
            dve.tensor_copy(COL[:, 0:N_ROWS], b[:, 0:N_ROWS])
            dve.tensor_copy(COL[:, P:P + N_ROWS2], b[:, P:P + N_ROWS2]).then_inc(freed, 1)
            wait_emptied(dve, "cols")
            dve.wait_ge(sems["const_ready"], 2)
            for kv in range(2):
                ins = dve.tensor_copy(XK[:, kv, 2, 0:CL:2], COL[:, P + R2_POS + 16 * kv:P + R2_POS + 16 * kv + 16])
            ins.then_inc(sems["pos_ready"], 1)

            def norm_apply(n, gain, shift=None):
                dve.wait_ge(sems["rstd_ready"], n + 1)
                for i in range(NT):
                    ts(XN[:, i, :], XR[:, i, :], RSTD[:, i:i + 1], None, ALU.mult).then_inc(sems["xn_ready"], 1)
                for b4 in range(4):
                    b = wait_filled(dve, f"norm{n}_{b4}")
                    for c in (2 * b4, 2 * b4 + 1):
                        src = b[:, (c % 2) * T:(c % 2 + 1) * T]
                        if shift is None:
                            ins = ts(HT[:, c, :], src, gain[:, c:c + 1], None, ALU.mult)
                        else:
                            ins = ts(HT[:, c, :], src, gain[:, c:c + 1], shift[:, c:c + 1], ALU.mult, ALU.add)
                    ins.then_inc(freed, 1)

            dve.wait_ge(sems["counts_ready"], 1)
            tp1 = SG[:, :, :].rearrange("p a b -> p (a b)")[:, 0:T]
            for w in range(4):
                ins = ts(RCP[:, w, :], tp1, float(POOLS[w]), None, ALU.min)
            step(ins)
            dve.reciprocal(RCP, RCP).then_inc(sems["recip_ready"], 1)
            norm_apply(0, COL[:, R_MIX:R_MIX + 8])
            wait_emptied(dve, "qkv4")
            for k in range(4):
                for j in range(9):
                    w = COL[:, R_CONV + k * 9 + j:R_CONV + k * 9 + j + 1]
                    if k == 0:
                        ins = ts(CV[:, j, :], QKVT[:, j, 0:T], w, None, ALU.mult)
                    else:
                        ins = stt(CV[:, j, :], QKVT[:, j, k:k + T], w, CV[:, j, :], ALU.mult, ALU.add)
                if k < 3:
                    step(ins)
            ins.then_inc(sems["conv_ready"], 1)
            dve.wait_ge(sems["conv_exp"], 1)
            step(ts(EX[:, :, :], EX[:, :, :], 1.0, None, ALU.add))
            step(dve.reciprocal(EX[:, :, :], EX[:, :, :]))
            tt(CV[:, :, :], CV[:, :, :], EX[:, :, :], ALU.mult).then_inc(sems["silu_ready"], 1)
            dve.wait_ge(sems["misc_loaded"], 16 * 8)
            wait_emptied(dve, "bq1")
            tt(SPV, BG[:, :, 6:12], bc(PBC[:, 6:12], 1, NT), ALU.add).then_inc(sems["dt_added"], 1)
            dve.wait_ge(sems["sig_exp"], 1)
            step(ts(SG[:, :, :], SG[:, :, :], 1.0, None, ALU.add))
            step(dve.reciprocal(SG[:, :, :], SG[:, :, :]))
            tt(SIG[:, :, 0:GW], SIG[:, :, 0:GW], SG[:, :, 0:GW], ALU.mult)
            dve.wait_ge(sems["dt_parts"], 1)
            step(stt(SPV, SPV, 0.0, SPE, ALU.max, ALU.add))
            stt(GG, SPV, -1.0, bc(EA, 1, NT), ALU.mult, ALU.mult).then_inc(sems["g_ready"], 1)
            wait_emptied(dve, "hid")
            for g in range(4):
                ins = ts(HX[:, g, :], HIDT[:, g, 0:30], HIDT[:, g, 30:31], None, ALU.add)
            ins.then_inc(sems["hid_bias"], 1)
            dve.wait_ge(sems["hid_exp"], 1)
            step(ts(HIDT[:, :, 0:30], HIDT[:, :, 0:30], 1.0, None, ALU.add))
            step(dve.reciprocal(HIDT[:, :, 0:30], HIDT[:, :, 0:30]))
            tt(HX[:, :, :], HX[:, :, :], HIDT[:, :, 0:30], ALU.mult).then_inc(sems["hid_ready"], 1)
            for j in range(2):
                b = wait_filled(dve, f"py{j}")
                ts(YT[:, 6 + j, :], b[:, 0:T], COL[:, R_PS + j:R_PS + j + 1], None, ALU.mult).then_inc(freed, 1)
            wait_emptied(dve, "kw1")
            SQ = EX[:, :, :].rearrange("p a b -> p (a b)")
            sq20 = SQ[:, 0:1280].rearrange("p (h d) -> p h d", d=HD)
            nq = NQK[:, :, :, :].rearrange("p i h d -> p (i h) d")
            step(tt(sq20, nq, nq, ALU.mult))
            dve.tensor_reduce(M2, sq20, X, ALU.add).then_inc(sems["nqk_sumsq"], 1)
            b = wait_filled(dve, "cmp")
            dve.tensor_copy(VC[0:NCB, :, :], b[0:NCB, HD:3 * HD].rearrange("p (h d) -> p h d", d=HD))
            dve.tensor_copy(KCN[0:30, :], b[0:30, 0:HD]).then_inc(freed, 1)
            wait_emptied(dve, "cmp")
            step(tt(SQ[0:30, 1280:1280 + HD], KCN[0:30, :], KCN[0:30, :], ALU.mult))
            dve.tensor_reduce(KN2[0:30, 0:1], SQ[0:30, 1280:1280 + HD], X, ALU.add).then_inc(sems["kc_sumsq"], 1)
            dve.wait_ge(sems["nqk_rnorm"], 1)
            tt(nq, nq, bc(MR, 2, HD), ALU.mult).then_inc(sems["nqk_ready"], 1)
            dve.wait_ge(sems["kc_rnorm"], 1)
            ts(KCN[0:30, :], KCN[0:30, :], KN2[0:30, 1:2], None, ALU.mult).then_inc(sems["kc_ready"], 1)
            wait_emptied(dve, "tr12")
            sq24 = SQ[:, 0:1536].rearrange("p (h d) -> p h d", d=HD)
            for i in range(NT):
                ins = tt(sq24[:, 12 * i:12 * i + 12, :], TOK[:, i, 0:12, :], TOK[:, i, 0:12, :], ALU.mult)
            step(ins)
            dve.tensor_reduce(N2, sq24, X, ALU.add).then_inc(sems["qk_sumsq"], 1)
            dve.wait_ge(sems["qk_rnorm"], 1)
            rn = RN.rearrange("p (i h) -> p i h", i=NT)
            step(ts(rn[:, :, 0:6], rn[:, :, 0:6], SCALE, None, ALU.mult))
            for i in range(NT):
                ins = tt(TOK[:, i, 0:12, :], TOK[:, i, 0:12, :], bc(rn[:, i, :], 2, HD), ALU.mult)
            ins.then_inc(sems["qk_ready"], 1)
            for b3 in range(3):
                b = wait_filled(dve, f"nt{b3}")
                for j in range(2 * b3, min(2 * b3 + 2, 5)):
                    r = R_QN if j < 3 else R_KN + j - 2
                    ins = ts(NTT[:, j, :], b[:, (j % 2) * T:(j % 2 + 1) * T], COL[:, r:r + 1], None, ALU.mult)
                ins.then_inc(freed, 1)
            b = wait_filled(dve, "kct")
            ts(KCT[0:HD, 0:NCB], b[0:HD, 0:NCB], COL[0:HD, R_KN:R_KN + 1], None, ALU.mult)
            ts(KCT[HD:P, 0:NCB], b[0:HD, NCB:2 * NCB], COL[0:HD, R_KN:R_KN + 1], None, ALU.mult).then_inc(freed, 1)
            dve.wait_ge(sems["const_ready"], 4)
            gates = SG[:, :, GW + 6:GW + 24].rearrange("p i (h k) -> p i h k", k=3)
            for i in range(NT):
                nb, w = 2 + i, (i + 1) * P
                b = wait_filled(dve, f"cs{i}")
                cs = b[:, 0:96].rearrange("p (h n) -> p h n", n=16)[:, :, 0:NCB]
                pc = PCM[:, :, 0:NCB]
                if i:
                    dve.wait_ge(sems["filled"], order["no0"] + 1)
                tt(pc, cs, bc(CNEG[:, i, 0:NCB], 1, GH), ALU.add).then_inc(freed, 1)
                wait_emptied(dve, f"cs{i}")
                step(dve.tensor_reduce(CSUM[:, 0, :], pc, X, ALU.max))
                tt(pc, pc, bc(CSUM[:, 0, :], 2, NCB), ALU.subtract).then_inc(sems["cmax"], 1)
                for t in "sw":
                    pr = PR[t][:, :, 0:w]
                    per = 512 // w
                    for b3 in range(nb):
                        b = wait_filled(dve, f"s{t}{i}{b3}")
                        n = min(per, GH - per * b3)
                        mask = QNEG[:, 1 - i:2, :].rearrange("p a b -> p (a b)")
                        ins = tt(pr[:, per * b3:per * b3 + n, :], b[:, 0:n * w].rearrange("p (h k) -> p h k", k=w), bc(mask, 1, n), ALU.add)
                        ins.then_inc(freed, 1)
                    wait_emptied(dve, f"s{t}{i}{nb - 1}")
                    mx = MX if t == "w" else NMX
                    step(dve.tensor_reduce(mx, pr, X, ALU.max))
                    ts(mx, mx, -SCALE, None, ALU.mult).then_inc(sems["smax"], 1)
                dve.wait_ge(sems["cexp"], i + 1)
                step(dve.tensor_reduce(CSUM[:, 1, :], pc, X, ALU.add))
                step(dve.reciprocal(CSUM[:, 1, :], CSUM[:, 1, :]))
                step(tt(CSUM[:, 2, :], CSUM[:, 1, :], gates[:, i, :, 0], ALU.mult))
                step(tt(pc, pc, bc(CSUM[:, 2, :], 2, NCB), ALU.mult))
                tt(pc, pc, bc(CONE[:, i, 0:NCB], 1, GH), ALU.mult).then_inc(sems["probs_ready"], 1)
                for k, t in enumerate("sw"):
                    dve.wait_ge(sems["sexp"], 2 * i + k + 1)
                    sm_ = (SUM, CF)[k]
                    step(dve.reciprocal(sm_, sm_))
                    step(tt(sm_, sm_, gates[:, i, :, 1 + k], ALU.mult))
                    tt(PR[t][:, :, 0:w], PR[t][:, :, 0:w], bc(sm_, 2, w), ALU.mult).then_inc(sems["probs_ready"], 1)

            b = wait_filled(dve, "gc")
            dve.tensor_copy(GCS, b[:, 0:12])
            dve.tensor_copy(GLS, b[:, 12:18]).then_inc(freed, 1)
            wait_emptied(dve, "gc")
            step(tt(KDE, GLS, GCS[:, 0:6], ALU.subtract))
            for b3 in range(3):
                b = wait_filled(dve, f"r{b3}")
                for q in range(4 * b3, 4 * b3 + 4):
                    ins = ts(DEC[:, q, :], b[:, (q % 4) * P:(q % 4 + 1) * P], GCS[:, q:q + 1], 0.0, ALU.subtract, ALU.min)
                ins.then_inc(freed, 1)
            dve.wait_ge(sems["decay_exp"], 1)
            step(tt(DEC[:, :, :], DEC[:, :, :], bc(UPI[:, :], 1, 12), ALU.mult))
            for b6 in range(6):
                b = wait_filled(dve, f"kk{b6}")
                bb = b[:, 0:512].rearrange("p (q k t) -> p q k t", q=2, k=2)
                ins = tt(QKD[:, 2 * b6:2 * b6 + 2, :], bb[:, :, 0, :], DEC[:, 2 * b6:2 * b6 + 2, :], ALU.mult)
                for q in (2 * b6, 2 * b6 + 1):
                    i, h = q // 6, q % 6
                    ins = stt(LT[:, q, :], bb[:, q % 2, 1, :], SG[:, i, GW + h:GW + h + 1], DEC[:, q, :], ALU.mult, ALU.mult)
                ins.then_inc(freed, 1)
            wait_emptied(dve, "kk5")
            tt(LT[:, :, :], LT[:, :, :], bc(UPS[:, :], 1, 12), ALU.mult).then_inc(sems["lt_ready"], 1)
            dve.wait_ge(sems["const_ready"], 5)
            for lv in range(7):
                for b3 in range(3):
                    b = wait_filled(dve, f"P{lv}{b3}")
                    pm = PM[:, 4 * b3:4 * b3 + 4, :]
                    tt(pm, b[:, 0:512].rearrange("p (a b) -> p a b", b=P), bc(LVM[:, lv, :], 1, 4), ALU.mult).then_inc(freed, 1)
                    wait_emptied(dve, f"P{lv}{b3}")
                    tt(pm, pm, bc(IDENT[:, :], 1, 4), ALU.add).then_inc(sems["pm_ready"], 1)
            dve.wait_ge(sems["egc_ready"], 1)
            wait_emptied(dve, "T52")
            dve.wait_ge(sems["filled"], order["TT62"] + 1)
            tt(KD[:, :, :], TOK[:, 0, 6:12, :], bc(KDE, 2, HD), ALU.mult).then_inc(sems["kd_ready"], 1)
            beta = [SG[:, i, GW:GW + 6] for i in range(NT)]
            v3 = lambda b: b[:, 0:GW].rearrange("p (h d) -> p h d", d=HD)
            b = wait_filled(dve, "x0")
            tt(VN[:, 0], v3(b), bc(beta[0], 2, HD), ALU.mult).then_inc(freed, 1)
            b = wait_filled(dve, "S")
            dve.tensor_copy(SST[:, :, :], b[:, 0:3 * HD].rearrange("p (j d) -> p j d", d=HD)).then_inc(freed, 1)
            b = wait_filled(dve, "ks1")
            tt(RHS[:, :, :], v3(b), bc(EGC, 2, HD), ALU.mult).then_inc(freed, 1)
            wait_emptied(dve, "ks1")
            tt(RHS[:, :, :], TOK[:, 1, 12:18, :], RHS[:, :, :], ALU.subtract).then_inc(sems["rhs_ready"], 1)
            b = wait_filled(dve, "x1")
            tt(VN[:, 1], v3(b), bc(beta[1], 2, HD), ALU.mult).then_inc(freed, 1)
            b = wait_filled(dve, "o0")
            dve.tensor_copy(OT2[:, 0], v3(b)).then_inc(freed, 1)
            b = wait_filled(dve, "qs1")
            tt(TMP[:, 0], v3(b), bc(EGC, 2, HD), ALU.mult).then_inc(freed, 1)
            wait_emptied(dve, "qs1")
            b = wait_filled(dve, "o1")
            tt(OT2[:, 1], v3(b), TMP[:, 0], ALU.add).then_inc(freed, 1)
            wait_emptied(dve, "o1")
            oo = OT2[:, :, :, :].rearrange("p i h d -> p (i h) d")
            tm = TMP[:, :, :, :].rearrange("p i h d -> p (i h) d")
            step(tt(tm, oo, oo, ALU.mult))
            dve.tensor_reduce(O2, tm, X, ALU.add).then_inc(sems["o_sumsq"], 1)
            dve.wait_ge(sems["o_rnorm"], 1)
            step(tt(oo, oo, bc(OR, 2, HD), ALU.mult))
            for i in range(NT):
                ins = tt(OT2[:, i], OT2[:, i], SIG[:, i, 0:GW].rearrange("p (h d) -> p h d", d=HD), ALU.mult)
            ins.then_inc(sems["ya_ready"], 1)
            for j in range(3):
                b = wait_filled(dve, f"ya{j}")
                ins = ts(YT[:, j, :], b[:, 0:T], COL[:, R_GN:R_GN + 1], None, ALU.mult)
                ins.then_inc(freed, 1)
            for n in range(2):
                for i in range(NT):
                    b = wait_filled(dve, f"out{n}{i}")
                    ins = tt(XR[:, i, n * 512:(n + 1) * 512], b[:, 0:512], XR[:, i, n * 512:(n + 1) * 512], ALU.add)
                    ins.then_inc(freed, 1)
            norm_apply(1, COL[:, R_FFN:R_FFN + 8])
            dve.wait_ge(sems["cond_exp"], 1)
            step(ts(COND[:, 8:16], COND[:, 8:16], 1.0, None, ALU.add))
            step(dve.reciprocal(COND[:, 8:16], COND[:, 8:16]))
            step(tt(COND[:, 0:8], COND[:, 8:16], COL[:, P + R2_C:P + R2_C + 8], ALU.mult))
            with dve.Fori(0, 8) as v:
                for c in range(KC):
                    for k in range(2):
                        if c == 0:
                            dve.wait_ge(sems[f"ada_loaded{k}"], 16 * v + 16)
                        else:
                            dve.wait_ge(sems["ada_step"], 14 * v + 2 * c + k - 1)
                        acc = ACC[:, bass.ds((2 * v + k) * ADW, ADW)]
                        if c == 0:
                            ins = ts(acc, ADA[:, k, c, :], COND[:, c:c + 1], None, ALU.mult)
                        else:
                            ins = stt(acc, ADA[:, k, c, :], COND[:, c:c + 1], acc, ALU.mult, ALU.add)
                        ins.then_inc(sems["ada_step" if c < KC - 1 else f"ada_used{k}"], 1)
            dve.wait_ge(sems["ffn_out_done"], 8)
            for i in range(NT):
                for n in range(2):
                    ins = dve.tensor_copy(XR[:, i, n * 512:(n + 1) * 512], PS[:, 4 + 2 * i + n, :])
            ins.then_inc(sems["x_ready"], 1)
            dve.wait_ge(sems["x_ready"], 1)
            b = wait_filled(dve, "mod")
            for k, seg in enumerate((0, 1, 3, 4)):
                ins = tt(MODC[:, 8 * k:8 * k + 8], b[:, 8 * k:8 * k + 8], COL[:, R_ADA + 8 * seg:R_ADA + 8 * seg + 8], ALU.add)
            ins.then_inc(freed, 1)
            wait_emptied(dve, "mod")
            for k in range(2):
                ins = stt(MODC[:, 32 + 8 * k:40 + 8 * k], MODC[:, 16 * k + 8:16 * k + 16], 1.0,
                          COL[:, R_NG + 8 * k:R_NG + 8 * k + 8], ALU.add, ALU.mult)
            step(ins)
            dve.wait_ge(sems["rows_bc"], 48)
            for k in range(2):
                for n in range(2):
                    b = wait_filled(dve, f"gb{2 * k + n}")
                    g12 = G12[:, k, n * 512:(n + 1) * 512]
                    tt(g12, b[:, 0:512], g12, ALU.add).then_inc(freed, 1)
            norm_apply(2, MODC[:, 32:40], MODC[:, 0:8])
            for s in range(SBH + 4):
                if s < SBH:
                    b = wait_filled(dve, f"Z{s}")
                    dve.wait_ge(sems["sp_ln"], s + 1)
                    if s >= 3:
                        dve.wait_ge(sems["filled"], order[f"C{s - 3}"] + 1)
                    spb = SPB[:, s % 3, :]
                    stt(spb, b[:, 0:3 * P], 0.0, SAB[:, s % 3, :], ALU.max, ALU.add).then_inc(freed, 1)
                    wait_emptied(dve, f"Z{s}")
                    dg = spb.rearrange("p (k q) -> p k q", q=P)[:, 0:3:2, :]
                    tt(dg, dg, bc(UPS[:, :], 1, 2), ALU.mult).then_inc(sems["sp_ready"], 1)
                if 2 <= s < SBH + 2:
                    h = s - 2
                    b = wait_filled(dve, f"C{h}")
                    if h >= 3:
                        dve.wait_ge(sems["filled"], pv_seen(h - 3))
                    stt(SA[:, h % 3, :], b[:, 0:3 * P], 0.0, SBNEG[:, :, :].rearrange("p k q -> p (k q)"), ALU.min, ALU.add)\
                        .then_inc(freed, 1)

            for n in range(2):
                for i in range(NT):
                    b = wait_filled(dve, f"so{n}{i}")
                    t = YTMP[:, i, n * 512:(n + 1) * 512]
                    xr = XR[:, i, n * 512:(n + 1) * 512]
                    step(tt(t, b[:, 0:512], G12[:, 0, n * 512:(n + 1) * 512], ALU.mult))
                    tt(xr, xr, t, ALU.add).then_inc(freed, 1)
            norm_apply(3, MODC[:, 40:48], MODC[:, 16:24])

            dve.memset(KEY[:, :, NE:NE + 2], -1.0)
            dve.memset(WT[:, :, NE:NE + 2], 0.0)
            dve.memset(GT[:, :], 0.0).then_inc(sems["gt_ready"], 1)
            dve.memset(YB[:, 0:512], 0.0).then_inc(sems["yb0_ready"], 1)
            dve.memset(YB[:, 512:D], 0.0).then_inc(sems["yb1_ready"], 1)
            dve.wait_ge(sems["const_ready"], 6)
            step(ts(REV[:, :], IOTA[:, 0:8], -1.0, 8.0, ALU.mult, ALU.add))
            b = wait_filled(dve, "lg")
            tt(LG[:, :, :], b[:, 0:72].rearrange("p (i n) -> p i n", n=36), bc(PBC[:, 12:48], 1, NT), ALU.add).then_inc(freed, 1)
            wait_emptied(dve, "lg")
            lg4 = LG[:, :, 0:NG]

            def first_max(src, n, k):
                step(dve.tensor_reduce(rv(k, 1), src, X, ALU.max))
                step(tt(rv(k + 1, n), src, rv(k, 1).to_broadcast([P, NT, n]), ALU.is_equal))
                step(tt(rv(k + 1, n), rv(k + 1, n), bc(REV[:, 8 - n:8], 1, NT), ALU.mult))
                step(dve.tensor_reduce(rv(k + 2, 1), rv(k + 1, n), X, ALU.max))
                step(tt(rv(k + 3, n), rv(k + 1, n), rv(k + 2, 1).to_broadcast([P, NT, n]), ALU.is_equal))

            first_max(lg4, NG, 0)
            tt(rv(4, 4), lg4, rv(0, 1).to_broadcast([P, NT, NG]), ALU.subtract).then_inc(sems["gr_in"], 1)
            prod = E32[:, 0, :].rearrange("p (i e g) -> p i e g", i=NT, g=NG)
            step(tt(prod, LG[:, :, NG:36].rearrange("p i (g e) -> p i e g", g=NG), bc(rv(3, 4), 2, PG), ALU.mult))
            step(dve.tensor_reduce(rv(6, 8), prod, X, ALU.add))
            first_max(rv(6, 8), PG, 7)
            step(stt(rv(11, 8), rv(10, 8), NEG, rv(6, 8), ALU.mult, ALU.add))
            first_max(rv(11, 8), PG, 12)
            tt(rv(16, 1), rv(12, 1), rv(7, 1), ALU.subtract).then_inc(sems["t2_in"], 1)
            dve.wait_ge(sems["gr_exp"], 1)
            step(dve.tensor_reduce(rv(5, 1), rv(4, 4), X, ALU.add))
            step(dve.reciprocal(rv(5, 1), rv(5, 1)))
            step(tt(rv(20, 8), rv(10, 8), rv(15, 8), ALU.add))
            hot = lambda v: (bc(rv(3, 4), 3, PG), bc(v, 2, NG))
            v4 = lambda t: t.rearrange("p i (g e) -> p i g e", g=NG)
            tt(v4(E32[:, 1, :].rearrange("p (i n) -> p i n", i=NT)), *hot(rv(20, 8)), ALU.mult).then_inc(sems["onehot_ready"], 1)
            dve.wait_ge(sems["t2_exp"], 1)
            step(ts(rv(17, 1), rv(16, 1), 1.0, None, ALU.add))
            step(dve.reciprocal(rv(17, 1), rv(17, 1)))
            step(tt(rv(18, 1), rv(17, 1), rv(5, 1), ALU.mult))
            step(tt(rv(19, 1), rv(18, 1), rv(16, 1), ALU.mult))
            tt(rv(21, 8), rv(10, 8), rv(18, 1).to_broadcast([P, NT, 8]), ALU.mult)
            step(tt(rv(22, 8), rv(15, 8), rv(19, 1).to_broadcast([P, NT, 8]), ALU.mult))
            step(tt(rv(21, 8), rv(21, 8), rv(22, 8), ALU.add))
            step(tt(v4(WT[:, :, 0:NE]), *hot(rv(21, 8)), ALU.mult))
            b = wait_filled(dve, "rank")
            dve.tensor_copy(E32[:, 2, :], b[:, 0:2 * NE])
            dve.tensor_copy(E32[:, 3, 0:NE], b[:, 2 * NE:3 * NE]).then_inc(freed, 1)
            wait_emptied(dve, "rank")
            two = lambda k: E32[:, k, :].rearrange("p (i n) -> p i n", i=NT)
            rank, went = two(2), two(1)
            step(stt(KEY[:, :, 0:NE], rank, 1.0, went, ALU.add, ALU.mult))
            step(ts(KEY[:, :, 0:NE], KEY[:, :, 0:NE], -1.0, None, ALU.add))

            def selections(dst, pair, weighted):
                for i in range(NT):
                    for k in range(2):
                        key = KEY[:, i, bass.ds(2 * pair + k, 1)]
                        d = dst[:, i, k * CAP:(k + 1) * CAP]
                        if weighted:
                            ins = ts(d, IOTA[:, 0:CAP], key, WT[:, i, bass.ds(2 * pair + k, 1)], ALU.is_equal, ALU.mult)
                        else:
                            ins = ts(d, IOTA[:, 0:CAP], key, None, ALU.is_equal)
                return ins

            selections(SEL, 0, False).then_inc(sems["sel_ready"], 1)
            selections(SELW, 0, True).then_inc(sems["selw_ready"], 1)

            def half_of_tokens(count):
                dve.wait_ge(sems["gathered"], count)
                dve.tensor_copy(HS[:, 0:4, :], PS[:, 6, :].rearrange("p (c n) -> p c n", n=2 * CAP)).then_inc(sems["hs0_ready"], 1)

            half_of_tokens(1)

            cnt, nov, incl, start = E32[:, 3, 0:NE], E32[:, 4, 0:NE], E32[:, 4, NE:2 * NE], E32[:, 5, 0:NE]
            dve.memset(E32[:, 3, NE:2 * NE], 0.0)
            step(ts(nov, cnt, float(CAP), None, ALU.is_gt))
            step(stt(nov, cnt, 2.0 * CAP, nov, ALU.is_gt, ALU.add))
            step(stt(nov, cnt, 3.0 * CAP, nov, ALU.is_gt, ALU.add))
            step(dve.tensor_tensor_scan(incl, nov, E32[:, 3, NE:2 * NE], 0.0, ALU.add, ALU.add))
            step(tt(start, incl, nov, ALU.subtract))
            rb, gs, pos1 = two(6), two(7), two(0)
            step(ts(rb, rank, float(CAP), None, ALU.is_ge))
            step(stt(rb, rank, 2.0 * CAP, rb, ALU.is_ge, ALU.add))
            step(stt(rb, rank, 3.0 * CAP, rb, ALU.is_ge, ALU.add))
            step(stt(pos1, rb, -float(CAP), rank, ALU.mult, ALU.add))
            step(ts(pos1, pos1, 1.0, None, ALU.add))
            step(tt(gs, rb, bc(start, 1, NT), ALU.add))
            step(tt(gs, gs, went, ALU.mult))
            step(stt(gs, rb, 1.0, gs, ALU.min, ALU.mult))
            for i in range(NT):
                step(tt(OVS[:, 0], bc(gs[:, i, :], 1, OVN), bc(IOTA[:, 1:OVN + 1], 2, NE), ALU.is_equal))
                step(tt(OVS[:, 1], OVS[:, 0], bc(pos1[:, i, :], 1, OVN), ALU.mult))
                step(dve.tensor_reduce(OVK[:, i, :], OVS[:, 1], X, ALU.add))
                step(ts(OVK[:, i, :], OVK[:, i, :], -1.0, None, ALU.add))
                step(tt(OVS[:, 1], OVS[:, 0], bc(WT[:, i, 0:NE], 1, OVN), ALU.mult))
                step(dve.tensor_reduce(OVW[:, i, :], OVS[:, 1], X, ALU.add))
            step(tt(OVS[:, 0], bc(incl, 1, OVN), bc(IOTA[:, 0:OVN], 2, NE), ALU.is_le))
            step(dve.tensor_reduce(OVF[:, 0:OVN], OVS[:, 0], X, ALU.add))
            dve.tensor_copy(OVF[:, OVN:OVN + 1], incl[:, NE - 1:NE])
            step(ts(OVF[:, 0:OVN], OVF[:, 0:OVN], float(NE - 1), None, ALU.min))
            dve.tensor_copy(OVI[:, 0:OVN + 1], OVF[:, 0:OVN + 1]).then_inc(sems["over_ready"], 1)

            def silu_times_up(m, width):
                es = ES[:, 0:width]
                n = [0]

                def link(ins):
                    n[0] += 1
                    ins.then_inc(sems["silu_step"], 1)
                    dve.wait_ge(sems["silu_step"], 3 * m + n[0])

                dve.wait_ge(sems["gate_exp"], m + 1)
                link(ts(es, es, 1.0, None, ALU.add))
                link(dve.reciprocal(es, es))
                link(tt(es, PS[:, 4, 0:width], es, ALU.mult))
                dve.wait_ge(sems["up_filled"], m + 1)
                tt(AM[:, 0:width], PS[:, 5, 0:width], es, ALU.mult).then_inc(sems["am_ready"], 1)

            with dve.Fori(0, NE // 2) as m:
                dve.wait_ge(sems["gathered"], m + 1)
                selections(SEL, m + 1, False).then_inc(sems["sel_ready"], 1)
                silu_times_up(m, EFF)
                half_of_tokens(m + 2)
                dve.wait_ge(sems["weights_turned"], m + 1)
                selections(SELW, m + 1, True).then_inc(sems["selw_ready"], 1)
                dve.wait_ge(sems["down_filled"], 2 * m + 2)
                dve.tensor_copy(YB[:, 512:D], PS[:, 7, :]).then_inc(sems["yb1_ready"], 1)

            dve.wait_ge(sems["over_ready"], 1)
            n_over = dve.value_load(OVI[0:1, OVN:OVN + 1], min_val=0, max_val=OVN)
            with dve.Fori(0, OVN) as x:
                with dve.If(n_over > x):
                    dve.wait_ge(sems["gathered"], x + NE // 2 + 1)
                    dve.wait_ge(sems["weights_turned"], x + NE // 2)
                    dve.wait_ge(sems["selw_ready"], x + NE // 2 + 1)
                    for i in range(NT):
                        key = OVK[:, i, bass.ds(x, 1)]
                        for k in range(2):
                            d = slice(k * CAP, (k + 1) * CAP)
                            ins = ts(SEL[:, i, d], IOTA[:, 0:CAP], key, None, ALU.is_equal)
                    ins.then_inc(sems["sel_ready"], 1)
                    for i in range(NT):
                        key = OVK[:, i, bass.ds(x, 1)]
                        for k in range(2):
                            d = slice(k * CAP, (k + 1) * CAP)
                            ins = ts(SELW[:, i, d], IOTA[:, 0:CAP], key, OVW[:, i, bass.ds(x, 1)], ALU.is_equal, ALU.mult)
                    ins.then_inc(sems["selw_ready"], 1)
                    half_of_tokens(x + NE // 2 + 2)
                    silu_times_up(x + NE // 2, EFF // 2)
            dve.wait_ge(sems["x_done"], n_over + 1)
            for i in range(NT):
                for n in range(2):
                    t = YTMP[:, i, n * 512:(n + 1) * 512]
                    xr = XR[:, i, n * 512:(n + 1) * 512]
                    step(tt(t, PS[:, 2 * i + n, :], G12[:, 1, n * 512:(n + 1) * 512], ALU.mult))
                    ins = tt(xr, xr, t, ALU.add)
            ins.then_inc(sems["x_ready"], 1)
            dve.wait_ge(sems["rstd_ready"], 5)
            for i in range(NT):
                stt(XR[:, i, :], XR[:, i, :], RSTD[:, i:i + 1], FG[:, :], ALU.mult, ALU.mult).then_inc(sems["out_ready"], 1)



NAMES = ["x", "norm_mix", "w_in", "conv_w", "a_log", "dt_bias", "gdn_norm", "nsa_q_norm", "nsa_k_norm", "cmp_pos",
         "cmp_w1", "cmp_w2", "pool_w", "pool_scale", "w_out", "norm_ffn", "w_ffn1", "w_ffn2", "c_2", "ada_w_2",
         "ada_b_2", "norm_g_2", "final_g_2", "sb_w_in_2", "sb_w_out_2", "moe_w_grp_2", "moe_b_grp_2", "moe_w_exp_2",
         "moe_b_exp_2", "moe_w_gate_2", "moe_w_up_2", "moe_w_down_2"]


def kernel(**inputs):
    import numpy as np
    import concourse.bacc as bacc
    from concourse.bass_utils import run_bass_kernel_spmd

    nc = bacc.Bacc("TRN2", target_bir_lowering=False, num_devices=1, dynamic_dma_scratch_size=1024)
    arrays, aps = {}, {}
    for name in NAMES:
        v = np.ascontiguousarray(inputs[name])
        arrays[f"in_{name}_dram"] = v
        aps[name] = nc.dram_tensor(f"in_{name}_dram", v.shape, F32, kind="ExternalInput").ap()
    out = nc.dram_tensor("out_0_dram", (1, T, D), F32, kind="ExternalOutput").ap()
    build(nc, aps, out)
    r = run_bass_kernel_spmd(nc, [arrays], core_ids=[0])
    return r.results[0]["out_0_dram"]
```

```python
from contextlib import ExitStack

import concourse.bass as bass
from concourse import mybir

F32 = mybir.dt.float32
I32 = mybir.dt.int32
ALU = mybir.AluOpType
ACT = mybir.ActivationFunctionType
X = mybir.AxisListType.X

P = 128
T = 256
NT = T // P
D = 1024
KC = D // P
EPS = 1e-6
NEG = -1e30
GH, HD = 6, 64
GW = GH * HD
HID = 256
CL, CS = 32, 16
NCB = T // CS - CL // CS + 1
NHB = 2 * T // CS + 1
POOLS = (2, 4, 8, 16)
DFF = 4 * D
SBH = D // HD
NPAIR = SBH // 2
NE, EFF = 32, 512
NG, PG = 4, 8
CAP = 64
SLOT = 4096
NSLOT = 6
SCALE = HD ** -0.5
NLV = 6

C_QKV, C_Z, C_B = 0, 3 * GW, 4 * GW
C_Q = C_B + 2 * GH
C_KV = C_Q + GW
C_GATE = C_KV + 6 * P
C_U = C_GATE + 3 * GH
D_IN = C_U + 4 * HD
IN_UNITS = [(0, 512), (512, 512), (1024, 512), (C_B, 2 * GH + GW), (C_KV, 512), (C_KV + 512, 256 + 3 * GH), (C_U, 256)]

R_MIX, R_FFN, R_NG, R_CONV, R_PS, R_ADA, R_QN, R_KN, R_GN = 0, 8, 16, 32, 68, 70, 118, 119, 122
N_ROWS = 123
R2_POS, R2_C, N_ROWS2 = 0, 32, 40


def group_table():
    g = [("cols", "D")]
    g += [(f"norm0_{b}", "D") for b in range(4)]
    g += [(f"qkv{b}", "A") for b in range(5)]
    for n in ("z", "bq"):
        g += [(f"{n}{i}", "A") for i in range(NT)]
    g += [(f"tr{i}{b}", "A") for i in range(NT) for b in range(3)]
    g += [("kcvc", "A"), ("kv0", "A"), ("kv1", "A")]
    g += [(f"qk{b}", "A") for b in range(3)] + [("gc", "D")] + [(f"r{b}", "D") for b in range(3)]
    g += [("kw0", "A"), ("kw1", "A")]
    g += [(f"kk{b}", "D") for b in range(3)] + [("u0", "A")] + [(f"kk{b}", "D") for b in range(3, 6)] + [("hid0", "A")]
    between = ([("hid1", "A")],
               [("u1", "A")],
               [("hidt", "A"), ("pm0", "A"), ("pm1", "A")],
               [("nt0", "D"), ("nt1", "D"), ("nt2", "D")],
               [("cmp", "D"), ("py0", "D"), ("py1", "D")],
               [("kct", "D")] + [(f"ss0{b}", "D") for b in range(2)],
               [(f"sw0{b}", "D") for b in range(2)] + [("cs0", "D")])
    for lv in range(NLV + 1):
        g += [(f"P{lv}{b}", "D") for b in range(2)]
        g += between[lv]
        for b in range(2):
            g += ([(f"T{lv}{b}", "A")] if 0 < lv < NLV else []) + ([(f"TT{lv}{b}", "A")] if lv > 0 else [])
    g += [("x0", "D"), ("pc00", "A"), ("pc01", "A"), ("S", "D"), ("ps00", "A"), ("ps01", "A"), ("ks1", "D"),
          ("pw00", "A"), ("pw01", "A"), ("x1", "D"), ("no0", "A"), ("o0", "D"), ("qs1", "D"), ("o1", "D")]
    g += [(f"s{t}1{b}", "D") for t in "sw" for b in range(3)] + [("cs1", "D")]
    g += [(f"ya{b}", "D") for b in range(3)]
    g += [("pc10", "A"), ("pc11", "A")] + [(f"p{t}1{b}", "A") for t in "sw" for b in range(3)] + [("no1", "A")]
    g += [(f"out{n}{i}", "D") for n in range(2) for i in range(NT)]
    g += [(f"norm1_{b}", "D") for b in range(4)]
    g += [(f"norm2_{b}", "D") for b in range(4)]
    g += [(f"sq{b}", "A") for b in range(8)]
    g += [(f"sv{n}{i}", "A") for n in range(2) for i in range(NT)]
    g += [(f"so{n}{i}", "D") for n in range(2) for i in range(NT)]
    g += [(f"norm3_{b}", "D") for b in range(4)]
    g += [("lg", "D")] + [(f"h2{i}{b}", "A") for i in range(NT) for b in range(2)] + [("rank", "D")]
    return g


def build(nc, a, out):
    ctx = ExitStack()
    with ctx:
        def sb(name, shape, dt=F32):
            return ctx.enter_context(nc.sbuf_tensor(name, shape, dt))

        sems = {}

        def sem(*names):
            for n in names:
                sems[n] = ctx.enter_context(nc.semaphore(n))

        PS = ctx.enter_context(nc.psum_tensor("PS", [P, 8, 512], F32))

        slots = [sb(f"slot{s}", [P, SLOT]) for s in range(NSLOT)]
        XH = sb("XH", [P, 2 * NT * D])
        XR = XH[:, 0:NT * D].rearrange("p (a b) -> p a b", b=D)
        HT = XH[:, NT * D:2 * NT * D].rearrange("p (a b) -> p a b", b=T)
        XN = sb("XN", [P, NT, D])
        IDENT = sb("IDENT", [P, P])
        UPI = sb("UPI", [P, P])
        UPS = sb("UPS", [P, P])
        ONES = sb("ONES", [P, P])
        NLOW = sb("NLOW", [P, P])
        NONES = sb("NONES", [P, P])
        LVM = sb("LVM", [P, NLV, HD])
        LVMT = sb("LVMT", [P, HD])
        IDB = sb("IDB", [P, HD])
        QNEG = sb("QNEG", [P, 2, P])
        SBNEG = sb("SBNEG", [P, 3, P])
        CNEG = sb("CNEG", [P, NT, 16])
        CONE = sb("CONE", [P, NT, 16])
        IOTA = sb("IOTA", [P, 4 * CAP])
        EPSC = sb("EPSC", [P, 2])
        COL = sb("COL", [P, 168])
        ROWS = sb("ROWS", [P, 2, P])
        PBC = sb("PBC", [P, 12 + 36])
        W2 = sb("W2", [P, 4, HD])
        POOLW = sb("POOLW", [P, 2, HD])
        RW = sb("RW", [P, KC, 36])
        SM = sb("SM", [P, 640])
        YT_AT, RING_AT = 17900, 17472
        AR = sb("AR", [P, RING_AT + SLOT])
        YT = AR[:, YT_AT:YT_AT + KC * T].rearrange("p (a b) -> p a b", b=T)

        def carve(at, *dims):
            n = 1
            for d in dims:
                n *= d
            v = AR[:, at:at + n]
            if len(dims) == 2:
                v = v.rearrange("p (a b) -> p a b", b=dims[1])
            if len(dims) == 3:
                v = v.rearrange("p (a b c) -> p a b c", b=dims[1], c=dims[2])
            return v

        at = 0
        TOK = carve(at, NT, 18, HD); at += NT * 18 * HD
        NTT = carve(at, 5, T); at += 5 * T
        QKT = carve(at, 6, T); at += 6 * T
        SIG = carve(at, NT, 408); at += NT * 408
        SG = carve(at, NT, 408); at += NT * 408
        VS = carve(at, NT, P); at += NT * P
        VW = carve(at, NT, P); at += NT * P
        KCN = carve(at, 64); at += 64
        VC = carve(at, 2, HD); at += 128
        KCT = carve(at, 16); at += 16
        HIDT = carve(at, 2, 2, NHB); at += 4 * NHB
        HIDT4 = HIDT.rearrange("p k c n -> p (k c) n")
        HX = carve(at, 4, 30); at += 120
        B0 = at
        QKVT = carve(at, 9, 3 + T); at += 9 * (3 + T)
        CV = carve(at, 9, T); C0 = at; at += 9 * T
        EX = carve(at, 9, T); E0 = at; at += 9 * T
        D0 = at
        XK = carve(at, 2, 3, T); at += 2 * 3 * T
        NQK = carve(at, NT, 10, HD); at += NT * 10 * HD
        assert at <= YT_AT, at
        BAND = XN[:, :, :].rearrange("p a b -> p (a b)").rearrange("p (w i t) -> p w i t", w=4, i=NT)
        UTOK = carve(B0, 2, T)
        MT = carve(B0 + 2 * T, 2, T)
        HIDC = carve(B0 + 4 * T, 2, HID)
        DEC = carve(C0, 12, P)
        LT = carve(C0 + 12 * P, 12, P)
        SQ = AR[:, E0 + 6 * P:E0 + 18 * P]
        assert C0 + 24 * P == E0 + 6 * P
        TTM = carve(E0 + 6 * P, 12, P)
        slot_view = lambda s, lo, a_, b_: slots[s][:, lo:lo + a_ * b_].rearrange("p (a b) -> p a b", b=b_)
        QKD = slot_view(5, 0, 12, P)
        TB = slot_view(5, 12 * P, 12, HD)
        TTB = slot_view(5, 18 * P, 12, HD)
        PM = slot_view(5, 24 * P, 12, HD)
        VN = slots[5][:, 24 * P:24 * P + 2 * GW].rearrange("p (i h d) -> p i h d", i=NT, h=GH)
        OT2 = AR[:, C0:C0 + 2 * GW].rearrange("p (i h d) -> p i h d", i=NT, h=GH)
        TMP = AR[:, C0 + 2 * GW:C0 + 4 * GW].rearrange("p (i h d) -> p i h d", i=NT, h=GH)
        SST = slot_view(5, 12 * P, 3, HD)
        KD = slot_view(5, 12 * P + 256, GH, HD)
        RHS = slot_view(5, 12 * P + 700, GH, HD)
        PR = {"s": carve(D0, GH, T), "w": carve(D0 + GH * T, GH, T)}
        assert D0 + 2 * GH * T <= YT_AT
        PT = {"s": slot_view(0, 0, 2, GH * P), "w": slot_view(0, 2 * GH * P, 2, GH * P)}
        PCT = slot_view(0, 4 * GH * P, GH, P)
        PCM = slot_view(0, 5 * GH * P, GH, 16)

        AT = carve(0, 2, 4 * T)
        ADW = 384
        ADA = carve(2048, 2, KC, ADW)
        ACC = carve(2048 + 2 * KC * ADW, 6 * D)
        at = 2048 + 2 * KC * ADW + 6 * D
        G12 = carve(at, 2, D); at += 2 * D
        FG = carve(at, D); at += D
        MODC = carve(at, 48); at += 48
        COND = carve(at, 16); at += 16
        MROW = carve(2048, D)
        assert at <= RING_AT, at
        SQK = carve(0, 16, T)
        SV = carve(4096, NT, D)
        at = 6144
        SAB = carve(at, 2, 2, 3 * P); at += 12 * P
        SPB = carve(at, 2, 2, 3 * P); at += 12 * P
        SA = carve(at, 2, 2, 3 * P); at += 12 * P
        assert YT_AT + KC * T <= RING_AT + SLOT
        RING = tuple((slots[r][:, :], slots[r + 3][:, :]) for r in range(3)) + (
            (AR[:, 6144:6144 + SLOT], AR[:, 6144 + SLOT:6144 + 2 * SLOT]), (AR[:, RING_AT:RING_AT + SLOT], XH[:, :]))
        NR = len(RING)
        OVER = (RING[3][0], RING[3][1], RING[4][0])
        assert NE // 2 % NR == 1
        at = 0
        H2 = XN
        LG = carve(at, NT, 36); at += 72
        RT = carve(at, 24 * NT * 8); at += 24 * NT * 8
        E32 = carve(at, 8, NT * NE); at += 8 * NT * NE
        KEY = carve(at, NT, NE + 2); at += NT * (NE + 2)
        WT = carve(at, NT, NE + 2); at += NT * (NE + 2)
        REV = carve(at, 8); at += 8
        SEL = carve(at, NT, 2 * CAP); at += NT * 2 * CAP
        SELW = carve(at, NT, 2 * CAP); at += NT * 2 * CAP
        HS = carve(at, KC, 2 * CAP); at += KC * 2 * CAP
        ES = carve(at, EFF); at += EFF
        AM = carve(at, EFF); at += EFF
        AC = carve(at, 4, 2 * CAP); at += 4 * 2 * CAP
        GT = carve(at, T); at += T
        YB = carve(at, D); at += D
        OVN = T * 2 // (CAP + 1)
        OVK = carve(at, NT, OVN); at += NT * OVN
        OVW = carve(at, NT, OVN); at += NT * OVN
        OVS = carve(at, 2, OVN, NE); at += 2 * OVN * NE
        OVF = carve(at, 16); at += 16
        OVI = carve(at, 16).bitcast(I32); at += 16
        assert at <= 6144, at
        assert at <= 2048 + 2 * KC * ADW + 6 * D, at

        YTMP = XN[:, :, :]

        def rv(k, n):
            return RT[:, 16 * k:16 * k + NT * n].rearrange("p (i n) -> p i n", n=n)

        sm = [0]

        def small(*dims):
            n = 1
            for d in dims:
                n *= d
            v = SM[:, sm[0]:sm[0] + n]
            sm[0] += n
            assert sm[0] <= 640
            return v.rearrange("p (a b) -> p a b", b=dims[1]) if len(dims) == 2 else v

        SS = small(2)
        LNV = small(2)
        RSTD = small(2)
        N2 = small(24)
        RN = small(24)
        M2 = small(20)
        MR = small(20)
        SPV = small(NT, 6)
        SPE = small(NT, 6)
        GG = small(NT, 6)
        EA = small(6)
        GCS = small(12)
        GLS = small(6)
        EGC = small(6)
        KDE = small(6)
        MX = small(6)
        NMX = small(6)
        SUM = small(6)
        CF = small(6)
        CSUM = small(3, 6)
        O2 = small(12)
        OR = small(12)
        KN2 = small(2)
        BG = small(NT, 12)
        CNT = small(2, 16)
        RNL = small(24)
        RCP = small(4, 16)

        sem("x_loaded", "over_gate", "over_up", "over_down", "rows_loaded", "misc_loaded", "const_ready", "filled",
            "emptied_by_act", "emptied_by_dve", "halves_switched", "pool_step", "act_step", "dve_step", "rstd_ready",
            "xn_ready", "counts_ready", "recip_ready", "sig_exp", "conv_ready", "conv_exp", "silu_ready", "qk_sumsq",
            "qk_rnorm", "qk_ready", "hid_bias", "hid_exp", "hid_ready", "nqk_sumsq", "nqk_rnorm", "nqk_ready",
            "kc_sumsq", "kc_rnorm", "kc_ready", "pos_ready", "cmax", "cexp", "smax", "sexp", "probs_ready",
            "dt_added", "dt_parts", "g_ready", "decay_exp", "egc_ready", "lt_ready", "pm_ready", "rhs_ready",
            "o_sumsq", "o_rnorm", "ya_ready", "stored", "kd_ready", "x_ready", "ffn_hid_filled", "ffn_out_done",
            "ffn_relu", "ffn_act_ready", "ada_used0", "ada_used1", "ada_loaded0", "ada_loaded1", "ada_step",
            "rows_bc", "cond_exp", "sp_ln", "sp_ready", "gr_in", "gr_exp", "t2_in", "t2_exp", "onehot_ready",
            "over_ready", "out_ready", "down_filled", "hs0_ready", "hs1_ready", "gt_ready", "yb0_ready", "yb1_ready",
            "sel_ready", "selw_ready", "x_done", "sa_ready", "gate_filled", "up_filled", "gathered", "gate_exp",
            "hid_turned", "weights_turned", "ac_ready", "am_ready", "silu_step", "rw_loaded", "sb_scored", "sa_arg",
            "sb_out", "sb_out_copied", "sb_summed", "ttm_diagonal", "cprobs_ready", "t0_ready", "mod_rows_filled",
            "gates_filled", "mod_rows_copied", "mod_filled", "gates_taken", "x_in_sums")
        ring_loaded = [ctx.enter_context(nc.semaphore(f"ring_loaded{r}")) for r in range(NR)]
        for s in range(NSLOT):
            sem(f"loaded{s}")

        GROUPS = group_table()
        order = {n: k for k, (n, _) in enumerate(GROUPS)}

        def owner_count(k):
            return sum(o == GROUPS[k][1] for _, o in GROUPS[:k + 1])

        def bank(name):
            return PS[:, order[name] % 8, :]

        class Steps:

            def __init__(self, eng, name):
                self.eng, self.sem, self.n = eng, sems[name], 0

            def __call__(self, ins):
                self.n += 1
                ins.then_inc(self.sem, 1)
                self.eng.wait_ge(self.sem, self.n)

        emptied = {"A": sems["emptied_by_act"], "D": sems["emptied_by_dve"]}

        def pe_open(pe, name):
            k = order[name]
            if k >= 8:
                pe.wait_ge(emptied[GROUPS[k - 8][1]], owner_count(k - 8))
            return bank(name)

        def wait_emptied(eng, name):
            k = order[name]
            eng.wait_ge(emptied[GROUPS[k][1]], owner_count(k))

        def wait_filled(eng, name):
            eng.wait_ge(sems["filled"], order[name] + 1)
            return bank(name)

        uses = [("in0", 0, "qkv1"), ("in1", 1, "qkv3"), ("in2", 2, "z1"), ("in3", 3, "bq1"), ("in4", 4, "kv1"),
                ("in5", 5, "kw1"), ("in6", 0, "u1"), ("w1k", 1, "hid1"), ("w1v", 2, "hid1"), ("out0", 3, "out01"),
                ("out1", 4, "out11")]
        uses += [(f"ffn{v}{s}", s, None) for v in range(4) for s in range(4)]
        uses += [("sb0", 5, "sq1"), ("sb1", 4, "sq3"), ("sb2", 0, "sq5"), ("sb3", 1, "sq7"), ("sb4", 2, "sv01"),
                 ("sb5", 3, "sv11"), ("so0", 5, "so01"), ("so1", 4, "so11")]

        def use(name):
            k = [n for n, _, _ in uses].index(name)
            s = uses[k][1]
            return s, sum(t == s for _, t, _ in uses[:k + 1])

        def last_reader(name):
            k = [n for n, _, _ in uses].index(name)
            before = [r for _, t, r in uses[:k] if t == uses[k][1]]
            return before[-1] if before else None

        def bc(ap, axis, n):
            v = ap.unsqueeze(axis)
            shape = list(v.shape)
            shape[axis] = n
            return v.to_broadcast(shape)

        pieces = [
            (R_MIX, a["norm_mix"][0].rearrange("(r p) -> r p", p=P), 0, P),
            (R_FFN, a["norm_ffn"][0].rearrange("(r p) -> r p", p=P), 0, P),
            (R_NG, a["norm_g_2"][0].rearrange("n (r p) -> (n r) p", p=P), 0, P),
            (R_CONV, a["conv_w"][0].rearrange("k (r p) -> (k r) p", p=P), 0, P),
            (R_PS, a["pool_scale"][0].rearrange("(r p) -> r p", p=P), 0, P),
            (R_ADA, a["ada_b_2"][0].rearrange("(r p) -> r p", p=P), 0, P),
        ]
        for h in range(2):
            pieces += [
                (R_QN, a["nsa_q_norm"], h * HD, HD),
                (R_KN, a["nsa_k_norm"][0], h * HD, HD),
                (R_GN, a["gdn_norm"], h * HD, HD),
            ]
        row_loads = [(ROWS[r:r + src.shape[0], 0, c:c + w], src) for r, src, c, w in pieces]
        row_loads += [(ROWS[R2_POS + kv * 16:R2_POS + kv * 16 + 16, 1, :],
                       a["cmp_pos"][0, kv].rearrange("(m l) d -> m (l d)", l=2)) for kv in range(2)]
        row_loads += [(ROWS[R2_C:R2_C + 8, 1, :], a["c_2"][0].rearrange("(r p) -> r p", p=P))]

        block = ctx.enter_context(nc.Block())

        @block.sync
        def _(sp):
            def fill(s, src):
                return sp.dma_start(slots[s][:, 0:src.shape[1] * src.shape[2]].rearrange("p (c n) -> p c n", n=src.shape[2]), src)\
                    .then_inc(sems[f"loaded{s}"], 16)

            def load(name, src):
                s, n = use(name)
                r = last_reader(name)
                if r is not None:
                    sp.wait_ge(sems["filled"], order[r] + 1)
                fill(s, src)

            for i in range(NT):
                sp.dma_start(XR[:, i, :], a["x"][0, i * P:(i + 1) * P, :]).then_inc(sems["x_loaded"], 16)
            for k in range(8):
                sp.dma_start(*row_loads[k]).then_inc(sems["rows_loaded"], 16)
            w_in = a["w_in"][0].rearrange("(c p) n -> p c n", p=P)
            for u, (c0, w) in enumerate(IN_UNITS):
                if u == 1:
                    sp.wait_ge(sems["rows_loaded"], 16 * len(row_loads))
                load(f"in{u}", w_in[:, :, c0:c0 + w])
            for kv, n in enumerate(("w1k", "w1v")):
                load(n, a["cmp_w1"][0, kv].rearrange("(m p) n -> p m n", p=P))
            w_out = a["w_out"][0].rearrange("(c p) n -> p c n", p=P)
            for h in range(2):
                load(f"out{h}", w_out[:, :, h * 512:(h + 1) * 512])
            sp.dma_start(RW[:, :, 0:4], a["moe_w_grp_2"][0].rearrange("(c p) n -> p c n", p=P)).then_inc(sems["rw_loaded"], 16)
            sp.dma_start(RW[:, :, 4:36], a["moe_w_exp_2"][0].rearrange("(c p) n -> p c n", p=P)).then_inc(sems["rw_loaded"], 16)
            sb_in = a["sb_w_in_2"][0].rearrange("(c p) n -> p c n", p=P)
            sb_out = a["sb_w_out_2"][0].rearrange("(c p) n -> p c n", p=P)
            w_f1 = a["w_ffn1"][0].rearrange("(c p) n -> p c n", p=P)
            w_f2 = a["w_ffn2"][0].rearrange("(u c p) n -> u p c n", c=4, p=P)
            w_ada = a["ada_w_2"][0].rearrange("(c p) n -> p c n", p=P)

            def ffn_weights(v, j, first):
                if not first:
                    sp.wait_ge(sems["ffn_hid_filled"], 4 * v - 2 + 2 * j)
                fill(2 * j, w_f1[:, :, bass.ds((2 * v + j) * 512, 512)])
                if not first:
                    sp.wait_ge(sems["ffn_out_done"], 2 * v - 1 + j)
                fill(2 * j + 1, w_f2[bass.ds(2 * v + j, 1), :, :, :].rearrange("u p c n -> p (u c) n"))

            def ada_parts(v, j, first):
                for k in range(2):
                    if not (first and j == 0):
                        sp.wait_ge(sems[f"ada_used{k}"], 2 * v + j)
                    sp.dma_start(ADA[:, k], w_ada[:, :, bass.ds((4 * v + 2 * j + k) * ADW, ADW)])\
                        .then_inc(sems[f"ada_loaded{k}"], 16)

            sp.wait_ge(sems["filled"], order["no1"] + 1)
            ffn_weights(0, 0, True)
            sp.wait_ge(sems["filled"], order["out01"] + 1)
            ffn_weights(0, 1, True)
            wait_emptied(sp, "norm1_0")
            for j in range(2):
                ada_parts(0, j, True)
            for k, seg in enumerate((2, 5)):
                sp.dma_start(G12[:, k, :], a["ada_b_2"][0, seg * D:(seg + 1) * D].partition_broadcast(P)).then_inc(sems["rows_bc"], 16)
            sp.dma_start(FG[:, :], a["final_g_2"].partition_broadcast(P)).then_inc(sems["rows_bc"], 16)
            load("sb0", sb_in[:, :, 0:512])
            with sp.Fori(1, 4) as v:
                for j in range(2):
                    ffn_weights(v, j, False)
                    ada_parts(v, j, False)
            load("sb1", sb_in[:, :, 512:1024])
            sp.wait_ge(sems["ffn_hid_filled"], 14)
            fill(0, sb_in[:, :, 1024:1536])
            sp.wait_ge(sems["ffn_out_done"], 7)
            fill(1, sb_in[:, :, 1536:2048])
            sp.wait_ge(sems["ffn_hid_filled"], 16)
            fill(2, sb_in[:, :, 2048:2560])
            sp.wait_ge(sems["ffn_out_done"], 8)
            fill(3, sb_in[:, :, 2560:3072])
            load("so0", sb_out[:, :, 0:512])
            load("so1", sb_out[:, :, 512:1024])
            kinds = [a[f"moe_w_{w}_2"][0].rearrange("e (c p) n -> e p c n", p=P) for w in ("gate", "up", "down")]
            made = ("gate_filled", "up_filled", "down_filled")
            per_pair = (1, 1, 2)

            def expert(dst, kind, e):
                return sp.dma_start(dst, kinds[kind][bass.ds(e, 1), :, :, :].rearrange("e p c n -> p (e c) n"))

            def ring(u, k, g=0):
                dst = RING[u % NR][k].rearrange("p (c n) -> p c n", n=(EFF, EFF, D)[u % 3])
                expert(dst, u % 3, 2 * NR * g + 2 * (u // 3) + k).then_inc(ring_loaded[u % NR], 16)

            for u, k, r in ((0, 0, "sq5"), (1, 0, "sq7"), (2, 0, "sv01"), (0, 1, "sv11"), (2, 1, "so01"), (1, 1, "so11")):
                sp.wait_ge(sems["filled"], order[r] + 1)
                ring(u, k)
            sp.wait_ge(sems["sb_out"], NPAIR)
            ring(3, 0)
            ring(3, 1)
            ring(4, 0)
            sp.wait_ge(sems["x_in_sums"], 1)
            ring(4, 1)

            def ring_unit(u, g):
                pair_before, kind = (u - NR) // 3, (u - NR) % 3
                sp.wait_ge(sems[made[kind]], per_pair[kind] * (NR * g + pair_before + 1))
                ring(u, 0, g)
                ring(u, 1, g)

            for u in range(NR, 3 * NR):
                ring_unit(u, 0)
            with sp.Fori(1, NE // 2 // NR) as g:
                for u in range(3 * NR):
                    ring_unit(u, g)
            for u in range(3 * (NE // 2 % NR)):
                ring_unit(u, NE // 2 // NR)
            sp.wait_ge(sems["over_ready"], 1)
            n_over = sp.value_load(OVI[0:1, OVN:OVN + 1], min_val=0, max_val=OVN)
            with sp.Fori(0, OVN) as k:
                with sp.If(n_over > k):
                    e = sp.value_load(OVI[0:1, bass.ds(k, 1)], min_val=0, max_val=NE - 1)
                    for kind in range(3):
                        sp.wait_ge(sems[made[kind]], k + per_pair[kind] * (NE // 2))
                        dst = OVER[kind].rearrange("p (c n) -> p c n", n=(EFF, EFF, D)[kind])
                        expert(dst, kind, e).then_inc(sems[("over_gate", "over_up", "over_down")[kind]], 16)
            for i in range(NT):
                sp.wait_ge(sems["out_ready"], i + 1)
                sp.dma_start(out[0, i * P:(i + 1) * P, :], XR[:, i, :]).then_inc(sems["stored"], 16)
            sp.wait_ge(sems["stored"], 16 * NT)

        @block.gpsimd
        def _(pool):
            step = Steps(pool, "pool_step")
            ready = sems["const_ready"]

            def tri(t, fill_true, cond, base, mult, pattern, op=ALU.is_ge, fill=0.0):
                step(pool.affine_select(out=t, in_=t, compare_op=op, fill=fill, base=base,
                                        pattern=pattern, channel_multiplier=mult))

            step(pool.memset(IDENT[:, :], 0.0))
            pool.affine_select(out=IDENT[:, :], in_=IDENT[:, :], compare_op=ALU.not_equal, fill=1.0, base=0,
                               pattern=[[-1, P]], channel_multiplier=1).then_inc(ready, 1)
            pool.memset(EPSC[:, 0:1], EPS)
            step(pool.memset(EPSC[:, 1:2], 1.0))
            pool.memset(ONES[:, :], 1.0)
            pool.memset(NONES[:, :], -1.0)
            pool.memset(QKVT[:, :, 0:3], 0.0)
            pool.memset(XK[:, :, 2, :], 0.0)
            pool.memset(NLOW[:, :], -1.0)
            pool.memset(UPI[:, :], 1.0)
            step(pool.memset(UPS[:, :], 1.0))
            pool.affine_select(out=UPI[:, :], in_=UPI[:, :], compare_op=ALU.is_ge, fill=0.0, base=0,
                               pattern=[[1, P]], channel_multiplier=-1)
            pool.affine_select(out=UPS[:, :], in_=UPS[:, :], compare_op=ALU.is_gt, fill=0.0, base=0,
                               pattern=[[1, P]], channel_multiplier=-1)
            pool.affine_select(out=NLOW[:, :], in_=NLOW[:, :], compare_op=ALU.is_ge, fill=0.0, base=0,
                               pattern=[[-1, P]], channel_multiplier=1).then_inc(ready, 1)
            pool.iota(CNT[:, 0, :], [[1, 16]], base=1, channel_multiplier=0,
                      allow_small_or_imprecise_dtypes=True).then_inc(sems["counts_ready"], 1)
            pool.wait_ge(sems["filled"], order["norm0_3"] + 1)
            for w in range(4):
                step(pool.memset(BAND[:, w], 1.0 / POOLS[w]))
                step(pool.affine_select(out=BAND[:, w], in_=BAND[:, w], compare_op=ALU.is_ge, fill=0.0, base=0,
                                        pattern=[[-P, NT], [1, T]], channel_multiplier=-1))
                step(pool.affine_select(out=BAND[:, w], in_=BAND[:, w], compare_op=ALU.is_ge, fill=0.0,
                                        base=POOLS[w] - 1, pattern=[[P, NT], [-1, T]], channel_multiplier=1))
            pool.wait_ge(sems["recip_ready"], 1)
            for w in range(4):
                ins = pool.tensor_tensor(BAND[:, w, 0, 0:16], BAND[:, w, 0, 0:16], RCP[:, w, :], ALU.mult)
            step(ins)
            for w in range(4):
                for i in range(NT):
                    last = pool.tensor_tensor(BAND[:, w, i, i * P:(i + 1) * P], BAND[:, w, i, i * P:(i + 1) * P],
                                              IDENT[:, :], ALU.subtract)
            last.then_inc(ready, 1)
            pool.memset(QNEG[:, :, :], 0.0)
            pool.memset(CNEG[:, :, :], 0.0)
            pool.memset(SBNEG[:, :, :], 0.0)
            step(pool.memset(CONE[:, :, :], 1.0))
            pool.affine_select(out=QNEG[:, 1, :], in_=QNEG[:, 1, :], compare_op=ALU.is_ge, fill=NEG, base=0,
                               pattern=[[-1, P]], channel_multiplier=1)
            for m, fill in ((CNEG, NEG), (CONE, 0.0)):
                last = pool.affine_select(out=m[:, :, :], in_=m[:, :, :], compare_op=ALU.is_ge, fill=fill,
                                          base=-(CL - 1), pattern=[[P, NT], [-CS, 16]], channel_multiplier=1)
            for j in (0, 2):
                last = pool.affine_select(out=SBNEG[:, j, :], in_=SBNEG[:, j, :], compare_op=ALU.is_gt, fill=NEG,
                                          base=0, pattern=[[1, P]], channel_multiplier=-1)
            last.then_inc(ready, 1)
            full = YT[:, :, :].rearrange("p a b -> p (a b)").rearrange("p (l n) -> p l n", n=P)
            pool.iota(IOTA[:, :], [[1, 4 * CAP]], base=0, channel_multiplier=0,
                      allow_small_or_imprecise_dtypes=True).then_inc(ready, 1)
            step(pool.memset(full[:, NLV, :], 0.0))
            odd = full[:, NLV, :].rearrange("p (n h) -> p n h", h=2)[:, :, 1]
            step(pool.affine_select(out=odd, in_=odd, compare_op=ALU.not_equal, fill=-1.0, base=0,
                                    pattern=[[-2, P // 2]], channel_multiplier=1))
            for lv in range(NLV):
                b = 1 << lv
                v = full[:, lv, :].rearrange("p (n h r) -> p n h r", h=2, r=b)
                pool.memset(v[:, :, 0, :], -1.0)
                step(pool.memset(v[:, :, 1, :], 0.0))
                w = full[:, lv, :].rearrange("p (n r) -> p n r", r=2 * b)
                step(pool.affine_select(out=w, in_=w, compare_op=ALU.is_ge, fill=0.0, base=-b,
                                        pattern=[[-2 * b, P // (2 * b)], [0, 2 * b]], channel_multiplier=1))
                step(pool.affine_select(out=w, in_=w, compare_op=ALU.is_ge, fill=0.0, base=2 * b - 1,
                                        pattern=[[2 * b, P // (2 * b)], [0, 2 * b]], channel_multiplier=-1))
            for h in range(2):
                rows, cols = slice(h * HD, (h + 1) * HD), slice(h * HD, (h + 1) * HD)
                step(pool.tensor_copy(LVM[rows, :, :], full[rows, 0:NLV, cols]))
                step(pool.tensor_copy(LVMT[rows, :], full[rows, NLV, cols]))
                if h == 0:
                    step(pool.tensor_copy(IDB[rows, :], IDENT[rows, cols]))
                else:
                    pool.tensor_copy(IDB[rows, :], IDENT[rows, cols]).then_inc(ready, 1)
            wait_emptied(pool, f"TT{NLV - 1}1")
            pool.wait_ge(sems["nqk_ready"], 1)
            pool.wait_ge(ready, 6)
            step(pool.memset(TTM[HD:P, :, 0:HD], 0.0))
            step(pool.tensor_copy(TTM[0:HD, :, 0:HD], TTB[0:HD, :, :]))
            pool.tensor_copy(TTM[HD:P, :, HD:P], TTB[HD:P, :, :]).then_inc(sems["ttm_diagonal"], 1)

        @block.scalar
        def _(act):
            act.preload_act_table_set("natural_log_exp_and_others")
            step = Steps(act, "act_step")
            for k in range(8, len(row_loads)):
                act.dma_start(*row_loads[k]).then_inc(sems["rows_loaded"], 16)
            act.dma_start(PBC[:, 0:6], a["a_log"][0].partition_broadcast(P)).then_inc(sems["misc_loaded"], 16)
            act.dma_start(PBC[:, 6:12], a["dt_bias"][0].partition_broadcast(P)).then_inc(sems["misc_loaded"], 16)
            act.dma_start(W2[:, :, :].rearrange("p (k m) d -> p k m d", m=2),
                          a["cmp_w2"][0].rearrange("k (m p) d -> p k m d", p=P)).then_inc(sems["misc_loaded"], 16)
            act.dma_start(POOLW[:, :, :], a["pool_w"][0].rearrange("(j g) c d -> (g c) j d", g=2)).then_inc(sems["misc_loaded"], 16)
            act.dma_start(PBC[:, 12:16], a["moe_b_grp_2"][0].partition_broadcast(P)).then_inc(sems["misc_loaded"], 16)
            act.dma_start(PBC[:, 16:48], a["moe_b_exp_2"][0].partition_broadcast(P)).then_inc(sems["misc_loaded"], 16)

            def rsqrt(dst, src, scale, tmp, done):
                step(act.activation(tmp, src, ACT.Ln, scale=scale, bias=EPSC[0:src.shape[0], 0:1]))
                act.activation(dst, tmp, ACT.Exp, scale=-0.5).then_inc(done, 1)

            def norm_stats(n, ready=None, source=lambda i: XR[:, i, :].rearrange("p (h d) -> p h d", h=2)):
                for i in range(NT):
                    if ready:
                        act.wait_ge(sems["x_ready"], ready + i)
                    step(act.activation(XN[:, i, :].rearrange("p (h d) -> p h d", h=2), source(i), ACT.Square,
                                        accum_out=SS[:, i:i + 1]))
                rsqrt(RSTD, SS, 1.0 / D, LNV, sems["rstd_ready"])

            def empty(name, *pairs):
                b = wait_filled(act, name)
                for k, (dst, src) in enumerate(pairs):
                    ins = act.activation(dst, src(b), ACT.Copy)
                ins.then_inc(sems["emptied_by_act"], 1)

            act.wait_ge(sems["const_ready"], 1)
            act.wait_ge(sems["pool_step"], 2)
            act.wait_ge(sems["x_loaded"], 16 * NT)
            norm_stats(0)

            act.wait_ge(sems["const_ready"], 2)
            def silu_exp(b):
                n = 2 if b < 4 else 1
                act.wait_ge(sems["conv_ready"], b + 1)
                act.activation(EX[:, 2 * b:2 * b + n, :], CV[:, 2 * b:2 * b + n, :], ACT.Exp, scale=-1.0)\
                    .then_inc(sems["conv_exp"], 1)

            for b in range(5):
                n = 2 if b < 4 else 1
                empty(f"qkv{b}", (QKVT[:, 2 * b:2 * b + n, 3:3 + T], lambda s, n=n: s[:, 0:n * T].rearrange("p (j t) -> p j t", t=T)))
                if b:
                    silu_exp(b - 1)
            empty("z0", (SIG[:, 0, 0:GW], lambda s: s[:, 0:GW]))
            silu_exp(4)
            empty("z1", (SIG[:, 1, 0:GW], lambda s: s[:, 0:GW]))
            act.wait_ge(sems["const_ready"], 3)
            for i in range(NT):
                empty(f"bq{i}",
                      (BG[:, i, :], lambda s: s[:, 0:12]),
                      (SIG[:, i, GW:GW + 6], lambda s: s[:, 0:6]),
                      (NQK[:, i, 0:6, :].rearrange("p (j g) d -> p g j d", g=2),
                       lambda s: s[:, 12:12 + GW].rearrange("p (g j d) -> p g j d", g=2, d=HD)))
            wait_emptied(act, "bq1")
            act.activation(SG[:, :, 0:GW + 6], SIG[:, :, 0:GW + 6], ACT.Exp, scale=-1.0).then_inc(sems["sig_exp"], 1)
            for i in range(NT):
                for b in range(3):
                    n = 4 if b < 2 else 1
                    empty(f"tr{i}{b}", (TOK[:, i, 8 * b:8 * b + 2 * n, :],
                                        lambda s, n=n: s[:, 0:n * P].rearrange("p (h d) -> p h d", d=HD)))
            act.wait_ge(sems["dt_added"], 1)
            step(act.activation(SPE, SPV, ACT.Abs))
            step(act.activation(SPE, SPE, ACT.Exp, scale=-1.0))
            act.activation(EA, PBC[:, 0:6], ACT.Exp)
            act.activation(SPE, SPE, ACT.Ln, bias=EPSC[:, 1:2]).then_inc(sems["dt_parts"], 1)
            parts = []
            for kv in range(2):
                for h in range(2):
                    for l in range(2):
                        parts.append((XK[l * HD:(l + 1) * HD, kv, h, 0:T - l],
                                      lambda s, kv=kv, h=h, l=l: s[h * HD:(h + 1) * HD, kv * T + l:(kv + 1) * T]))
            empty("kcvc", *parts)
            act.wait_ge(sems["qk_sumsq"], 1)
            rsqrt(RN, N2, 1.0, RNL, sems["qk_rnorm"])
            for i in range(NT):
                empty(f"kv{i}", (NQK[:, i, 6:8, :], lambda s: s[:, 0:P].rearrange("p (h d) -> p h d", d=HD)),
                      (VS[:, i, :], lambda s: s[:, P:2 * P]))
            for b in range(3):
                empty(f"qk{b}", (QKT[:, 2 * b:2 * b + 2, :], lambda s: s[:, 0:512].rearrange("p (j t) -> p j t", t=T)))
            wait_emptied(act, "r2")
            act.activation(DEC[:, :, :], DEC[:, :, :], ACT.Exp).then_inc(sems["decay_exp"], 1)
            act.activation(EGC, GCS[:, 6:12], ACT.Exp)
            act.activation(KDE, KDE, ACT.Exp).then_inc(sems["egc_ready"], 1)
            for i in range(NT):
                empty(f"kw{i}", (NQK[:, i, 8:10, :], lambda s: s[:, 0:P].rearrange("p (h d) -> p h d", d=HD)),
                      (VW[:, i, :], lambda s: s[:, P:2 * P]),
                      (SIG[:, i, GW + 6:GW + 24], lambda s: s[:, 2 * P:2 * P + 18]))
            wait_emptied(act, "kw1")
            act.activation(SG[:, :, GW + 6:GW + 24], SIG[:, :, GW + 6:GW + 24], ACT.Exp, scale=-1.0).then_inc(sems["sig_exp"], 1)
            act.wait_ge(sems["nqk_sumsq"], 1)
            rsqrt(MR, M2, 1.0 / HD, N2[:, 0:20], sems["nqk_rnorm"])
            empty("u0", (UTOK[:, 0, :], lambda s: s[:, 0:T]))

            def hidden_part(n):
                empty(f"hid{n}", *[(HIDC[r:r + NHB, n, :], lambda s, r=r: s[r:r + NHB, 0:HID]) for r in (0, HD)])

            hidden_part(0)

            def nsa_exps(i):
                w = (i + 1) * P
                for t in range(2):
                    act.wait_ge(sems["smax"], 2 * i + t + 1)
                    for h in range(GH):
                        ins = act.activation(PR["sw"[t]][:, h, 0:w], PR["sw"[t]][:, h, 0:w], ACT.Exp, scale=SCALE,
                                             bias=(NMX if t == 0 else MX)[:, h:h + 1],
                                             accum_out=(SUM if t == 0 else CF)[:, h:h + 1])
                    ins.then_inc(sems["sexp"], 1)
                act.wait_ge(sems["cmax"], i + 1)
                act.activation(PCM[:, :, 0:NCB], PCM[:, :, 0:NCB], ACT.Exp, scale=SCALE).then_inc(sems["cexp"], 1)

            def nsa_compressed(i):
                if i > 0:
                    act.wait_ge(sems["filled"], order[f"no{i - 1}"] + 1)
                for j in range(2):
                    empty(f"pc{i}{j}", (PCT[0:NCB, 3 * j:3 * j + 3, :],
                                        lambda s: s[0:NCB, 0:3 * P].rearrange("p (h q) -> p h q", q=P)))

            def nsa_probs(i, t):
                for b in range(2 + i):
                    if i == 0:
                        n = 4 if b == 0 else 2
                        empty(f"p{t}{i}{b}", (PT[t][:, 0, 4 * b * P:(4 * b + n) * P], lambda s, n=n: s[:, 0:n * P]))
                    else:
                        empty(f"p{t}{i}{b}", (PT[t][:, :, 2 * b * P:(2 * b + 2) * P],
                                              lambda s: s[:, 0:512].rearrange("p (k q) -> p k q", k=2)))

            def nsa_output(i):
                empty(f"no{i}", (YT[:, 3:6, i * P:(i + 1) * P], lambda s: s[:, 0:3 * P].rearrange("p (j q) -> p j q", q=P)))

            v6 = lambda s: s[:, 0:GW].rearrange("p (a b) -> p a b", b=HD)
            for lv in range(NLV + 1):
                if lv == 0:
                    hidden_part(1)
                if lv == 1:
                    empty("u1", (UTOK[:, 1, :], lambda s: s[:, 0:T]))
                if lv == 2:
                    empty("hidt", (HIDT[:, :, :, :], lambda s: s[:, 0:4 * NHB].rearrange("p (k c n) -> p k c n", k=2, c=2)))
                    for j in range(2):
                        empty(f"pm{j}", (MT[:, j, :], lambda s: s[:, 0:T]))
                if lv == 3:
                    act.wait_ge(sems["hid_bias"], 1)
                    act.activation(HIDT4[:, :, 0:30], HX[:, :, :], ACT.Exp, scale=-1.0).then_inc(sems["hid_exp"], 1)
                if 0 < lv < NLV:
                    for b in range(2):
                        empty(f"T{lv}{b}", (TB[:, 6 * b:6 * b + 6, :], v6))
                        empty(f"TT{lv}{b}", (TTB[:, 6 * b:6 * b + 6, :], v6))
                if lv == 4:
                    act.wait_ge(sems["kc_sumsq"], 1)
                    rsqrt(KN2[0:30, 1:2], KN2[0:30, 0:1], 1.0 / HD, LNV[0:30, 0:1], sems["kc_rnorm"])
                if lv == NLV:
                    for b in range(2):
                        empty(f"TT{lv}{b}", (TTM[0:HD, 6 * b:6 * b + 6, HD:P],
                                             lambda s: s[0:HD, 0:GW].rearrange("p (a b) -> p a b", b=HD)))
            nsa_exps(0)
            nsa_compressed(0)
            nsa_probs(0, "s")
            nsa_probs(0, "w")
            nsa_output(0)
            act.wait_ge(sems["o_sumsq"], 1)
            rsqrt(OR, O2, 1.0 / HD, M2[:, 0:12], sems["o_rnorm"])
            nsa_exps(1)
            nsa_compressed(1)
            nsa_probs(1, "s")
            nsa_probs(1, "w")
            nsa_output(1)
            wait_emptied(act, "out11")
            norm_stats(1)
            act.activation(COND[:, 8:16], COL[:, P + R2_C:P + R2_C + 8], ACT.Exp, scale=-1.0).then_inc(sems["cond_exp"], 1)

            def ffn_units(v, first):
                for j in range(2):
                    if not first:
                        act.wait_ge(sems["ffn_out_done"], 2 * v - 1 + j)
                    for k in range(2):
                        act.wait_ge(sems["ffn_hid_filled"], 4 * v + 2 * j + k + 1)
                        act.activation(AT[:, j, k * 512:(k + 1) * 512], PS[:, 2 * j + k, :], ACT.Relu).then_inc(sems["ffn_relu"], 1)
                    for k in range(2):
                        act.wait_ge(sems["ffn_relu"], 4 * v + 2 * j + k + 1)
                        act.activation(AT[:, j, k * 512:(k + 1) * 512], AT[:, j, k * 512:(k + 1) * 512], ACT.Square)\
                            .then_inc(sems["ffn_act_ready"], 1)

            ffn_units(0, True)
            with act.Fori(1, 4) as v:
                ffn_units(v, False)
            norm_stats(2, 1)
            for b in range(8):
                bk = wait_filled(act, f"sq{b}")
                act.activation(SQK[:, 2 * b:2 * b + 2, :], bk[:, 0:512].rearrange("p (j t) -> p j t", t=T), ACT.Copy,
                               scale=SCALE if b < 4 else 1.0).then_inc(sems["emptied_by_act"], 1)
            for n in range(2):
                for i in range(NT):
                    empty(f"sv{n}{i}", (SV[:, i, n * 512:(n + 1) * 512], lambda s: s[:, 0:512]))
            def score_exps(t):
                act.wait_ge(sems["sb_scored"], t + 1)
                if t >= 2:
                    act.wait_ge(sems["sp_ready"], t - 1)
                ab = SAB[:, t % 2]
                step(act.activation(ab, PS[:, 2 * (t % 3):2 * (t % 3) + 2, 0:3 * P], ACT.Abs))
                step(act.activation(ab, ab, ACT.Exp, scale=-1.0))
                act.activation(ab, ab, ACT.Ln, bias=EPSC[:, 1:2]).then_inc(sems["sp_ln"], 1)

            score_exps(0)
            for t in range(NPAIR + 2):
                if 1 <= t <= NPAIR:
                    act.wait_ge(sems["sa_arg"], t)
                    act.activation(SA[:, (t - 1) % 2], SA[:, (t - 1) % 2], ACT.Exp).then_inc(sems["sa_ready"], 1)
                if t + 1 < NPAIR:
                    score_exps(t + 1)
                if t >= 2:
                    act.wait_ge(sems["sb_out"], t - 1)
                    act.activation(YT[:, t - 2, :], PS[:, 6 + t % 2, 0:T], ACT.Copy).then_inc(sems["sb_out_copied"], 1)
            wait_emptied(act, "so11")
            norm_stats(3)
            act.wait_ge(sems["gr_in"], 1)
            act.activation(rv(4, 4), rv(4, 4), ACT.Exp).then_inc(sems["gr_exp"], 1)
            for i in range(NT):
                for b in range(2):
                    empty(f"h2{i}{b}", (H2[:, i, b * 512:(b + 1) * 512], lambda s: s[:, 0:512]))
            act.wait_ge(sems["t2_in"], 1)
            act.activation(rv(16, 1), rv(16, 1), ACT.Exp).then_inc(sems["t2_exp"], 1)

            def half_of_tokens(count):
                act.wait_ge(sems["gathered"], count)
                act.activation(HS[:, 4:8, :], PS[:, 7, :].rearrange("p (c n) -> p c n", n=2 * CAP), ACT.Copy)\
                    .then_inc(sems["hs1_ready"], 1)

            def expert_copies(m, width):
                act.wait_ge(sems["gate_filled"], m + 1)
                act.activation(ES[:, 0:width], PS[:, 4, 0:width], ACT.Exp, scale=-1.0).then_inc(sems["gate_exp"], 1)

            def expert_transposed(m, width):
                act.wait_ge(sems["hid_turned"], m + 1)
                act.activation(AC[:, 0:width // P, :], PS[:, 4, 0:width].rearrange("p (f n) -> p f n", n=2 * CAP), ACT.Copy)\
                    .then_inc(sems["ac_ready"], 1)
                act.wait_ge(sems["weights_turned"], m + 1)
                act.activation(GT[:, :], PS[:, 5, 0:T], ACT.Copy).then_inc(sems["gt_ready"], 1)

            half_of_tokens(1)
            with act.Fori(0, NE // 2) as m:
                expert_copies(m, EFF)
                half_of_tokens(m + 2)
                expert_transposed(m, EFF)
            act.wait_ge(sems["over_ready"], 1)
            n_over = act.value_load(OVI[0:1, OVN:OVN + 1], min_val=0, max_val=OVN)

            def further_pass(x):
                expert_copies(x + NE // 2, EFF // 2)
                expert_transposed(x + NE // 2, EFF // 2)

            with act.If(n_over > 0):
                further_pass(0)
            with act.Fori(1, OVN) as x:
                with act.If(n_over > x):
                    half_of_tokens(x + NE // 2 + 1)
                    further_pass(x)
            act.wait_ge(sems["x_done"], n_over + 1)
            norm_stats(4, source=lambda i: PS[:, 2 * i:2 * i + 2, :])

        @block.tensor
        def _(pe):
            filled = sems["filled"]

            def weights(name):
                s, n = use(name)
                pe.wait_ge(sems[f"loaded{s}"], 16 * n)
                return slots[s]

            class Halves:
                n, last, p0 = 0, None, None

            def half(ins=None, p0=None, fresh=False):
                if fresh:
                    Halves.last = None
                elif ins is not None:
                    Halves.last, Halves.p0 = ins, p0
                elif Halves.last is not None and Halves.p0 != p0:
                    Halves.n += 1
                    Halves.last.then_inc(sems["halves_switched"], 1)
                    pe.wait_ge(sems["halves_switched"], Halves.n)
                return ins

            pe.wait_ge(sems["const_ready"], 1)
            pe.wait_ge(sems["rows_loaded"], 16 * len(row_loads))
            b = pe_open(pe, "cols")
            pe.transpose(b[:, 0:N_ROWS], ROWS[0:N_ROWS, 0, :], IDENT[0:N_ROWS, 0:N_ROWS])
            pe.transpose(b[:, P:P + N_ROWS2], ROWS[0:N_ROWS2, 1, :], IDENT[0:N_ROWS2, 0:N_ROWS2]).then_inc(filled, 1)

            def norm_transposes(n):
                for b4 in range(4):
                    b = pe_open(pe, f"norm{n}_{b4}")
                    for c in (2 * b4, 2 * b4 + 1):
                        for i in range(NT):
                            if b4 == 0 and c == 0:
                                pe.wait_ge(sems["xn_ready"], NT * n + i + 1)
                            o = (c % 2) * T + i * P
                            ins = pe.transpose(b[:, o:o + P], XN[:, i, c * P:(c + 1) * P], IDENT[:, :])
                    ins.then_inc(filled, 1)

            norm_transposes(0)
            wait_emptied(pe, "norm0_3")

            def channel_major(dst, w, width, col, n=P):
                for c in range(KC):
                    ins = pe.matmul(dst, w[:, c * width + col:c * width + col + n], HT[:, c, :], start=(c == 0), stop=(c == KC - 1))
                return ins

            def token_major(dst, w, width, col, n, i, src=HT):
                for c in range(KC):
                    ins = pe.matmul(dst, src[:, c, i * P:(i + 1) * P], w[:, c * width + col:c * width + col + n],
                                    start=(c == 0), stop=(c == KC - 1))
                return ins

            for g in range(5):
                b = pe_open(pe, f"qkv{g}")
                for j in (2 * g, 2 * g + 1):
                    if j < 9:
                        if j % 4 == 0:
                            w = weights(f"in{j // 4}")
                        ins = channel_major(b[:, (j % 2) * T:(j % 2) * T + T], w, 512, (j % 4) * P)
                        if j == 8 or j % 2 == 1:
                            ins.then_inc(filled, 1)
            def project(name, u, width, col, n):
                w = weights(f"in{u}")
                for i in range(NT):
                    b = pe_open(pe, f"{name}{i}")
                    token_major(b[:, 0:n], w, width, col, n, i).then_inc(filled, 1)

            project("z", 2, 512, P, GW)
            project("bq", 3, 396, 0, 396)
            pe.wait_ge(sems["silu_ready"], 5)
            for i in range(NT):
                for b3 in range(3):
                    b = pe_open(pe, f"tr{i}{b3}")
                    for j in range(4 * b3, min(4 * b3 + 4, 9)):
                        ins = pe.transpose(b[:, (j % 4) * P:(j % 4 + 1) * P], CV[:, j, i * P:(i + 1) * P], IDENT[:, :])
                    ins.then_inc(filled, 1)
            w = weights("in4")
            b = pe_open(pe, "kcvc")
            for kv in range(2):
                ins = channel_major(b[:, kv * T:(kv + 1) * T], w, 512, kv * P)
            ins.then_inc(filled, 1)
            project("kv", 4, 512, 256, 256)
            pe.wait_ge(sems["qk_ready"], 1)
            for b3 in range(3):
                b = pe_open(pe, f"qk{b3}")
                for j in (2 * b3, 2 * b3 + 1):
                    for i in range(NT):
                        o = (j % 2) * T + i * P
                        ins = pe.transpose(b[:, o:o + P], TOK[:, i, 2 * j:2 * j + 2, :].rearrange("p h d -> p (h d)"), IDENT[:, :])
                ins.then_inc(filled, 1)
            pe.wait_ge(sems["g_ready"], 1)
            b = pe_open(pe, "gc")
            for i in range(NT):
                pe.matmul(b[:, i * 6:(i + 1) * 6], UPI[:, :], GG[:, i, :], start=True, stop=True)
            pe.matmul(b[:, 12:18], ONES[:, :], GG[:, 0, :], start=True, stop=True).then_inc(filled, 1)
            for b3 in range(3):
                b = pe_open(pe, f"r{b3}")
                for q in range(4 * b3, 4 * b3 + 4):
                    ins = pe.matmul(b[:, (q % 4) * P:(q % 4 + 1) * P], GG[:, q // 6, q % 6:q % 6 + 1].to_broadcast([P, P]),
                                    UPI[:, :], start=True, stop=True)
                ins.then_inc(filled, 1)
            project("kw", 5, 274, 0, 274)
            wait_emptied(pe, "qk2")
            w_u = weights("in6")

            def project_u(i):
                b = pe_open(pe, f"u{i}")
                token_major(b[:, 0:T], w_u, T, 0, T, i).then_inc(filled, 1)

            for b6 in range(6):
                b = pe_open(pe, f"kk{b6}")
                half(fresh=True)
                for q in (2 * b6, 2 * b6 + 1):
                    i, h = q // 6, q % 6
                    p0 = (h % 2) * HD
                    half(p0=p0)
                    k = QKT[p0:p0 + HD, 3 + h // 2, i * P:(i + 1) * P]
                    ins = half(pe.matmul(b[:, (q % 2) * 256:(q % 2) * 256 + 256], k,
                                         QKT[p0:p0 + HD, h // 2:h // 2 + 4:3, i * P:(i + 1) * P], start=True, stop=True), p0)
                ins.then_inc(filled, 1)
                if b6 == 2:
                    project_u(0)

            def hidden_of_blocks(n):
                w = [weights("w1k"), weights("w1v")]
                xk = XK[:, :, :, :].rearrange("p k h t -> p k (h t)")
                b = pe_open(pe, f"hid{n}")
                wait_emptied(pe, "kcvc")
                pe.wait_ge(sems["pos_ready"], 1)
                for m in range(8 * n, 8 * n + 8):
                    for kv in range(2):
                        ins = pe.matmul(b[kv * HD:kv * HD + NHB, 0:HID], xk[:, kv, 2 * m:2 * m + CS * (NHB - 1) + 1:CS],
                                        w[kv][:, m * HID:(m + 1) * HID], start=(m % 8 == 0), stop=(m % 8 == 7))
                ins.then_inc(filled, 1)

            def turn_hidden_of_blocks():
                wait_emptied(pe, "hid1")
                b = pe_open(pe, "hidt")
                half(fresh=True)
                for kv in range(2):
                    p0 = kv * HD
                    half(p0=p0)
                    for hc in range(2):
                        for n in range(2):
                            ins = half(pe.matmul(b[:, (2 * kv + hc) * NHB:(2 * kv + hc + 1) * NHB],
                                                 HIDC[p0:p0 + NHB, n, hc * P:(hc + 1) * P], IDENT[p0:p0 + NHB, p0:p0 + NHB],
                                                 start=(n == 0), stop=(n == 1)), p0)
                ins.then_inc(filled, 1)

            def attention_turns():
                pe.wait_ge(sems["nqk_ready"], 1)
                for b3 in range(3):
                    b = pe_open(pe, f"nt{b3}")
                    for j in range(2 * b3, min(2 * b3 + 2, 5)):
                        for i in range(NT):
                            o = (j % 2) * T + i * P
                            ins = pe.transpose(b[:, o:o + P], NQK[:, i, 2 * j:2 * j + 2, :].rearrange("p h d -> p (h d)"), IDENT[:, :])
                    ins.then_inc(filled, 1)

            def pool_means():
                pe.wait_ge(sems["const_ready"], 3)
                wait_emptied(pe, "u1")
                for j in range(2):
                    b = pe_open(pe, f"pm{j}")
                    for g in range(2):
                        w = 2 * j + g
                        for i in range(NT):
                            ins = pe.matmul(b[g * HD:(g + 1) * HD, 0:T], UTOK[:, i, w * HD:(w + 1) * HD], BAND[:, w, i, :],
                                            start=(i == 0), stop=(i == NT - 1))
                    ins.then_inc(filled, 1)

            def compress_out():
                pe.wait_ge(sems["hid_ready"], 1)
                pe.wait_ge(sems["misc_loaded"], 16 * 6)
                b = pe_open(pe, "cmp")
                for hc in range(2):
                    pe.matmul(b[0:30, 0:HD], HX[:, hc, :], W2[:, hc, :], start=(hc == 0), stop=(hc == 1))
                for h in range(2):
                    for hc in range(2):
                        ins = pe.matmul(b[0:NCB, HD * (h + 1):HD * (h + 2)], HX[:, 2 + hc, h * NCB:(h + 1) * NCB], W2[:, 2 + hc, :],
                                        start=(hc == 0), stop=(hc == 1))
                ins.then_inc(filled, 1)

            def pool_out():
                for j in range(2):
                    wait_emptied(pe, f"pm{j}")
                    b = pe_open(pe, f"py{j}")
                    for g in range(2):
                        ins = pe.matmul(b[g * HD:(g + 1) * HD, 0:T], POOLW[g * HD:(g + 1) * HD, j, :], MT[g * HD:(g + 1) * HD, j, :],
                                        start=True, stop=True)
                    ins.then_inc(filled, 1)

            q_at = lambda h: ((h % 3), (h // 3) * HD)

            def nsa_scores(i, which="sw"):
                wait_emptied(pe, "nt2")
                w = (i + 1) * P
                for t in which:
                    kc = 3 + "sw".index(t)
                    for b3 in range(2 + i):
                        b = pe_open(pe, f"s{t}{i}{b3}")
                        per = 512 // w
                        half(fresh=True)
                        for h in range(per * b3, min(per * b3 + per, GH)):
                            j, p0 = q_at(h)
                            half(p0=p0)
                            ins = half(pe.matmul(b[:, (h % per) * w:(h % per) * w + w], NTT[p0:p0 + HD, j, i * P:(i + 1) * P],
                                                 NTT[p0:p0 + HD, kc, 0:w], start=True, stop=True), p0)
                        ins.then_inc(filled, 1)

            def nsa_compressed_scores(i):
                wait_emptied(pe, "kct")
                b = pe_open(pe, f"cs{i}")
                half(fresh=True)
                for h in range(GH):
                    j, p0 = q_at(h)
                    half(p0=p0)
                    ins = half(pe.matmul(b[:, h * 16:h * 16 + NCB], NTT[p0:p0 + HD, j, i * P:(i + 1) * P],
                                         KCT[p0:p0 + HD, 0:NCB], start=True, stop=True), p0)
                ins.then_inc(filled, 1)

            def nsa_turn_compressed(i):
                pe.wait_ge(sems["cprobs_ready"], i + 1)
                for j in range(2):
                    b = pe_open(pe, f"pc{i}{j}")
                    for h in range(3 * j, 3 * j + 3):
                        ins = pe.transpose(b[0:NCB, (h % 3) * P:(h % 3 + 1) * P], PCM[:, h, 0:NCB], IDENT[:, :])
                    ins.then_inc(filled, 1)

            def nsa_turn(i, t):
                pe.wait_ge(sems["probs_ready"], 2 * i + "sw".index(t) + 1)
                for b3 in range(2 + i):
                    b = pe_open(pe, f"p{t}{i}{b3}")
                    if i == 0:
                        for h in range(4 * b3, min(4 * b3 + 4, GH)):
                            ins = pe.transpose(b[:, (h % 4) * P:(h % 4 + 1) * P], PR[t][:, h, 0:P], IDENT[:, :])
                    else:
                        for kt in range(2):
                            for h in (2 * b3, 2 * b3 + 1):
                                o = kt * 256 + (h % 2) * P
                                ins = pe.transpose(b[:, o:o + P], PR[t][:, h, kt * P:(kt + 1) * P], IDENT[:, :])
                    ins.then_inc(filled, 1)

            def nsa_output(i):
                wait_emptied(pe, f"pw{i}{1 + i}")
                b = pe_open(pe, f"no{i}")
                for h in range(GH):
                    g = h // 3
                    o = b[(h % 2) * HD:(h % 2 + 1) * HD, (h // 2) * P:(h // 2 + 1) * P]
                    pe.matmul(o, VC[0:NCB, g, :], PCT[0:NCB, h, :], start=True, stop=False)
                    for t, v in (("s", VS), ("w", VW)):
                        for kt in range(i + 1):
                            ins = pe.matmul(o, v[:, kt, g * HD:(g + 1) * HD], PT[t][:, kt, h * P:(h + 1) * P],
                                            start=False, stop=(t == "w" and kt == i))
                ins.then_inc(filled, 1)

            def quadrants(name, tile, left, right):
                b = pe_open(pe, name)
                for q in range(6 * tile, 6 * tile + 6):
                    for h in range(2):
                        r = slice(h * HD, (h + 1) * HD)
                        ins = pe.matmul(b[r, (q % 6) * HD:(q % 6 + 1) * HD], left(q, r), right(q, r), start=True, stop=True,
                                        skip_group_check=True)
                ins.then_inc(filled, 1)

            lt_diag = lambda q, r: LT[r, q, r]
            tb = lambda q, r: TB[r, q, :]
            ttb = lambda q, r: TTB[r, q, :]
            pm = lambda q, r: PM[r, q, :]
            hidden_of_blocks(0)
            pe.wait_ge(sems["lt_ready"], 1)
            for lv in range(NLV + 1):
                for tile in range(NT):
                    if lv == 0:
                        quadrants(f"P0{tile}", tile, lt_diag, lambda q, r: IDENT[r, r])
                    elif lv < NLV:
                        if lv == 1:
                            pe.wait_ge(sems["t0_ready"], tile + 1)
                        else:
                            wait_emptied(pe, f"TT{lv - 1}{tile}")
                        quadrants(f"P{lv}{tile}", tile, lt_diag, tb)
                    else:
                        wait_emptied(pe, f"TT{NLV - 1}{tile}")
                        b = pe_open(pe, f"P{lv}{tile}")
                        for q in range(6 * tile, 6 * tile + 6):
                            ins = pe.matmul(b[HD:P, (q % 6) * HD:(q % 6 + 1) * HD], LT[0:HD, q, HD:P], TB[0:HD, q, :],
                                            start=True, stop=True)
                        ins.then_inc(filled, 1)
                if lv == 0:
                    hidden_of_blocks(1)
                elif lv == 1:
                    project_u(1)
                elif lv == 2:
                    turn_hidden_of_blocks()
                    pool_means()
                elif lv == 3:
                    attention_turns()
                elif lv == 4:
                    compress_out()
                    pool_out()
                elif lv == 5:
                    pe.wait_ge(sems["kc_ready"], 1)
                    b = pe_open(pe, "kct")
                    pe.transpose(b[0:HD, 0:30], KCN[0:30, :], IDENT[0:30, 0:30]).then_inc(filled, 1)
                    nsa_scores(0, "s")
                else:
                    nsa_scores(0, "w")
                    nsa_compressed_scores(0)
                for tile in range(NT):
                    if lv == 0:
                        continue
                    if lv < NLV:
                        pe.wait_ge(sems["pm_ready"], NT * (lv - 1) + tile + 1)
                        quadrants(f"T{lv}{tile}", tile, ttb, pm)
                        quadrants(f"TT{lv}{tile}", tile, pm, ttb)
                    else:
                        wait_emptied(pe, f"P{lv}{tile}")
                        b = pe_open(pe, f"TT{lv}{tile}")
                        for q in range(6 * tile, 6 * tile + 6):
                            ins = pe.matmul(b[0:HD, (q % 6) * HD:(q % 6 + 1) * HD], PM[HD:P, q, :], TTB[HD:P, q, :],
                                            start=True, stop=True)
                        ins.then_inc(filled, 1)
            pe.wait_ge(sems["ttm_diagonal"], 1)
            wait_emptied(pe, f"TT{NLV}1")

            def solve(i, rhs):
                b = pe_open(pe, f"x{i}")
                for h in range(GH):
                    ins = pe.matmul(b[:, h * HD:(h + 1) * HD], TTM[:, 6 * i + h, :], rhs(h), start=True, stop=True)
                ins.then_inc(filled, 1)

            def from_state(name, which):
                b = pe_open(pe, name)
                half(fresh=True)
                for h in (0, 2, 4, 1, 3, 5):
                    p0 = (h % 2) * HD
                    half(p0=p0)
                    ins = half(pe.matmul(b[:, h * HD:(h + 1) * HD], QKT[p0:p0 + HD, which + h // 2, P:T],
                                         SST[p0:p0 + HD, h // 2, :], start=True, stop=True), p0)
                ins.then_inc(filled, 1)

            def within_tile(i):
                wait_emptied(pe, f"x{i}")
                b = pe_open(pe, f"o{i}")
                for h in range(GH):
                    ins = pe.matmul(b[:, h * HD:(h + 1) * HD], QKD[:, 6 * i + h, :], VN[:, i, h, :], start=True, stop=True)
                ins.then_inc(filled, 1)

            solve(0, lambda h: TOK[:, 0, 12 + h, :])
            nsa_turn_compressed(0)
            wait_emptied(pe, "x0")
            pe.wait_ge(sems["kd_ready"], 1)
            b = pe_open(pe, "S")
            for h in range(GH):
                ins = pe.matmul(b[(h % 2) * HD:(h % 2 + 1) * HD, (h // 2) * HD:(h // 2 + 1) * HD], KD[:, h, :], VN[:, 0, h, :],
                                start=True, stop=True)
            ins.then_inc(filled, 1)
            nsa_turn(0, "s")
            wait_emptied(pe, "S")
            from_state("ks1", 3)
            nsa_turn(0, "w")
            pe.wait_ge(sems["rhs_ready"], 1)
            solve(1, lambda h: RHS[:, h, :])
            nsa_output(0)
            within_tile(0)
            from_state("qs1", 0)
            within_tile(1)
            nsa_scores(1)
            nsa_compressed_scores(1)
            pe.wait_ge(sems["ya_ready"], 1)
            for j in range(3):
                b = pe_open(pe, f"ya{j}")
                for i in range(NT):
                    ins = pe.transpose(b[:, i * P:(i + 1) * P], OT2[:, i, 2 * j:2 * j + 2, :].rearrange("p h d -> p (h d)"), IDENT[:, :])
                ins.then_inc(filled, 1)
            nsa_turn_compressed(1)
            nsa_turn(1, "s")
            nsa_turn(1, "w")
            nsa_output(1)
            wait_emptied(pe, "ya2")
            wait_emptied(pe, "no1")
            for n in range(2):
                w = weights(f"out{n}")
                for i in range(NT):
                    b = pe_open(pe, f"out{n}{i}")
                    token_major(b[:, 0:512], w, 512, 0, 512, i, src=YT).then_inc(filled, 1)
            norm_transposes(1)

            wait_emptied(pe, "norm1_3")
            for i in range(NT):
                for n in range(2):
                    pe.matmul(PS[:, 4 + 2 * i + n, :], IDENT[:, :], XR[:, i, n * 512:(n + 1) * 512], start=True, stop=False,
                              skip_group_check=True)

            def ffn_hidden(j, count):
                s = 2 * j
                pe.wait_ge(sems[f"loaded{s}"], 16 * (use(f"ffn0{s}")[1] + count))
                for f in range(4):
                    for c in range(KC):
                        ins = pe.matmul(PS[:, 2 * j + f // 2, (f % 2) * T:(f % 2 + 1) * T],
                                        slots[s][:, c * 512 + f * P:c * 512 + (f + 1) * P], HT[:, c, :],
                                        start=(c == 0), stop=(c == KC - 1), skip_group_check=True)
                    if f % 2 == 1:
                        ins.then_inc(sems["ffn_hid_filled"], 1)

            def ffn_out(j, v):
                s = 2 * j + 1
                pe.wait_ge(sems[f"loaded{s}"], 16 * (use(f"ffn0{s}")[1] + v))
                for f in range(4):
                    if f % 2 == 0:
                        pe.wait_ge(sems["ffn_act_ready"], 4 * v + 2 * j + f // 2 + 1)
                    for i in range(NT):
                        for n in range(2):
                            ins = pe.matmul(PS[:, 4 + 2 * i + n, :], AT[:, j, f * T + i * P:f * T + (i + 1) * P],
                                            slots[s][:, f * D + n * 512:f * D + (n + 1) * 512], start=False, stop=False,
                                            skip_group_check=True)
                ins.then_inc(sems["ffn_out_done"], 1)

            ffn_hidden(0, 0)
            ffn_hidden(1, 0)
            with pe.Fori(0, 3) as v:
                ffn_out(0, v)
                ffn_hidden(0, v + 1)
                ffn_out(1, v)
                ffn_hidden(1, v + 1)
            ffn_out(0, 3)

            pe.wait_ge(sems["ada_used0"], 8)
            pe.wait_ge(sems["ada_used1"], 8)
            pe.wait_ge(sems["ffn_act_ready"], 16)
            for n in range(2):
                for k, seg in enumerate((0, 1, 3, 4)):
                    ins = pe.matmul(PS[32 * k:32 * k + 32, n, :], ONES[:, 0:32], ACC[:, seg * D + n * 512:seg * D + (n + 1) * 512],
                                    start=True, stop=True, skip_group_check=True)
            ins.then_inc(sems["mod_rows_filled"], 1)

            def gate_rows(k, seg):
                for n in range(2):
                    pe.matmul(PS[:, 2 + n, :], ONES[:, :], ACC[:, seg * D + n * 512:seg * D + (n + 1) * 512], start=True, stop=True,
                              skip_group_check=True).then_inc(sems["gates_filled"], 1)

            gate_rows(0, 2)
            ffn_out(1, 3)
            pe.wait_ge(sems["mod_rows_copied"], 1)
            for c in range(KC):
                ins = pe.matmul(PS[:, 0, 4 * c:4 * c + 4], MROW[:, c * P:(c + 1) * P], IDENT[:, 0:P:32], start=True, stop=True,
                                skip_group_check=True)
            ins.then_inc(sems["mod_filled"], 1)
            pe.wait_ge(sems["gates_taken"], 2)
            gate_rows(1, 5)
            pe.wait_ge(sems["gates_taken"], 4)
            norm_transposes(2)
            wait_emptied(pe, "norm2_3")
            for b8 in range(8):
                b = pe_open(pe, f"sq{b8}")
                w = weights(f"sb{b8 // 2}")
                for j in range(2):
                    ins = channel_major(b[:, j * T:(j + 1) * T], w, 512, (b8 % 2) * 256 + j * P)
                ins.then_inc(filled, 1)
            for n in range(2):
                w = weights(f"sb{4 + n}")
                for i in range(NT):
                    b = pe_open(pe, f"sv{n}{i}")
                    token_major(b[:, 0:512], w, 512, 0, 512, i).then_inc(filled, 1)
            wait_emptied(pe, "sv11")

            def scores(t):
                for kt in range(NT):
                    for h in range(2):
                        p0 = h * HD
                        ins = pe.matmul(PS[:, 2 * (t % 3) + h, kt * T:kt * P + T], SQK[p0:p0 + HD, 8 + t, kt * P:(kt + 1) * P],
                                        SQK[p0:p0 + HD, t, kt * P:T], start=(kt == 0), stop=True, skip_group_check=True)
                ins.then_inc(sems["sb_scored"], 1)

            scores(0)
            for t in range(NPAIR + 1):
                if t + 1 < NPAIR:
                    if t >= 2:
                        pe.wait_ge(sems["sa_arg"], t - 1)
                    scores(t + 1)
                if t >= 1:
                    pe.wait_ge(sems["sa_ready"], t)
                    if t >= 3:
                        pe.wait_ge(sems["sb_out_copied"], t - 2)
                    for kt in range(NT):
                        for h in range(2):
                            o = PS[h * HD:(h + 1) * HD, 6 + (t - 1) % 2, kt * P:T]
                            c0 = (2 * (t - 1) + h) * HD
                            ins = pe.matmul(o, SV[:, kt, c0:c0 + HD], SA[:, (t - 1) % 2, h, kt * T:kt * P + T],
                                            start=(kt == 0), stop=True, skip_group_check=True)
                    ins.then_inc(sems["sb_out"], 1)
                if t < NPAIR:
                    pe.wait_ge(sems["sp_ready"], t + 1)
                    for h in range(2):
                        b = PS[:, 2 * (t % 3) + h, :]
                        sp_ = SPB[:, t % 2, h, :]
                        pe.matmul(b[:, 0:T], NLOW[:, :], sp_[:, 0:T], start=False, stop=True, skip_group_check=True)
                        pe.matmul(b[:, T:T + P], NLOW[:, :], sp_[:, T:T + P], start=False, stop=True, skip_group_check=True)
                        ins = pe.matmul(b[:, P:T], NONES[:, :], sp_[:, T:T + P], start=False, stop=True, skip_group_check=True)
                    ins.then_inc(sems["sb_summed"], 1)
            pe.wait_ge(sems["sb_out_copied"], NPAIR)
            for n in range(2):
                w = weights(f"so{n}")
                for i in range(NT):
                    b = pe_open(pe, f"so{n}{i}")
                    token_major(b[:, 0:512], w, 512, 0, 512, i, src=YT).then_inc(filled, 1)
            norm_transposes(3)
            wait_emptied(pe, "norm3_3")
            b = pe_open(pe, "lg")
            pe.wait_ge(sems["rw_loaded"], 32)
            for i in range(NT):
                for c in range(KC):
                    ins = pe.matmul(b[:, i * 36:(i + 1) * 36], HT[:, c, i * P:(i + 1) * P], RW[:, c, :],
                                    start=(c == 0), stop=(c == KC - 1))
            ins.then_inc(filled, 1)
            for i in range(NT):
                for b2 in range(2):
                    b = pe_open(pe, f"h2{i}{b2}")
                    for c in range(4 * b2, 4 * b2 + 4):
                        ins = pe.transpose(b[:, (c % 4) * P:(c % 4 + 1) * P], HT[:, c, i * P:(i + 1) * P], IDENT[:, :])
                    ins.then_inc(filled, 1)

            def begin_sum(q):
                return pe.matmul(PS[:, q, :], IDENT[:, :], XR[:, q // 2, q % 2 * 512:(q % 2 + 1) * 512], start=True,
                                 stop=False, skip_group_check=True)

            wait_emptied(pe, "h210")
            for q in range(2):
                begin_sum(q)
            pe.wait_ge(sems["onehot_ready"], 1)
            b = pe_open(pe, "rank")
            A0, A1 = E32[:, 1, 0:NE], E32[:, 1, NE:2 * NE]
            pe.matmul(b[:, 0:NE], UPS[:, :], A0, start=True, stop=True)
            pe.matmul(b[:, NE:2 * NE], UPS[:, :], A1, start=True, stop=False)
            pe.matmul(b[:, NE:2 * NE], ONES[:, :], A0, start=False, stop=True)
            pe.matmul(b[:, 2 * NE:3 * NE], ONES[:, :], A0, start=True, stop=False)
            pe.matmul(b[:, 2 * NE:3 * NE], ONES[:, :], A1, start=False, stop=True).then_inc(filled, 1)

            def gather():
                for c in range(KC):
                    for i in range(NT):
                        ins = pe.matmul(PS[:, 6 + c // 4, (c % 4) * 2 * CAP:(c % 4 + 1) * 2 * CAP], H2[:, i, c * P:(c + 1) * P],
                                        SEL[:, i, :], start=(i == 0), stop=(i == NT - 1))
                ins.then_inc(sems["gathered"], 1)

            def into_hidden(bank_, parts):
                for c in range(KC):
                    for k, (w, f0, n) in enumerate(parts):
                        ins = pe.matmul(PS[k * CAP:(k + 1) * CAP, bank_, 0:n], HS[:, c, k * CAP:(k + 1) * CAP],
                                        w[:, c * EFF + f0:c * EFF + f0 + n], start=(c == 0), stop=(c == KC - 1))
                return ins

            def turn_hidden(n):
                for f in range(n):
                    ins = pe.transpose(PS[:, 4, f * P:(f + 1) * P], AM[:, f * P:(f + 1) * P], IDENT[:, :])
                ins.then_inc(sems["hid_turned"], 1)

            def turn_weights():
                for i in range(NT):
                    ins = pe.transpose(PS[:, 5, i * P:(i + 1) * P], SELW[:, i, :], IDENT[:, :])
                ins.then_inc(sems["weights_turned"], 1)

            def scatter(i):
                for n in range(2):
                    ins = pe.matmul(PS[:, 2 * i + n, :], GT[:, i * P:(i + 1) * P], YB[:, n * 512:(n + 1) * 512],
                                    start=False, stop=False, skip_group_check=True)
                return ins

            wait_emptied(pe, "h211")
            wait_emptied(pe, "rank")
            for q in range(2, 4):
                ins = begin_sum(q)
            ins.then_inc(sems["x_in_sums"], 1)
            pe.wait_ge(sems["sel_ready"], 1)
            gather()

            def pair(g, i):
                m = NR * g + i

                def loaded(kind):
                    u = 3 * i + kind
                    pe.wait_ge(ring_loaded[u % NR], 32 * (3 * g + u // NR + 1))
                    return RING[u % NR]

                pe.wait_ge(sems["hs0_ready"], m + 1)
                pe.wait_ge(sems["hs1_ready"], m + 1)
                into_hidden(4, tuple((w, 0, EFF) for w in loaded(0))).then_inc(sems["gate_filled"], 1)
                pe.wait_ge(sems["gt_ready"], m + 1)
                into_hidden(5, tuple((w, 0, EFF) for w in loaded(1))).then_inc(sems["up_filled"], 1)
                pe.wait_ge(sems["yb0_ready"], m + 1)
                pe.wait_ge(sems["yb1_ready"], m + 1)
                scatter(0)
                pe.wait_ge(sems["sel_ready"], m + 2)
                gather()
                pe.wait_ge(sems["am_ready"], m + 1)
                turn_hidden(4)
                scatter(1)
                pe.wait_ge(sems["selw_ready"], m + 1)
                turn_weights()
                pe.wait_ge(sems["hs0_ready"], m + 2)
                pe.wait_ge(sems["hs1_ready"], m + 2)
                down = loaded(2)
                pe.wait_ge(sems["ac_ready"], m + 1)
                for n in range(2):
                    for f in range(4):
                        for k in range(2):
                            ins = pe.matmul(PS[k * CAP:(k + 1) * CAP, 6 + n, :], AC[:, f, k * CAP:(k + 1) * CAP],
                                            down[k][:, f * D + n * 512:f * D + (n + 1) * 512],
                                            start=(f == 0), stop=(f == 3))
                    ins.then_inc(sems["down_filled"], 1)

            with pe.Fori(0, NE // 2 // NR) as g:
                for i in range(NR):
                    pair(g, i)
            pair(NE // 2 // NR, 0)
            pe.wait_ge(sems["gt_ready"], NE // 2 + 1)
            pe.wait_ge(sems["yb0_ready"], NE // 2 + 1)
            pe.wait_ge(sems["yb1_ready"], NE // 2 + 1)
            scatter(0)
            scatter(1).then_inc(sems["x_done"], 1)
            pe.wait_ge(sems["over_ready"], 1)
            n_over = pe.value_load(OVI[0:1, OVN:OVN + 1], min_val=0, max_val=OVN)

            def further_pass(x):
                pe.wait_ge(sems["hs0_ready"], x + NE // 2 + 1)
                pe.wait_ge(sems["hs1_ready"], x + NE // 2 + 1)
                for kind, name in enumerate(("gate_filled", "up_filled")):
                    pe.wait_ge(sems[("over_gate", "over_up")[kind]], 16 * (x + 1))
                    w = OVER[kind]
                    into_hidden(4 + kind, ((w, 0, EFF // 2), (w, EFF // 2, EFF // 2))).then_inc(sems[name], 1)
                pe.wait_ge(sems["am_ready"], x + NE // 2 + 1)
                turn_hidden(2)
                pe.wait_ge(sems["selw_ready"], x + NE // 2 + 1)
                turn_weights()
                pe.wait_ge(sems["over_down"], 16 * (x + 1))
                pe.wait_ge(sems["ac_ready"], x + NE // 2 + 1)
                for f in range(4):
                    for n in range(2):
                        ins = pe.matmul(PS[n * CAP:(n + 1) * CAP, 6, :], AC[:, f % 2, (f // 2) * CAP:(f // 2 + 1) * CAP],
                                        OVER[2][:, f * D + n * 512:f * D + (n + 1) * 512], start=(f == 0), stop=(f == 3))
                ins.then_inc(sems["down_filled"], 1)
                pe.wait_ge(sems["gt_ready"], x + NE // 2 + 2)
                pe.wait_ge(sems["yb0_ready"], x + NE // 2 + 2)
                for i in range(NT):
                    for n in range(2):
                        ins = pe.matmul(PS[:, 2 * i + n, :], GT[n * CAP:(n + 1) * CAP, i * P:(i + 1) * P],
                                        YB[n * CAP:(n + 1) * CAP, 0:512], start=False, stop=False, skip_group_check=True)
                ins.then_inc(sems["x_done"], 1)

            with pe.If(n_over > 0):
                further_pass(0)
            with pe.Fori(1, OVN) as x:
                with pe.If(n_over > x):
                    pe.wait_ge(sems["sel_ready"], x + NE // 2 + 1)
                    gather()
                    further_pass(x)

        @block.vector
        def _(dve):
            step = Steps(dve, "dve_step")
            tt, ts, stt = dve.tensor_tensor, dve.tensor_scalar, dve.scalar_tensor_tensor
            freed = sems["emptied_by_dve"]

            b = wait_filled(dve, "cols")
            dve.tensor_copy(COL[:, 0:N_ROWS], b[:, 0:N_ROWS])
            dve.tensor_copy(COL[:, P:P + N_ROWS2], b[:, P:P + N_ROWS2]).then_inc(freed, 1)
            wait_emptied(dve, "cols")
            dve.wait_ge(sems["const_ready"], 2)
            for kv in range(2):
                ins = dve.tensor_copy(XK[:, kv, 2, 0:CL:2], COL[:, P + R2_POS + 16 * kv:P + R2_POS + 16 * kv + 16])
            ins.then_inc(sems["pos_ready"], 1)

            def norm_apply(n, gain, shift=None):
                dve.wait_ge(sems["rstd_ready"], n + 1)
                for i in range(NT):
                    ts(XN[:, i, :], XR[:, i, :], RSTD[:, i:i + 1], None, ALU.mult).then_inc(sems["xn_ready"], 1)
                for b4 in range(4):
                    b = wait_filled(dve, f"norm{n}_{b4}")
                    for c in (2 * b4, 2 * b4 + 1):
                        src = b[:, (c % 2) * T:(c % 2 + 1) * T]
                        if shift is None:
                            ins = ts(HT[:, c, :], src, gain[:, c:c + 1], None, ALU.mult)
                        else:
                            ins = ts(HT[:, c, :], src, gain[:, c:c + 1], shift[:, c:c + 1], ALU.mult, ALU.add)
                    ins.then_inc(freed, 1)

            dve.wait_ge(sems["counts_ready"], 1)
            step(dve.reciprocal(CNT[:, 1, :], CNT[:, 0, :]))
            for w in range(4):
                ins = ts(RCP[:, w, :], CNT[:, 1, :], float(POOLS[w]), 1.0, ALU.mult, ALU.max)
            ins.then_inc(sems["recip_ready"], 1)
            norm_apply(0, COL[:, R_MIX:R_MIX + 8])
            def convolve(g):
                wait_emptied(dve, f"qkv{g}")
                for k in range(4):
                    for j in range(2 * g, min(2 * g + 2, 9)):
                        w = COL[:, R_CONV + k * 9 + j:R_CONV + k * 9 + j + 1]
                        if k == 0:
                            ins = ts(CV[:, j, :], QKVT[:, j, 0:T], w, None, ALU.mult)
                        else:
                            ins = stt(CV[:, j, :], QKVT[:, j, k:k + T], w, CV[:, j, :], ALU.mult, ALU.add)
                    if k < 3:
                        step(ins)
                ins.then_inc(sems["conv_ready"], 1)

            def silu(g):
                dve.wait_ge(sems["conv_exp"], g + 1)
                js = slice(2 * g, min(2 * g + 2, 9))
                step(ts(EX[:, js, :], EX[:, js, :], 1.0, None, ALU.add))
                step(dve.reciprocal(EX[:, js, :], EX[:, js, :]))
                tt(CV[:, js, :], CV[:, js, :], EX[:, js, :], ALU.mult).then_inc(sems["silu_ready"], 1)

            convolve(0)
            for g in range(5):
                if g < 4:
                    convolve(g + 1)
                silu(g)
            dve.wait_ge(sems["misc_loaded"], 16 * 6)
            wait_emptied(dve, "bq1")
            tt(SPV, BG[:, :, 6:12], bc(PBC[:, 6:12], 1, NT), ALU.add).then_inc(sems["dt_added"], 1)
            wait_emptied(dve, "tr12")
            sq24 = SQ.rearrange("p (h d) -> p h d", d=HD)
            for i in range(NT):
                ins = tt(sq24[:, 12 * i:12 * i + 12, :], TOK[:, i, 0:12, :], TOK[:, i, 0:12, :], ALU.mult)
            step(ins)
            dve.tensor_reduce(N2, sq24, X, ALU.add).then_inc(sems["qk_sumsq"], 1)
            dve.wait_ge(sems["dt_parts"], 1)
            step(stt(SPV, SPV, 0.0, SPE, ALU.max, ALU.add))
            stt(GG, SPV, -1.0, bc(EA, 1, NT), ALU.mult, ALU.mult).then_inc(sems["g_ready"], 1)
            dve.wait_ge(sems["qk_rnorm"], 1)
            rn = RN.rearrange("p (i h) -> p i h", i=NT)
            step(ts(rn[:, :, 0:6], rn[:, :, 0:6], SCALE, None, ALU.mult))
            for i in range(NT):
                ins = tt(TOK[:, i, 0:12, :], TOK[:, i, 0:12, :], bc(rn[:, i, :], 2, HD), ALU.mult)
            ins.then_inc(sems["qk_ready"], 1)
            dve.wait_ge(sems["sig_exp"], 1)
            zb = SG[:, :, 0:GW + 6]
            step(ts(zb, zb, 1.0, None, ALU.add))
            step(dve.reciprocal(zb, zb))
            tt(SIG[:, :, 0:GW], SIG[:, :, 0:GW], SG[:, :, 0:GW], ALU.mult)
            b = wait_filled(dve, "gc")
            dve.tensor_copy(GCS, b[:, 0:12])
            dve.tensor_copy(GLS, b[:, 12:18]).then_inc(freed, 1)
            wait_emptied(dve, "gc")
            step(tt(KDE, GLS, GCS[:, 0:6], ALU.subtract))
            for b3 in range(3):
                b = wait_filled(dve, f"r{b3}")
                for q in range(4 * b3, 4 * b3 + 4):
                    ins = ts(DEC[:, q, :], b[:, (q % 4) * P:(q % 4 + 1) * P], GCS[:, q:q + 1], 0.0, ALU.subtract, ALU.min)
                ins.then_inc(freed, 1)
            dve.wait_ge(sems["decay_exp"], 1)
            step(tt(DEC[:, :, :], DEC[:, :, :], bc(UPI[:, :], 1, 12), ALU.mult))
            for b6 in range(6):
                b = wait_filled(dve, f"kk{b6}")
                bb = b[:, 0:512].rearrange("p (q k t) -> p q k t", q=2, k=2)
                ins = tt(QKD[:, 2 * b6:2 * b6 + 2, :], bb[:, :, 0, :], DEC[:, 2 * b6:2 * b6 + 2, :], ALU.mult)
                for q in (2 * b6, 2 * b6 + 1):
                    i, h = q // 6, q % 6
                    ins = stt(LT[:, q, :], bb[:, q % 2, 1, :], SG[:, i, GW + h:GW + h + 1], DEC[:, q, :], ALU.mult, ALU.mult)
                ins.then_inc(freed, 1)
            wait_emptied(dve, "kk5")
            tt(LT[:, :, :], LT[:, :, :], bc(UPS[:, :], 1, 12), ALU.mult).then_inc(sems["lt_ready"], 1)
            dve.wait_ge(sems["lt_ready"], 1)
            dve.wait_ge(sems["const_ready"], 6)
            for h in range(2):
                r = slice(h * HD, (h + 1) * HD)
                ins = tt(TTB[r, :, :], LT[r, :, r], bc(LVMT[r, :], 1, 12), ALU.mult)
            step(ins)
            tt(TTB[:, :, :], TTB[:, :, :], bc(IDB[:, :], 1, 12), ALU.add)
            wait_emptied(dve, "kw1")
            sq20 = SQ[:, 0:1280].rearrange("p (h d) -> p h d", d=HD)
            nq = NQK[:, :, :, :].rearrange("p i h d -> p (i h) d")
            step(tt(sq20, nq, nq, ALU.mult))
            dve.tensor_reduce(M2, sq20, X, ALU.add).then_inc(sems["nqk_sumsq"], 1)

            def level(lv):
                for tile in range(NT):
                    six = slice(6 * tile, 6 * tile + 6)
                    b = wait_filled(dve, f"P{lv}{tile}")
                    if lv == NLV:
                        ts(PM[HD:P, six, :], b[HD:P, 0:GW].rearrange("p (a b) -> p a b", b=HD), -1.0, None, ALU.mult)\
                            .then_inc(freed, 1)
                        continue
                    dst = (PM if lv else TB)[:, six, :]
                    tt(dst, b[:, 0:GW].rearrange("p (a b) -> p a b", b=HD), bc(LVM[:, lv, :], 1, 6), ALU.mult).then_inc(freed, 1)
                    wait_emptied(dve, f"P{lv}{tile}")
                    tt(dst, dst, bc(IDB[:, :], 1, 6), ALU.add).then_inc(sems["pm_ready" if lv else "t0_ready"], 1)

            level(0)
            dve.wait_ge(sems["nqk_rnorm"], 1)
            tt(nq, nq, bc(MR, 2, HD), ALU.mult).then_inc(sems["nqk_ready"], 1)
            dve.wait_ge(sems["sig_exp"], 2)
            gt = SG[:, :, GW + 6:GW + 24]
            step(ts(gt, gt, 1.0, None, ALU.add))
            dve.reciprocal(gt, gt)
            level(1)
            level(2)
            wait_emptied(dve, "hidt")
            for g in range(4):
                ins = ts(HX[:, g, :].rearrange("p (h n) -> p h n", n=NCB),
                         HIDT4[:, g, 0:32].rearrange("p (h n) -> p h n", n=16)[:, :, 0:NCB], HIDT4[:, g, 32:33], None, ALU.add)
            ins.then_inc(sems["hid_bias"], 1)
            level(3)
            for b3 in range(3):
                b = wait_filled(dve, f"nt{b3}")
                for j in range(2 * b3, min(2 * b3 + 2, 5)):
                    r = R_QN if j < 3 else R_KN + j - 2
                    ins = ts(NTT[:, j, :], b[:, (j % 2) * T:(j % 2 + 1) * T], COL[:, r:r + 1], None, ALU.mult)
                ins.then_inc(freed, 1)
            dve.wait_ge(sems["hid_exp"], 1)
            step(ts(HIDT4[:, :, 0:30], HIDT4[:, :, 0:30], 1.0, None, ALU.add))
            step(dve.reciprocal(HIDT4[:, :, 0:30], HIDT4[:, :, 0:30]))
            tt(HX[:, :, :], HX[:, :, :], HIDT4[:, :, 0:30], ALU.mult).then_inc(sems["hid_ready"], 1)
            level(4)
            b = wait_filled(dve, "cmp")
            dve.tensor_copy(VC[0:NCB, :, :], b[0:NCB, HD:3 * HD].rearrange("p (h d) -> p h d", d=HD))
            dve.tensor_copy(KCN[0:30, :], b[0:30, 0:HD]).then_inc(freed, 1)
            wait_emptied(dve, "cmp")
            dve.wait_ge(sems["hid_ready"], 1)
            kcsq = HIDC[0:30, 0, 0:HD]
            step(tt(kcsq, KCN[0:30, :], KCN[0:30, :], ALU.mult))
            dve.tensor_reduce(KN2[0:30, 0:1], kcsq, X, ALU.add).then_inc(sems["kc_sumsq"], 1)
            for j in range(2):
                b = wait_filled(dve, f"py{j}")
                ts(YT[:, 6 + j, :], b[:, 0:T], COL[:, R_PS + j:R_PS + j + 1], None, ALU.mult).then_inc(freed, 1)
            dve.wait_ge(sems["kc_rnorm"], 1)
            ts(KCN[0:30, :], KCN[0:30, :], KN2[0:30, 1:2], None, ALU.mult).then_inc(sems["kc_ready"], 1)
            level(5)
            b = wait_filled(dve, "kct")
            ts(KCT[0:HD, 0:NCB], b[0:HD, 0:NCB], COL[0:HD, R_KN:R_KN + 1], None, ALU.mult)
            ts(KCT[HD:P, 0:NCB], b[0:HD, NCB:2 * NCB], COL[0:HD, R_KN:R_KN + 1], None, ALU.mult).then_inc(freed, 1)
            dve.wait_ge(sems["const_ready"], 4)
            gates = SG[:, :, GW + 6:GW + 24].rearrange("p i (h k) -> p i h k", k=3)

            def nsa_masked(i, which="sw"):
                nb, w = 2 + i, (i + 1) * P
                if i:
                    dve.wait_ge(sems["filled"], order["no0"] + 1)
                for t in which:
                    pr = PR[t][:, :, 0:w]
                    per = 512 // w
                    for b3 in range(nb):
                        b = wait_filled(dve, f"s{t}{i}{b3}")
                        n = min(per, GH - per * b3)
                        mask = QNEG[:, 1 - i:2, :].rearrange("p a b -> p (a b)")
                        ins = tt(pr[:, per * b3:per * b3 + n, :], b[:, 0:n * w].rearrange("p (h k) -> p h k", k=w), bc(mask, 1, n), ALU.add)
                        ins.then_inc(freed, 1)
                    wait_emptied(dve, f"s{t}{i}{nb - 1}")
                    mx = MX if t == "w" else NMX
                    step(dve.tensor_reduce(mx, pr, X, ALU.max))
                    ts(mx, mx, -SCALE, None, ALU.mult).then_inc(sems["smax"], 1)

            def nsa_compressed_masked(i):
                b = wait_filled(dve, f"cs{i}")
                cs = b[:, 0:96].rearrange("p (h n) -> p h n", n=16)[:, :, 0:NCB]
                pc = PCM[:, :, 0:NCB]
                tt(pc, cs, bc(CNEG[:, i, 0:NCB], 1, GH), ALU.add).then_inc(freed, 1)
                wait_emptied(dve, f"cs{i}")
                step(dve.tensor_reduce(CSUM[:, 0, :], pc, X, ALU.max))
                tt(pc, pc, bc(CSUM[:, 0, :], 2, NCB), ALU.subtract).then_inc(sems["cmax"], 1)

            def nsa_compressed_probs(i):
                pc = PCM[:, :, 0:NCB]
                dve.wait_ge(sems["cexp"], i + 1)
                step(dve.tensor_reduce(CSUM[:, 1, :], pc, X, ALU.add))
                step(dve.reciprocal(CSUM[:, 1, :], CSUM[:, 1, :]))
                step(tt(CSUM[:, 2, :], CSUM[:, 1, :], gates[:, i, :, 0], ALU.mult))
                step(tt(pc, pc, bc(CSUM[:, 2, :], 2, NCB), ALU.mult))
                tt(pc, pc, bc(CONE[:, i, 0:NCB], 1, GH), ALU.mult).then_inc(sems["cprobs_ready"], 1)

            def nsa_probs(i, t):
                k = "sw".index(t)
                w = (i + 1) * P
                dve.wait_ge(sems["sexp"], 2 * i + k + 1)
                sm_ = (SUM, CF)[k]
                step(dve.reciprocal(sm_, sm_))
                step(tt(sm_, sm_, gates[:, i, :, 1 + k], ALU.mult))
                tt(PR[t][:, :, 0:w], PR[t][:, :, 0:w], bc(sm_, 2, w), ALU.mult).then_inc(sems["probs_ready"], 1)

            nsa_masked(0, "s")
            level(6)
            nsa_masked(0, "w")
            nsa_compressed_masked(0)
            dve.wait_ge(sems["egc_ready"], 1)
            dve.wait_ge(sems["filled"], order[f"TT{NLV}1"] + 1)
            dve.wait_ge(sems["ttm_diagonal"], 1)
            tt(KD[:, :, :], TOK[:, 0, 6:12, :], bc(KDE, 2, HD), ALU.mult).then_inc(sems["kd_ready"], 1)
            beta = [SG[:, i, GW:GW + 6] for i in range(NT)]
            v3 = lambda b: b[:, 0:GW].rearrange("p (h d) -> p h d", d=HD)
            b = wait_filled(dve, "x0")
            tt(VN[:, 0], v3(b), bc(beta[0], 2, HD), ALU.mult).then_inc(freed, 1)
            nsa_compressed_probs(0)
            nsa_probs(0, "s")
            b = wait_filled(dve, "S")
            dve.tensor_copy(SST[:, :, :], b[:, 0:3 * HD].rearrange("p (j d) -> p j d", d=HD)).then_inc(freed, 1)
            nsa_probs(0, "w")
            b = wait_filled(dve, "ks1")
            tt(RHS[:, :, :], v3(b), bc(EGC, 2, HD), ALU.mult).then_inc(freed, 1)
            wait_emptied(dve, "ks1")
            tt(RHS[:, :, :], TOK[:, 1, 12:18, :], RHS[:, :, :], ALU.subtract).then_inc(sems["rhs_ready"], 1)
            b = wait_filled(dve, "x1")
            tt(VN[:, 1], v3(b), bc(beta[1], 2, HD), ALU.mult).then_inc(freed, 1)
            b = wait_filled(dve, "o0")
            dve.tensor_copy(OT2[:, 0], v3(b)).then_inc(freed, 1)
            b = wait_filled(dve, "qs1")
            tt(TMP[:, 0], v3(b), bc(EGC, 2, HD), ALU.mult).then_inc(freed, 1)
            wait_emptied(dve, "qs1")
            b = wait_filled(dve, "o1")
            tt(OT2[:, 1], v3(b), TMP[:, 0], ALU.add).then_inc(freed, 1)
            wait_emptied(dve, "o1")
            oo = OT2[:, :, :, :].rearrange("p i h d -> p (i h) d")
            tm = TMP[:, :, :, :].rearrange("p i h d -> p (i h) d")
            step(tt(tm, oo, oo, ALU.mult))
            dve.tensor_reduce(O2, tm, X, ALU.add).then_inc(sems["o_sumsq"], 1)
            nsa_masked(1)
            nsa_compressed_masked(1)
            dve.wait_ge(sems["o_rnorm"], 1)
            step(tt(oo, oo, bc(OR, 2, HD), ALU.mult))
            for i in range(NT):
                ins = tt(OT2[:, i], OT2[:, i], SIG[:, i, 0:GW].rearrange("p (h d) -> p h d", d=HD), ALU.mult)
            ins.then_inc(sems["ya_ready"], 1)
            for j in range(3):
                b = wait_filled(dve, f"ya{j}")
                ins = ts(YT[:, j, :], b[:, 0:T], COL[:, R_GN:R_GN + 1], None, ALU.mult)
                ins.then_inc(freed, 1)
            nsa_compressed_probs(1)
            nsa_probs(1, "s")
            nsa_probs(1, "w")
            for n in range(2):
                for i in range(NT):
                    b = wait_filled(dve, f"out{n}{i}")
                    ins = tt(XR[:, i, n * 512:(n + 1) * 512], b[:, 0:512], XR[:, i, n * 512:(n + 1) * 512], ALU.add)
                    ins.then_inc(freed, 1)
            norm_apply(1, COL[:, R_FFN:R_FFN + 8])
            dve.wait_ge(sems["cond_exp"], 1)
            step(ts(COND[:, 8:16], COND[:, 8:16], 1.0, None, ALU.add))
            step(dve.reciprocal(COND[:, 8:16], COND[:, 8:16]))
            step(tt(COND[:, 0:8], COND[:, 8:16], COL[:, P + R2_C:P + R2_C + 8], ALU.mult))
            with dve.Fori(0, 8) as v:
                for c in range(KC):
                    for k in range(2):
                        if c == 0:
                            dve.wait_ge(sems[f"ada_loaded{k}"], 16 * v + 16)
                        else:
                            dve.wait_ge(sems["ada_step"], 14 * v + 2 * c + k - 1)
                        acc = ACC[:, bass.ds((2 * v + k) * ADW, ADW)]
                        if c == 0:
                            ins = ts(acc, ADA[:, k, c, :], COND[:, c:c + 1], None, ALU.mult)
                        else:
                            ins = stt(acc, ADA[:, k, c, :], COND[:, c:c + 1], acc, ALU.mult, ALU.add)
                        ins.then_inc(sems["ada_step" if c < KC - 1 else f"ada_used{k}"], 1)
            dve.wait_ge(sems["mod_rows_filled"], 1)
            dve.tensor_copy(MROW.rearrange("p (n d) -> p n d", n=2), PS[:, 0:2, :]).then_inc(sems["mod_rows_copied"], 1)
            dve.wait_ge(sems["rows_bc"], 48)

            def take_gates(k):
                for n in range(2):
                    dve.wait_ge(sems["gates_filled"], 2 * k + n + 1)
                    g12 = G12[:, k, n * 512:(n + 1) * 512]
                    tt(g12, PS[:, 2 + n, :], g12, ALU.add).then_inc(sems["gates_taken"], 1)

            take_gates(0)
            dve.wait_ge(sems["ffn_out_done"], 8)
            for i in range(NT):
                dve.tensor_copy(XR[:, i, :].rearrange("p (n d) -> p n d", n=2), PS[:, 4 + 2 * i:6 + 2 * i, :])                    .then_inc(sems["x_ready"], 1)
            dve.wait_ge(sems["x_ready"], NT)
            dve.wait_ge(sems["mod_filled"], 1)
            for k, seg in enumerate((0, 1, 3, 4)):
                ins = tt(MODC[:, 8 * k:8 * k + 8], PS[:, 0, k:32:4], COL[:, R_ADA + 8 * seg:R_ADA + 8 * seg + 8], ALU.add)
            step(ins)
            for k in range(2):
                ins = stt(MODC[:, 32 + 8 * k:40 + 8 * k], MODC[:, 16 * k + 8:16 * k + 16], 1.0,
                          COL[:, R_NG + 8 * k:R_NG + 8 * k + 8], ALU.add, ALU.mult)
            step(ins)
            take_gates(1)
            norm_apply(2, MODC[:, 32:40], MODC[:, 0:8])
            def score_banks(t):
                return PS[:, 2 * (t % 3):2 * (t % 3) + 2, 0:3 * P]

            for t in range(NPAIR + 1):
                if t >= 1:
                    dve.wait_ge(sems["sb_summed"], t)
                    if t >= 3:
                        dve.wait_ge(sems["sb_out"], t - 2)
                    stt(SA[:, (t - 1) % 2], score_banks(t - 1), 0.0, bc(SBNEG[:, :, :].rearrange("p k q -> p (k q)"), 1, 2),
                        ALU.min, ALU.add).then_inc(sems["sa_arg"], 1)
                if t < NPAIR:
                    dve.wait_ge(sems["sp_ln"], t + 1)
                    if t >= 2:
                        dve.wait_ge(sems["sb_summed"], t - 1)
                    spb = SPB[:, t % 2]
                    step(stt(spb, score_banks(t), 0.0, SAB[:, t % 2], ALU.max, ALU.add))
                    for h in range(2):
                        dg = spb[:, h, :].rearrange("p (k q) -> p k q", q=P)[:, 0:3:2, :]
                        ins = tt(dg, dg, bc(UPS[:, :], 1, 2), ALU.mult)
                    ins.then_inc(sems["sp_ready"], 1)

            for n in range(2):
                for i in range(NT):
                    b = wait_filled(dve, f"so{n}{i}")
                    t = YTMP[:, i, n * 512:(n + 1) * 512]
                    xr = XR[:, i, n * 512:(n + 1) * 512]
                    step(tt(t, b[:, 0:512], G12[:, 0, n * 512:(n + 1) * 512], ALU.mult))
                    tt(xr, xr, t, ALU.add).then_inc(freed, 1)
            norm_apply(3, MODC[:, 40:48], MODC[:, 16:24])

            dve.memset(GT[:, :], 0.0).then_inc(sems["gt_ready"], 1)
            dve.memset(YB[:, 0:512], 0.0).then_inc(sems["yb0_ready"], 1)
            dve.memset(YB[:, 512:D], 0.0).then_inc(sems["yb1_ready"], 1)
            dve.wait_ge(sems["const_ready"], 6)
            step(ts(REV[:, :], IOTA[:, 0:8], -1.0, 8.0, ALU.mult, ALU.add))
            b = wait_filled(dve, "lg")
            tt(LG[:, :, :], b[:, 0:72].rearrange("p (i n) -> p i n", n=36), bc(PBC[:, 12:48], 1, NT), ALU.add).then_inc(freed, 1)
            wait_emptied(dve, "lg")
            lg4 = LG[:, :, 0:NG]

            def first_max(src, n, k):
                step(dve.tensor_reduce(rv(k, 1), src, X, ALU.max))
                step(tt(rv(k + 1, n), src, rv(k, 1).to_broadcast([P, NT, n]), ALU.is_equal))
                step(tt(rv(k + 1, n), rv(k + 1, n), bc(REV[:, 8 - n:8], 1, NT), ALU.mult))
                step(dve.tensor_reduce(rv(k + 2, 1), rv(k + 1, n), X, ALU.max))
                step(tt(rv(k + 3, n), rv(k + 1, n), rv(k + 2, 1).to_broadcast([P, NT, n]), ALU.is_equal))

            first_max(lg4, NG, 0)
            tt(rv(4, 4), lg4, rv(0, 1).to_broadcast([P, NT, NG]), ALU.subtract).then_inc(sems["gr_in"], 1)
            prod = E32[:, 0, :].rearrange("p (i e g) -> p i e g", i=NT, g=NG)
            step(tt(prod, LG[:, :, NG:36].rearrange("p i (g e) -> p i e g", g=NG), bc(rv(3, 4), 2, PG), ALU.mult))
            step(dve.tensor_reduce(rv(6, 8), prod, X, ALU.add))
            first_max(rv(6, 8), PG, 7)
            step(stt(rv(11, 8), rv(10, 8), NEG, rv(6, 8), ALU.mult, ALU.add))
            first_max(rv(11, 8), PG, 12)
            tt(rv(16, 1), rv(12, 1), rv(7, 1), ALU.subtract).then_inc(sems["t2_in"], 1)
            dve.wait_ge(sems["gr_exp"], 1)
            step(dve.tensor_reduce(rv(5, 1), rv(4, 4), X, ALU.add))
            step(dve.reciprocal(rv(5, 1), rv(5, 1)))
            step(tt(rv(20, 8), rv(10, 8), rv(15, 8), ALU.add))
            hot = lambda v: (bc(rv(3, 4), 3, PG), bc(v, 2, NG))
            v4 = lambda t: t.rearrange("p i (g e) -> p i g e", g=NG)
            tt(v4(E32[:, 1, :].rearrange("p (i n) -> p i n", i=NT)), *hot(rv(20, 8)), ALU.mult).then_inc(sems["onehot_ready"], 1)
            dve.wait_ge(sems["t2_exp"], 1)
            step(ts(rv(17, 1), rv(16, 1), 1.0, None, ALU.add))
            step(dve.reciprocal(rv(17, 1), rv(17, 1)))
            step(tt(rv(18, 1), rv(17, 1), rv(5, 1), ALU.mult))
            step(tt(rv(19, 1), rv(18, 1), rv(16, 1), ALU.mult))
            tt(rv(21, 8), rv(10, 8), rv(18, 1).to_broadcast([P, NT, 8]), ALU.mult)
            step(tt(rv(22, 8), rv(15, 8), rv(19, 1).to_broadcast([P, NT, 8]), ALU.mult))
            step(tt(rv(21, 8), rv(21, 8), rv(22, 8), ALU.add))
            step(tt(v4(WT[:, :, 0:NE]), *hot(rv(21, 8)), ALU.mult))
            b = wait_filled(dve, "rank")
            dve.tensor_copy(E32[:, 2, :], b[:, 0:2 * NE])
            dve.tensor_copy(E32[:, 3, 0:NE], b[:, 2 * NE:3 * NE]).then_inc(freed, 1)
            wait_emptied(dve, "rank")
            two = lambda k: E32[:, k, :].rearrange("p (i n) -> p i n", i=NT)
            rank, went = two(2), two(1)
            step(stt(KEY[:, :, 0:NE], rank, 1.0, went, ALU.add, ALU.mult))
            step(ts(KEY[:, :, 0:NE], KEY[:, :, 0:NE], -1.0, None, ALU.add))

            def selections(dst, pair, weighted):
                for i in range(NT):
                    for k in range(2):
                        key = KEY[:, i, bass.ds(2 * pair + k, 1)]
                        d = dst[:, i, k * CAP:(k + 1) * CAP]
                        if weighted:
                            ins = ts(d, IOTA[:, 0:CAP], key, WT[:, i, bass.ds(2 * pair + k, 1)], ALU.is_equal, ALU.mult)
                        else:
                            ins = ts(d, IOTA[:, 0:CAP], key, None, ALU.is_equal)
                return ins

            selections(SEL, 0, False).then_inc(sems["sel_ready"], 1)
            selections(SELW, 0, True).then_inc(sems["selw_ready"], 1)

            def half_of_tokens(count):
                dve.wait_ge(sems["gathered"], count)
                dve.tensor_copy(HS[:, 0:4, :], PS[:, 6, :].rearrange("p (c n) -> p c n", n=2 * CAP)).then_inc(sems["hs0_ready"], 1)

            half_of_tokens(1)

            cnt, nov, incl, start = E32[:, 3, 0:NE], E32[:, 4, 0:NE], E32[:, 4, NE:2 * NE], E32[:, 5, 0:NE]
            dve.memset(E32[:, 3, NE:2 * NE], 0.0)
            step(ts(nov, cnt, float(CAP), None, ALU.is_gt))
            step(stt(nov, cnt, 2.0 * CAP, nov, ALU.is_gt, ALU.add))
            step(stt(nov, cnt, 3.0 * CAP, nov, ALU.is_gt, ALU.add))
            step(dve.tensor_tensor_scan(incl, nov, E32[:, 3, NE:2 * NE], 0.0, ALU.add, ALU.add))
            step(tt(start, incl, nov, ALU.subtract))
            rb, gs, pos1 = two(6), two(7), two(0)
            step(ts(rb, rank, float(CAP), None, ALU.is_ge))
            step(stt(rb, rank, 2.0 * CAP, rb, ALU.is_ge, ALU.add))
            step(stt(rb, rank, 3.0 * CAP, rb, ALU.is_ge, ALU.add))
            step(stt(pos1, rb, -float(CAP), rank, ALU.mult, ALU.add))
            step(ts(pos1, pos1, 1.0, None, ALU.add))
            step(tt(gs, rb, bc(start, 1, NT), ALU.add))
            step(tt(gs, gs, went, ALU.mult))
            step(stt(gs, rb, 1.0, gs, ALU.min, ALU.mult))
            for i in range(NT):
                step(tt(OVS[:, 0], bc(gs[:, i, :], 1, OVN), bc(IOTA[:, 1:OVN + 1], 2, NE), ALU.is_equal))
                step(tt(OVS[:, 1], OVS[:, 0], bc(pos1[:, i, :], 1, OVN), ALU.mult))
                step(dve.tensor_reduce(OVK[:, i, :], OVS[:, 1], X, ALU.add))
                step(ts(OVK[:, i, :], OVK[:, i, :], -1.0, None, ALU.add))
                step(tt(OVS[:, 1], OVS[:, 0], bc(WT[:, i, 0:NE], 1, OVN), ALU.mult))
                step(dve.tensor_reduce(OVW[:, i, :], OVS[:, 1], X, ALU.add))
            dve.tensor_copy(KEY[:, :, NE:NE + 2], OVK[:, :, 0:1].to_broadcast([P, NT, 2]))
            step(dve.tensor_copy(WT[:, :, NE:NE + 2], OVW[:, :, 0:1].to_broadcast([P, NT, 2])))
            step(tt(OVS[:, 0], bc(incl, 1, OVN), bc(IOTA[:, 0:OVN], 2, NE), ALU.is_le))
            step(dve.tensor_reduce(OVF[:, 0:OVN], OVS[:, 0], X, ALU.add))
            dve.tensor_copy(OVF[:, OVN:OVN + 1], incl[:, NE - 1:NE])
            step(ts(OVF[:, 0:OVN], OVF[:, 0:OVN], float(NE - 1), None, ALU.min))
            dve.tensor_copy(OVI[:, 0:OVN + 1], OVF[:, 0:OVN + 1]).then_inc(sems["over_ready"], 1)

            def silu_times_up(m, width):
                es = ES[:, 0:width]
                n = [0]

                def link(ins):
                    n[0] += 1
                    ins.then_inc(sems["silu_step"], 1)
                    dve.wait_ge(sems["silu_step"], 3 * m + n[0])

                dve.wait_ge(sems["gate_exp"], m + 1)
                link(ts(es, es, 1.0, None, ALU.add))
                link(dve.reciprocal(es, es))
                link(tt(es, PS[:, 4, 0:width], es, ALU.mult))
                dve.wait_ge(sems["up_filled"], m + 1)
                tt(AM[:, 0:width], PS[:, 5, 0:width], es, ALU.mult).then_inc(sems["am_ready"], 1)

            with dve.Fori(0, NE // 2) as m:
                dve.wait_ge(sems["gathered"], m + 1)
                selections(SEL, m + 1, False).then_inc(sems["sel_ready"], 1)
                silu_times_up(m, EFF)
                half_of_tokens(m + 2)
                dve.wait_ge(sems["weights_turned"], m + 1)
                selections(SELW, m + 1, True).then_inc(sems["selw_ready"], 1)
                for n in range(2):
                    d = slice(n * 512, (n + 1) * 512)
                    dve.wait_ge(sems["down_filled"], 2 * m + n + 1)
                    tt(YB[:, d], PS[:, 6 + n, :], G12[:, 1, d], ALU.mult).then_inc(sems[("yb0_ready", "yb1_ready")[n]], 1)

            dve.wait_ge(sems["over_ready"], 1)
            n_over = dve.value_load(OVI[0:1, OVN:OVN + 1], min_val=0, max_val=OVN)

            def further_pass(x):
                silu_times_up(x + NE // 2, EFF // 2)
                dve.wait_ge(sems["down_filled"], x + NE + 1)
                for n in range(2):
                    h = slice(n * CAP, (n + 1) * CAP)
                    ins = tt(YB[h, 0:512], PS[h, 6, :], G12[h, 1, n * 512:(n + 1) * 512], ALU.mult)
                ins.then_inc(sems["yb0_ready"], 1)

            with dve.If(n_over > 0):
                further_pass(0)
            with dve.Fori(1, OVN) as x:
                with dve.If(n_over > x):
                    dve.wait_ge(sems["gathered"], x + NE // 2)
                    dve.wait_ge(sems["weights_turned"], x + NE // 2)
                    dve.wait_ge(sems["selw_ready"], x + NE // 2)
                    for i in range(NT):
                        key = OVK[:, i, bass.ds(x, 1)]
                        for k in range(2):
                            d = slice(k * CAP, (k + 1) * CAP)
                            ins = ts(SEL[:, i, d], IOTA[:, 0:CAP], key, None, ALU.is_equal)
                    ins.then_inc(sems["sel_ready"], 1)
                    for i in range(NT):
                        key = OVK[:, i, bass.ds(x, 1)]
                        for k in range(2):
                            d = slice(k * CAP, (k + 1) * CAP)
                            ins = ts(SELW[:, i, d], IOTA[:, 0:CAP], key, OVW[:, i, bass.ds(x, 1)], ALU.is_equal, ALU.mult)
                    ins.then_inc(sems["selw_ready"], 1)
                    half_of_tokens(x + NE // 2 + 1)
                    further_pass(x)
            dve.wait_ge(sems["rstd_ready"], 5)
            for i in range(NT):
                two_halves = lambda t: t.rearrange("p (h d) -> p h d", h=2)
                stt(two_halves(XR[:, i, :]), PS[:, 2 * i:2 * i + 2, :], RSTD[:, i:i + 1], two_halves(FG[:, :]), ALU.mult, ALU.mult)\
                    .then_inc(sems["out_ready"], 1)

NAMES = ["x", "norm_mix", "w_in", "conv_w", "a_log", "dt_bias", "gdn_norm", "nsa_q_norm", "nsa_k_norm", "cmp_pos",
         "cmp_w1", "cmp_w2", "pool_w", "pool_scale", "w_out", "norm_ffn", "w_ffn1", "w_ffn2", "c_2", "ada_w_2",
         "ada_b_2", "norm_g_2", "final_g_2", "sb_w_in_2", "sb_w_out_2", "moe_w_grp_2", "moe_b_grp_2", "moe_w_exp_2",
         "moe_b_exp_2", "moe_w_gate_2", "moe_w_up_2", "moe_w_down_2"]


def kernel(**inputs):
    import numpy as np
    import concourse.bacc as bacc
    from concourse.bass_utils import run_bass_kernel_spmd

    nc = bacc.Bacc("TRN2", target_bir_lowering=False, num_devices=1, dynamic_dma_scratch_size=1024)
    arrays, aps = {}, {}
    for name in NAMES:
        v = np.ascontiguousarray(inputs[name])
        arrays[f"in_{name}_dram"] = v
        aps[name] = nc.dram_tensor(f"in_{name}_dram", v.shape, F32, kind="ExternalInput").ap()
    out = nc.dram_tensor("out_0_dram", (1, T, D), F32, kind="ExternalOutput").ap()
    build(nc, aps, out)
    r = run_bass_kernel_spmd(nc, [arrays], core_ids=[0])
    return r.results[0]["out_0_dram"]
```
